# Optimizing a Trainium2 kernel written in Bass

```python
import jax
import jax.numpy as jnp
from jax import lax
import numpy as np

D_MODEL = 1024
BATCH = 1
SEQ = 512
DEPTH = 2

N_HEADS = 4
HEAD_DIM = 64
BR_WIDTH = N_HEADS * HEAD_DIM
N_BRANCH = 5
N_MEM = 256
ROPE_THETA = 10000.0
EPS = 1e-6
Q_BLOCK = 128
DSA_TOPK_MAX = 256
IDX_HEADS = 4
IDX_DIM = 32
KV_LATENT = 128
NSA_KV_DIM = 64
CMP_LEN = 32
CMP_STRIDE = 16
CMP_HIDDEN = 128
SLC_BLOCK = 64
SLC_TOPN = 16
WINDOW = 512
FORCE_SCORE = 1e4

IN_LAYOUT = (
    ('dsa_q', BR_WIDTH), ('dsa_ckv', KV_LATENT), ('idx_q', IDX_HEADS * IDX_DIM), ('idx_k', IDX_DIM), ('idx_w', IDX_HEADS), ('dsa_z', BR_WIDTH),
    ('fox_q', BR_WIDTH), ('fox_k', BR_WIDTH), ('fox_v', BR_WIDTH), ('fox_f', N_HEADS), ('fox_z', BR_WIDTH),
    ('sb_q', BR_WIDTH), ('sb_k', BR_WIDTH), ('sb_v', BR_WIDTH), ('sb_z', BR_WIDTH),
    ('nsa_q', BR_WIDTH), ('nsa_kc', NSA_KV_DIM), ('nsa_vc', NSA_KV_DIM), ('nsa_ks', NSA_KV_DIM), ('nsa_vs', NSA_KV_DIM),
    ('nsa_kw', NSA_KV_DIM), ('nsa_vw', NSA_KV_DIM), ('nsa_g', 3 * N_HEADS), ('nsa_z', BR_WIDTH),
    ('mem_q', BR_WIDTH), ('mem_z', BR_WIDTH),
    ('merge', N_BRANCH * D_MODEL),
)
N_IN = sum(n for _, n in IN_LAYOUT)


def _rmsnorm(x, g):
    xf = x.astype(jnp.float32)
    y = xf * lax.rsqrt(jnp.mean(xf * xf, axis=-1, keepdims=True) + EPS)
    return (y * g.astype(jnp.float32)).astype(x.dtype)

def _rope(x, pos):
    dh = x.shape[-1]
    inv = ROPE_THETA ** (-jnp.arange(0, dh, 2, dtype=jnp.float32) / dh)
    ang = pos.astype(jnp.float32)[..., None] * inv
    ang = ang.reshape(ang.shape[:2] + (1,) * (x.ndim - 3) + ang.shape[-1:])
    cos, sin = jnp.cos(ang), jnp.sin(ang)
    xf = x.astype(jnp.float32)
    x1, x2 = xf[..., : dh // 2], xf[..., dh // 2:]
    return jnp.concatenate([x1 * cos - x2 * sin, x2 * cos + x1 * sin], axis=-1).astype(x.dtype)

def _masked_softmax(logits, mask):
    l = jnp.where(mask, logits, -jnp.inf)
    m = jnp.max(l, axis=-1, keepdims=True)
    m = jnp.where(jnp.isfinite(m), m, 0.0)
    e = jnp.where(mask, jnp.exp(l - m), 0.0)
    return e / jnp.maximum(jnp.sum(e, axis=-1, keepdims=True), 1e-30)

def _to_blocks(a):
    b, s = a.shape[:2]
    return jnp.moveaxis(a.reshape((b, s // Q_BLOCK, Q_BLOCK) + a.shape[2:]), 1, 0)

def _from_blocks(a):
    nq, b, q = a.shape[:3]
    return jnp.moveaxis(a, 0, 1).reshape((b, nq * q) + a.shape[3:])

def _gather_rows(table, idx):
    return jax.vmap(lambda tb, ib: tb[ib])(table, idx)

def _split_columns(p):
    out, off = {}, 0
    for name, n in IN_LAYOUT:
        out[name] = p[..., off:off + n]
        off += n
    return out

def _dsa_attention(q, k, v, qi, ki, wi):
    B, S, H, Dh = q.shape
    k_sel = min(DSA_TOPK_MAX, S // 4)
    s_pos = jnp.arange(S)
    scale = Dh ** -0.5
    idx_scale = (IDX_DIM ** -0.5) * (IDX_HEADS ** -0.5)

    def block(args):
        qb, q_blk, qi_blk, wi_blk = args
        t = qb * Q_BLOCK + jnp.arange(Q_BLOCK)
        rel = jax.nn.relu(jnp.einsum('bqhd,bsd->bqhs', qi_blk, ki).astype(jnp.float32))
        score = jnp.einsum('bqhs,bqh->bqs', rel, wi_blk.astype(jnp.float32)) * idx_scale
        score = jnp.where(s_pos[None, None, :] <= t[None, :, None], score, -jnp.inf)
        _, sel = lax.top_k(score, k_sel)
        kg = _gather_rows(k, sel)
        vg = _gather_rows(v, sel)
        logits = jnp.einsum('bqhd,bqkhd->bhqk', q_blk, kg).astype(jnp.float32) * scale
        mask = (sel <= t[None, :, None])[:, None]
        p = _masked_softmax(logits, mask).astype(v.dtype)
        return jnp.einsum('bhqk,bqkhd->bqhd', p, vg)

    out = lax.map(block, (jnp.arange(S // Q_BLOCK), _to_blocks(q), _to_blocks(qi), _to_blocks(wi)))
    return _from_blocks(out)

def _fox_attention(q, k, v, log_f):
    B, S, H, Dh = q.shape
    s_pos = jnp.arange(S)
    scale = Dh ** -0.5
    cum = jnp.cumsum(log_f.astype(jnp.float32), axis=1)
    cum_s = jnp.moveaxis(cum, 1, 2)

    def block(args):
        qb, q_blk, c_blk = args
        t = qb * Q_BLOCK + jnp.arange(Q_BLOCK)
        logits = (jnp.einsum('bqhd,bshd->bhqs', q_blk, k).astype(jnp.float32) * scale
                  + jnp.moveaxis(c_blk, 1, 2)[..., None] - cum_s[:, :, None, :])
        mask = (s_pos[None, :] <= t[:, None])[None, None]
        p = _masked_softmax(logits, mask).astype(v.dtype)
        return jnp.einsum('bhqs,bshd->bqhd', p, v)

    out = lax.map(block, (jnp.arange(S // Q_BLOCK), _to_blocks(q), _to_blocks(cum)))
    return _from_blocks(out)

def _stick_breaking_attention(q, k, v):
    B, S, H, Dh = q.shape
    s_pos = jnp.arange(S)
    scale = Dh ** -0.5

    def block(args):
        qb, q_blk = args
        t = qb * Q_BLOCK + jnp.arange(Q_BLOCK)
        z = jnp.einsum('bqhd,bshd->bhqs', q_blk, k).astype(jnp.float32) * scale
        strict = (s_pos[None, :] < t[:, None])[None, None]
        log_keep = jnp.where(strict, jax.nn.log_sigmoid(-z), 0.0)
        later = lax.cumsum(log_keep, axis=3, reverse=True) - log_keep
        a = jnp.where(strict, jnp.exp(jax.nn.log_sigmoid(z) + later), 0.0).astype(v.dtype)
        return jnp.einsum('bhqs,bshd->bqhd', a, v)

    out = lax.map(block, (jnp.arange(S // Q_BLOCK), _to_blocks(q)))
    return _from_blocks(out)

def _nsa_attention(q, kc_tok, vc_tok, ks, vs, kw, vw, gates, pe_k, pe_v, wc1_k, wc2_k, wc1_v, wc2_v):
    B, S, H, Dh = q.shape
    scale = Dh ** -0.5
    n_cmp = (S - CMP_LEN) // CMP_STRIDE + 1
    n_blk = S // SLC_BLOCK
    n_sel = min(SLC_TOPN, n_blk)
    per_blk = SLC_BLOCK // CMP_STRIDE
    tok = (jnp.arange(n_cmp) * CMP_STRIDE)[:, None] + jnp.arange(CMP_LEN)[None, :]

    def compress(x_tok, pe, w1, w2):
        blocks = (x_tok[:, tok] + pe).reshape(B, n_cmp, CMP_LEN * x_tok.shape[-1])
        return jax.nn.silu(blocks @ w1) @ w2

    kc = compress(kc_tok, pe_k, wc1_k, wc2_k)
    vc = compress(vc_tok, pe_v, wc1_v, wc2_v)
    cmp_end = jnp.arange(n_cmp) * CMP_STRIDE + CMP_LEN - 1
    ks_blk = ks.reshape(B, n_blk, SLC_BLOCK, -1)
    vs_blk = vs.reshape(B, n_blk, SLC_BLOCK, -1)
    kw_pad = jnp.pad(kw, ((0, 0), (WINDOW, 0), (0, 0)))
    vw_pad = jnp.pad(vw, ((0, 0), (WINDOW, 0), (0, 0)))
    blk_ids = jnp.arange(n_blk)
    in_blk = jnp.arange(SLC_BLOCK)
    win_off = jnp.arange(WINDOW + Q_BLOCK) - WINDOW

    def block(args):
        qb, q_blk, g_blk = args
        t = qb * Q_BLOCK + jnp.arange(Q_BLOCK)
        lc = jnp.einsum('bqhd,bnd->bhqn', q_blk, kc).astype(jnp.float32) * scale
        pc = _masked_softmax(lc, (cmp_end[None, :] <= t[:, None])[None, None])
        o_cmp = jnp.einsum('bhqn,bnd->bqhd', pc.astype(vc.dtype), vc)
        imp = jnp.pad(jnp.sum(pc, axis=1), ((0, 0), (0, 0), (0, n_blk * per_blk - n_cmp)))
        imp = jnp.sum(imp.reshape(B, Q_BLOCK, n_blk, per_blk), axis=-1)
        cur = t // SLC_BLOCK
        forced = (blk_ids[None, :] == 0) | (blk_ids[None, :] == cur[:, None]) | (blk_ids[None, :] == cur[:, None] - 1)
        visible = blk_ids[None, :] <= cur[:, None]
        imp = jnp.where(forced[None], FORCE_SCORE, jnp.where(visible[None], imp, -1.0))
        _, sel = lax.top_k(imp, n_sel)
        ksg = _gather_rows(ks_blk, sel).reshape(B, Q_BLOCK, n_sel * SLC_BLOCK, -1)
        vsg = _gather_rows(vs_blk, sel).reshape(B, Q_BLOCK, n_sel * SLC_BLOCK, -1)
        pos = (sel[..., None] * SLC_BLOCK + in_blk).reshape(B, Q_BLOCK, n_sel * SLC_BLOCK)
        ls = jnp.einsum('bqhd,bqkd->bhqk', q_blk, ksg).astype(jnp.float32) * scale
        ps = _masked_softmax(ls, (pos <= t[None, :, None])[:, None])
        o_slc = jnp.einsum('bhqk,bqkd->bqhd', ps.astype(vs.dtype), vsg)
        kwb = lax.dynamic_slice_in_dim(kw_pad, qb * Q_BLOCK, WINDOW + Q_BLOCK, axis=1)
        vwb = lax.dynamic_slice_in_dim(vw_pad, qb * Q_BLOCK, WINDOW + Q_BLOCK, axis=1)
        s = qb * Q_BLOCK + win_off
        d = t[:, None] - s[None, :]
        mw = ((d >= 0) & (d < WINDOW) & (s[None, :] >= 0))[None, None]
        lw = jnp.einsum('bqhd,bkd->bhqk', q_blk, kwb).astype(jnp.float32) * scale
        pw = _masked_softmax(lw, mw)
        o_win = jnp.einsum('bhqk,bkd->bqhd', pw.astype(vw.dtype), vwb)
        return (g_blk[:, :, 0, :, None] * o_cmp + g_blk[:, :, 1, :, None] * o_slc
                + g_blk[:, :, 2, :, None] * o_win)

    out = lax.map(block, (jnp.arange(S // Q_BLOCK), _to_blocks(q), _to_blocks(gates)))
    return _from_blocks(out)

def _memory_attention(q, mem_k, mem_v):
    logits = jnp.einsum('bshd,bmhd->bhsm', q, mem_k).astype(jnp.float32) * HEAD_DIM ** -0.5
    p = jax.nn.softmax(logits, axis=-1).astype(mem_v.dtype)
    return jnp.einsum('bhsm,bmhd->bshd', p, mem_v)

def _layer(x, mem, positions, norm_g, w_in, kv_norm, w_uk, w_uv, fox_b, pe_k, pe_v,
           wc1_k, wc2_k, wc1_v, wc2_v, mem_norm, w_mem_kv, w_branch, w_out):
    B, S, _ = x.shape
    h = _rmsnorm(x, norm_g)
    p = _split_columns(h @ w_in)
    heads = lambda a: a.reshape(B, S, N_HEADS, HEAD_DIM)

    c_kv = _rmsnorm(p['dsa_ckv'], kv_norm)
    k_a = _rope(heads(c_kv @ w_uk), positions)
    v_a = heads(c_kv @ w_uv)
    q_a = _rope(heads(p['dsa_q']), positions)
    qi = _rope(p['idx_q'].reshape(B, S, IDX_HEADS, IDX_DIM), positions)
    ki = _rope(p['idx_k'], positions)
    y_a = _dsa_attention(q_a, k_a, v_a, qi, ki, p['idx_w'])

    log_f = jax.nn.log_sigmoid(p['fox_f'].astype(jnp.float32) + fox_b.astype(jnp.float32))
    y_b = _fox_attention(heads(p['fox_q']), heads(p['fox_k']), heads(p['fox_v']), log_f)

    y_c = _stick_breaking_attention(heads(p['sb_q']), heads(p['sb_k']), heads(p['sb_v']))

    q_d = _rope(heads(p['nsa_q']), positions)
    gates = jax.nn.sigmoid(p['nsa_g'].reshape(B, S, 3, N_HEADS))
    y_d = _nsa_attention(q_d, _rope(p['nsa_kc'], positions), p['nsa_vc'],
                         _rope(p['nsa_ks'], positions), p['nsa_vs'],
                         _rope(p['nsa_kw'], positions), p['nsa_vw'], gates,
                         pe_k, pe_v, wc1_k, wc2_k, wc1_v, wc2_v)

    mkv = _rmsnorm(mem, mem_norm) @ w_mem_kv
    mem_k = mkv[..., :BR_WIDTH].reshape(B, -1, N_HEADS, HEAD_DIM)
    mem_v = mkv[..., BR_WIDTH:].reshape(B, -1, N_HEADS, HEAD_DIM)
    y_e = _memory_attention(heads(p['mem_q']), mem_k, mem_v)

    ys = jnp.stack([
        y_a.reshape(B, S, BR_WIDTH) * jax.nn.silu(p['dsa_z']),
        y_b.reshape(B, S, BR_WIDTH) * jax.nn.silu(p['fox_z']),
        y_c.reshape(B, S, BR_WIDTH) * jax.nn.silu(p['sb_z']),
        y_d.reshape(B, S, BR_WIDTH) * jax.nn.silu(p['nsa_z']),
        y_e.reshape(B, S, BR_WIDTH) * jax.nn.silu(p['mem_z']),
    ], axis=2)
    merge = jax.nn.sigmoid(p['merge'].reshape(B, S, N_BRANCH, D_MODEL))
    merged = jnp.sum(merge * jnp.einsum('bsnc,ncd->bsnd', ys, w_branch), axis=2)
    return x + merged @ w_out

def first_inputs(seed: int = 0) -> dict:
    key = jax.random.key(seed)
    ks = jax.random.split(key, 24)
    f32 = jnp.float32

    def nrm(k, shape, fan_in):
        return jax.random.normal(k, shape, f32) * fan_in ** -0.5

    def gain(k, shape):
        return 1.0 + 0.02 * jax.random.normal(k, shape, f32)

    return {
        'x': jax.random.normal(ks[0], (BATCH, SEQ, D_MODEL), f32),
        'mem': jax.random.normal(ks[1], (BATCH, N_MEM, D_MODEL), f32),
        'positions': jnp.broadcast_to(jnp.arange(SEQ, dtype=jnp.int32), (BATCH, SEQ)),
        'norm_g': gain(ks[2], (DEPTH, D_MODEL)),
        'w_in': nrm(ks[3], (DEPTH, D_MODEL, N_IN), D_MODEL),
        'kv_norm': gain(ks[4], (DEPTH, KV_LATENT)),
        'w_uk': nrm(ks[5], (DEPTH, KV_LATENT, BR_WIDTH), KV_LATENT),
        'w_uv': nrm(ks[6], (DEPTH, KV_LATENT, BR_WIDTH), KV_LATENT),
        'fox_bias': jnp.linspace(1.0, 4.0, N_HEADS, dtype=f32)[None, :] + 0.1 * jax.random.normal(ks[7], (DEPTH, N_HEADS), f32),
        'nsa_pe_k': 0.1 * jax.random.normal(ks[8], (DEPTH, CMP_LEN, NSA_KV_DIM), f32),
        'nsa_pe_v': 0.1 * jax.random.normal(ks[9], (DEPTH, CMP_LEN, NSA_KV_DIM), f32),
        'nsa_wc1_k': nrm(ks[10], (DEPTH, CMP_LEN * NSA_KV_DIM, CMP_HIDDEN), CMP_LEN * NSA_KV_DIM),
        'nsa_wc2_k': nrm(ks[11], (DEPTH, CMP_HIDDEN, NSA_KV_DIM), CMP_HIDDEN),
        'nsa_wc1_v': nrm(ks[12], (DEPTH, CMP_LEN * NSA_KV_DIM, CMP_HIDDEN), CMP_LEN * NSA_KV_DIM),
        'nsa_wc2_v': nrm(ks[13], (DEPTH, CMP_HIDDEN, NSA_KV_DIM), CMP_HIDDEN),
        'mem_norm': gain(ks[14], (DEPTH, D_MODEL)),
        'w_mem_kv': nrm(ks[15], (DEPTH, D_MODEL, 2 * BR_WIDTH), D_MODEL),
        'w_branch': nrm(ks[16], (DEPTH, N_BRANCH, BR_WIDTH, D_MODEL), BR_WIDTH),
        'w_out': nrm(ks[17], (DEPTH, D_MODEL, D_MODEL), D_MODEL),
        'final_norm': gain(ks[18], (D_MODEL,)),
    }

def first_block(x, mem, positions, norm_g, w_in, kv_norm, w_uk, w_uv, fox_bias, nsa_pe_k, nsa_pe_v,
              nsa_wc1_k, nsa_wc2_k, nsa_wc1_v, nsa_wc2_v, mem_norm, w_mem_kv, w_branch, w_out, final_norm):
    for l in range(DEPTH):
        x = _layer(x, mem, positions, norm_g[l], w_in[l], kv_norm[l], w_uk[l], w_uv[l], fox_bias[l],
                   nsa_pe_k[l], nsa_pe_v[l], nsa_wc1_k[l], nsa_wc2_k[l], nsa_wc1_v[l], nsa_wc2_v[l],
                   mem_norm[l], w_mem_kv[l], w_branch[l], w_out[l])
    return _rmsnorm(x, final_norm)


GRID_W = 64
CTX_LEN = 256

CONV_DIM = 512
CONV_WIDTH = 31
MLSTM_HEADS = 4
MLSTM_QK = 64
MLSTM_V = 128
MLSTM_CHUNK = 64
AB_SIZES = (CONV_DIM, CONV_DIM, MLSTM_HEADS * MLSTM_QK, MLSTM_HEADS * MLSTM_QK,
            MLSTM_HEADS * MLSTM_V, MLSTM_HEADS * MLSTM_V, 4 * MLSTM_HEADS)
AB_IN = sum(AB_SIZES)
AB_OUT = CONV_DIM + MLSTM_HEADS * MLSTM_V

MLA_HEADS = 16
MLA_Q_LORA = 512
MLA_KV_LORA = 256
MLA_NOPE = 64
MLA_ROPE = 32
MLA_V = 64
MLA_QK = MLA_NOPE + MLA_ROPE
MLA_IN = MLA_Q_LORA + MLA_KV_LORA + MLA_ROPE
ROPE_BASE = 10000.0
ATTN_BLOCK = 128

FFN_DIM = 2816
FFN_CONV_WIDTH = 3


def _split_cols(a, sizes):
    return jnp.split(a, np.cumsum(sizes)[:-1].tolist(), axis=-1)

def _rms(x):
    xf = x.astype(jnp.float32)
    return (xf * lax.rsqrt(jnp.mean(xf * xf, axis=-1, keepdims=True) + EPS)).astype(x.dtype)

def _layer_norm(x, g, b):
    xf = x.astype(jnp.float32)
    mu = jnp.mean(xf, axis=-1, keepdims=True)
    var = jnp.mean(jnp.square(xf - mu), axis=-1, keepdims=True)
    return ((xf - mu) * lax.rsqrt(var + EPS)).astype(x.dtype) * g + b

def _modulate(x, shift, scale):
    return _rms(x) * (1 + scale) + shift

def _dwconv(x, w, b):
    k, ch = w.shape
    pad = (k - 1) // 2
    y = lax.conv_general_dilated(x, w[:, None, :].astype(x.dtype), (1,), [(pad, k - 1 - pad)],
                                 dimension_numbers=('NWC', 'WIO', 'NWC'), feature_group_count=ch)
    return y + b

def _zero_state(batch):
    return (jnp.zeros((batch, MLSTM_HEADS, MLSTM_V, MLSTM_QK), jnp.float32),
            jnp.zeros((batch, MLSTM_HEADS, MLSTM_QK), jnp.float32),
            jnp.zeros((batch, MLSTM_HEADS), jnp.float32))

def _mlstm_chunkwise(q, k, v, log_i, log_f, state):
    bsz, nh, t, _ = q.shape
    nc = t // MLSTM_CHUNK

    def chunks(a):
        return jnp.moveaxis(a.reshape(bsz, nh, nc, MLSTM_CHUNK, *a.shape[3:]), 2, 0)

    lower = jnp.tril(jnp.ones((MLSTM_CHUNK, MLSTM_CHUNK), bool))

    def step(carry, inp):
        c_mat, n_vec, m = carry
        qj, kj, vj, li, lf = inp
        b = jnp.cumsum(lf, axis=-1)
        log_d = jnp.where(lower, b[..., :, None] - b[..., None, :] + li[..., None, :], -jnp.inf)
        log_inter = b + m[..., None]
        m_row = jnp.maximum(log_inter, jnp.max(log_d, axis=-1))
        s = jnp.einsum('bhid,bhjd->bhij', qj, kj) * jnp.exp(log_d - m_row[..., None])
        inter = jnp.exp(log_inter - m_row)
        num = jnp.einsum('bhij,bhjv->bhiv', s, vj) + inter[..., None] * jnp.einsum('bhvd,bhid->bhiv', c_mat, qj)
        den = jnp.sum(s, axis=-1) + inter * jnp.einsum('bhd,bhid->bhi', n_vec, qj)
        h = num / jnp.maximum(jnp.abs(den), jnp.exp(-m_row))[..., None]
        b_last = b[..., -1]
        log_w = b_last[..., None] - b + li
        m_new = jnp.maximum(b_last + m, jnp.max(log_w, axis=-1))
        w = jnp.exp(log_w - m_new[..., None])
        decay = jnp.exp(b_last + m - m_new)
        c_new = decay[..., None, None] * c_mat + jnp.einsum('bhj,bhjv,bhjd->bhvd', w, vj, kj)
        n_new = decay[..., None] * n_vec + jnp.einsum('bhj,bhjd->bhd', w, kj)
        return (c_new, n_new, m_new), h

    state, h = lax.scan(step, state, (chunks(q), chunks(k), chunks(v), chunks(log_i), chunks(log_f)))
    return jnp.moveaxis(h, 0, 2).reshape(bsz, nh, t, -1), state

def _flip(t):
    return jnp.flip(t, axis=2)

def _ab_project(h, w_in, gate_bias):
    a, g, q, k, v, o, gates = _split_cols(h @ w_in, AB_SIZES)

    def heads(t, d):
        return t.reshape(*t.shape[:2], -1, d).transpose(0, 2, 1, 3).astype(jnp.float32)

    q = heads(q, MLSTM_QK)
    k = heads(k, MLSTM_QK) * (MLSTM_QK ** -0.5)
    v = heads(v, MLSTM_V)
    gates = (gates + gate_bias).astype(jnp.float32).transpose(0, 2, 1)
    ig_f, fg_f, ig_b, fg_b = jnp.split(gates, 4, axis=1)
    fwd = (ig_f, jax.nn.log_sigmoid(fg_f))
    bwd = (ig_b, jax.nn.log_sigmoid(fg_b))
    return a, g, q, k, v, o, fwd, bwd

def _conformer_mlstm_mixer(h_lat, h_ctx, w_in, gate_bias, conv_w, conv_b, ln_g, ln_b,
                           head_gain, w_out, with_ctx_out):
    lat = _ab_project(h_lat, w_in, gate_bias)
    ctx = _ab_project(h_ctx, w_in, gate_bias)
    zero = _zero_state(h_lat.shape[0])

    def scans(p, init_f, init_b):
        _, _, q, k, v, _, fwd, bwd = p
        h_f, st_f = _mlstm_chunkwise(q, k, v, fwd[0], fwd[1], init_f)
        h_b, st_b = _mlstm_chunkwise(_flip(q), _flip(k), _flip(v), _flip(bwd[0]), _flip(bwd[1]), init_b)
        return h_f + _flip(h_b), st_f, st_b

    h_ctx_seq, st_f, st_b = scans(ctx, zero, zero)
    h_lat_seq, _, _ = scans(lat, st_f, st_b)

    def merge(p, h_seq):
        a, g, _, _, _, o, _, _ = p
        u = _dwconv(a * jax.nn.sigmoid(g), conv_w, conv_b)
        u = jax.nn.silu(_layer_norm(u, ln_g, ln_b))
        hm = _rms(h_seq).transpose(0, 2, 1, 3)
        hm = hm.reshape(*hm.shape[:2], -1).astype(o.dtype) * head_gain * jax.nn.sigmoid(o)
        return jnp.concatenate([u, hm], axis=-1) @ w_out

    y_lat = merge(lat, h_lat_seq)
    y_ctx = merge(ctx, h_ctx_seq) if with_ctx_out else None
    return y_lat, y_ctx

def _axial_rope_tables(rows):
    row = jnp.repeat(jnp.arange(rows, dtype=jnp.float32), GRID_W)
    col = jnp.tile(jnp.arange(GRID_W, dtype=jnp.float32), rows)
    half = MLA_ROPE // 2
    inv_freq = ROPE_BASE ** (-jnp.arange(0, half, 2, dtype=jnp.float32) / half)
    ang = jnp.concatenate([row[:, None] * inv_freq, col[:, None] * inv_freq], axis=-1)
    return jnp.cos(ang), jnp.sin(ang)

def _rope_tail(t, cos, sin):
    nope, r = t[..., :MLA_NOPE], t[..., MLA_NOPE:]
    r = r.reshape(*r.shape[:-1], -1, 2)
    c = cos[None, :, None, :].astype(t.dtype)
    s = sin[None, :, None, :].astype(t.dtype)
    r1, r2 = r[..., 0], r[..., 1]
    rot = jnp.stack([r1 * c - r2 * s, r1 * s + r2 * c], axis=-1).reshape(*nope.shape[:-1], MLA_ROPE)
    return jnp.concatenate([nope, rot], axis=-1)

def _block_attention(q, k, v):
    bsz, tq, nh, dk = q.shape
    nb = tq // ATTN_BLOCK
    qb = jnp.moveaxis(q.reshape(bsz, nb, ATTN_BLOCK, nh, dk), 1, 0)
    scale = dk ** -0.5

    def one_block(qi):
        s = jnp.einsum('bqhd,bkhd->bhqk', qi, k).astype(jnp.float32) * scale
        p = jax.nn.softmax(s, axis=-1).astype(v.dtype)
        return jnp.einsum('bhqk,bkhd->bqhd', p, v)

    out = lax.map(one_block, qb)
    return jnp.moveaxis(out, 0, 1).reshape(bsz, tq, nh * v.shape[-1])

def _mla_mixer(h_lat, h_ctx, cos, sin, w_in, q_norm, kv_norm, w_uq, w_ukv, q_gain, k_gain,
               w_out, with_ctx_out):
    def queries(cq, rotate):
        q = (_rms(cq) * q_norm) @ w_uq
        q = _rms(q.reshape(*q.shape[:2], MLA_HEADS, MLA_QK)) * q_gain
        return _rope_tail(q, cos, sin) if rotate else q

    def keys_values(ckv, k_rope, rotate):
        ukv = ((_rms(ckv) * kv_norm) @ w_ukv).reshape(*ckv.shape[:2], MLA_HEADS, MLA_NOPE + MLA_V)
        k_nope, v = ukv[..., :MLA_NOPE], ukv[..., MLA_NOPE:]
        k_rope = jnp.broadcast_to(k_rope[:, :, None, :], (*k_nope.shape[:3], MLA_ROPE))
        k = _rms(jnp.concatenate([k_nope, k_rope], axis=-1)) * k_gain
        return (_rope_tail(k, cos, sin) if rotate else k), v

    cq_l, ckv_l, kr_l = _split_cols(h_lat @ w_in, (MLA_Q_LORA, MLA_KV_LORA, MLA_ROPE))
    ckv_c, kr_c = _split_cols(h_ctx @ w_in[:, MLA_Q_LORA:], (MLA_KV_LORA, MLA_ROPE))
    k_l, v_l = keys_values(ckv_l, kr_l, True)
    k_c, v_c = keys_values(ckv_c, kr_c, False)
    k_all = jnp.concatenate([k_c, k_l], axis=1)
    v_all = jnp.concatenate([v_c, v_l], axis=1)
    y_lat = _block_attention(queries(cq_l, True), k_all, v_all) @ w_out
    y_ctx = None
    if with_ctx_out:
        q_c = queries(h_ctx @ w_in[:, :MLA_Q_LORA], False)
        y_ctx = _block_attention(q_c, k_c, v_c) @ w_out
    return y_lat, y_ctx

def _conv_ffn(h, w_in, conv_w, conv_b, w_out):
    g, val = jnp.split(h @ w_in, 2, axis=-1)
    return (jax.nn.gelu(_dwconv(g, conv_w, conv_b), approximate=True) * val) @ w_out

def second_inputs(seed: int = 0) -> dict:
    key = jax.random.key(seed)
    ks = iter(jax.random.split(key, 32))
    n_even = (DEPTH + 1) // 2
    n_odd = DEPTH // 2
    f32 = jnp.float32

    def nrm(shape, scale):
        return jax.random.normal(next(ks), shape, f32) * scale

    def gain(shape):
        return 1.0 + nrm(shape, 0.1)

    inp = {}
    inp['x'] = nrm((BATCH, SEQ, D_MODEL), 1.0)
    inp['c'] = nrm((BATCH, D_MODEL), 1.0)
    inp['ctx'] = nrm((BATCH, CTX_LEN, D_MODEL), 1.0)
    inp['c_ctx'] = nrm((D_MODEL,), 1.0)
    inp['ada_w'] = nrm((DEPTH, D_MODEL, 6 * D_MODEL), 0.5 * D_MODEL ** -0.5)
    inp['ada_b'] = nrm((DEPTH, 6 * D_MODEL), 0.02)
    inp['ab_w_in'] = nrm((n_even, D_MODEL, AB_IN), D_MODEL ** -0.5)
    ig = nrm((n_even, 2, 1, MLSTM_HEADS), 0.1)
    fg = jnp.linspace(3.0, 6.0, MLSTM_HEADS, dtype=f32) + nrm((n_even, 2, 1, MLSTM_HEADS), 0.1)
    inp['ab_gate_bias'] = jnp.concatenate([ig, fg], axis=2).reshape(n_even, 4 * MLSTM_HEADS)
    inp['ab_conv_w'] = nrm((n_even, CONV_WIDTH, CONV_DIM), CONV_WIDTH ** -0.5)
    inp['ab_conv_b'] = nrm((n_even, CONV_DIM), 0.02)
    inp['ab_ln_g'] = gain((n_even, CONV_DIM))
    inp['ab_ln_b'] = nrm((n_even, CONV_DIM), 0.02)
    inp['ab_head_gain'] = gain((n_even, MLSTM_HEADS * MLSTM_V))
    inp['ab_w_out'] = nrm((n_even, AB_OUT, D_MODEL), AB_OUT ** -0.5)
    inp['mla_w_in'] = nrm((n_odd, D_MODEL, MLA_IN), D_MODEL ** -0.5)
    inp['mla_q_norm'] = gain((n_odd, MLA_Q_LORA))
    inp['mla_kv_norm'] = gain((n_odd, MLA_KV_LORA))
    inp['mla_w_uq'] = nrm((n_odd, MLA_Q_LORA, MLA_HEADS * MLA_QK), MLA_Q_LORA ** -0.5)
    inp['mla_w_ukv'] = nrm((n_odd, MLA_KV_LORA, MLA_HEADS * (MLA_NOPE + MLA_V)), MLA_KV_LORA ** -0.5)
    inp['mla_q_gain'] = gain((n_odd, MLA_QK))
    inp['mla_k_gain'] = gain((n_odd, MLA_QK))
    inp['mla_w_out'] = nrm((n_odd, MLA_HEADS * MLA_V, D_MODEL), (MLA_HEADS * MLA_V) ** -0.5)
    inp['ffn_w_in'] = nrm((DEPTH, D_MODEL, 2 * FFN_DIM), D_MODEL ** -0.5)
    inp['ffn_conv_w'] = nrm((DEPTH, FFN_CONV_WIDTH, FFN_DIM), FFN_CONV_WIDTH ** -0.5)
    inp['ffn_conv_b'] = nrm((DEPTH, FFN_DIM), 0.02)
    inp['ffn_w_out'] = nrm((DEPTH, FFN_DIM, D_MODEL), FFN_DIM ** -0.5)
    return inp

def second_block(x, c, ctx, c_ctx, ada_w, ada_b, ab_w_in, ab_gate_bias, ab_conv_w, ab_conv_b,
              ab_ln_g, ab_ln_b, ab_head_gain, ab_w_out, mla_w_in, mla_q_norm, mla_kv_norm,
              mla_w_uq, mla_w_ukv, mla_q_gain, mla_k_gain, mla_w_out, ffn_w_in, ffn_conv_w,
              ffn_conv_b, ffn_w_out):
    rows = x.shape[1] // GRID_W
    cos, sin = _axial_rope_tables(rows)
    xl, xc = x, ctx
    for layer in range(DEPTH):
        last = layer == DEPTH - 1
        j = layer // 2
        mod_l = jnp.split((jax.nn.silu(c) @ ada_w[layer] + ada_b[layer])[:, None, :], 6, axis=-1)
        mod_c = jnp.split(jax.nn.silu(c_ctx) @ ada_w[layer] + ada_b[layer], 6, axis=-1)
        h_lat = _modulate(xl, mod_l[0], mod_l[1])
        h_ctx = _modulate(xc, mod_c[0], mod_c[1])
        if layer % 2 == 0:
            y_lat, y_ctx = _conformer_mlstm_mixer(
                h_lat, h_ctx, ab_w_in[j], ab_gate_bias[j], ab_conv_w[j], ab_conv_b[j],
                ab_ln_g[j], ab_ln_b[j], ab_head_gain[j], ab_w_out[j], not last)
        else:
            y_lat, y_ctx = _mla_mixer(
                h_lat, h_ctx, cos, sin, mla_w_in[j], mla_q_norm[j], mla_kv_norm[j], mla_w_uq[j],
                mla_w_ukv[j], mla_q_gain[j], mla_k_gain[j], mla_w_out[j], not last)
        xl = xl + mod_l[2] * y_lat
        xl = xl + mod_l[5] * _conv_ffn(_modulate(xl, mod_l[3], mod_l[4]), ffn_w_in[layer],
                                       ffn_conv_w[layer], ffn_conv_b[layer], ffn_w_out[layer])
        if not last:
            xc = xc + mod_c[2] * y_ctx
            xc = xc + mod_c[5] * _conv_ffn(_modulate(xc, mod_c[3], mod_c[4]), ffn_w_in[layer],
                                           ffn_conv_w[layer], ffn_conv_b[layer], ffn_w_out[layer])
    return xl


def setup_inputs(seed=0):
    out = dict(first_inputs(seed))
    for name, value in second_inputs(seed + 1).items():
        if name != "x":
            out[name + "_2"] = value
    return out


def reference(
    x, mem, positions, norm_g, w_in, kv_norm, w_uk, w_uv, fox_bias, nsa_pe_k, nsa_pe_v,
    nsa_wc1_k, nsa_wc2_k, nsa_wc1_v, nsa_wc2_v, mem_norm, w_mem_kv, w_branch, w_out, final_norm,
    c_2, ctx_2, c_ctx_2, ada_w_2, ada_b_2, ab_w_in_2, ab_gate_bias_2, ab_conv_w_2, ab_conv_b_2,
    ab_ln_g_2, ab_ln_b_2, ab_head_gain_2, ab_w_out_2, mla_w_in_2, mla_q_norm_2, mla_kv_norm_2,
    mla_w_uq_2, mla_w_ukv_2, mla_q_gain_2, mla_k_gain_2, mla_w_out_2, ffn_w_in_2, ffn_conv_w_2,
    ffn_conv_b_2, ffn_w_out_2,
):
    x = first_block(
        x, mem, positions, norm_g, w_in, kv_norm, w_uk, w_uv, fox_bias, nsa_pe_k, nsa_pe_v,
        nsa_wc1_k, nsa_wc2_k, nsa_wc1_v, nsa_wc2_v, mem_norm, w_mem_kv, w_branch, w_out,
        final_norm,
    )
    return second_block(
        x, c_2, ctx_2, c_ctx_2, ada_w_2, ada_b_2, ab_w_in_2, ab_gate_bias_2, ab_conv_w_2,
        ab_conv_b_2, ab_ln_g_2, ab_ln_b_2, ab_head_gain_2, ab_w_out_2, mla_w_in_2, mla_q_norm_2,
        mla_kv_norm_2, mla_w_uq_2, mla_w_ukv_2, mla_q_gain_2, mla_k_gain_2, mla_w_out_2,
        ffn_w_in_2, ffn_conv_w_2, ffn_conv_b_2, ffn_w_out_2,
    )


_drawn_inputs = setup_inputs


def setup_inputs(seed=0):
    import zlib

    import numpy as np

    out = dict(_drawn_inputs(seed))
    spreads = {}
    factors = {'norm_g': 3.399,
     'kv_norm': 8.0,
     'nsa_pe_k': 8.0,
     'nsa_pe_v': 3.702,
     'mem_norm': 8.0,
     'final_norm': 2.674,
     'ab_conv_b_2': 8.0,
     'ab_ln_g_2': 3.483,
     'ab_ln_b_2': 8.0,
     'ab_head_gain_2': 4.635,
     'mla_q_norm_2': 8.0,
     'mla_kv_norm_2': 7.474,
     'mla_q_gain_2': 8.0,
     'mla_k_gain_2': 8.0,
     'ffn_conv_b_2': 8.0}
    for name, (base, spread) in spreads.items():
        noise = np.random.default_rng([zlib.crc32(name.encode()), seed]).standard_normal(out[name].shape)
        drawn = base * np.exp(spread * noise) if base else spread * noise
        out[name] = jnp.asarray(drawn.astype(out[name].dtype))
    for name, factor in factors.items():
        out[name] = (out[name] * factor).astype(out[name].dtype)
    return out
```

```python
from contextlib import ExitStack

import numpy as np

import concourse.bass as bass
from concourse import mybir

F32 = mybir.dt.float32
I32 = mybir.dt.int32
ALU = mybir.AluOpType
ACT = mybir.ActivationFunctionType
AX_X = mybir.AxisListType.X
P = 128
BANK = 512
NEG = -1.0e30
LOWEST = -3.0e38
EPS = 1e-6

D_MODEL, SEQ, DEPTH, N_MEM, CTX = 1024, 512, 2, 256, 256
HEADS, HD = 4, 64
BR = HEADS * HD
N_BRANCH = 5
IDX_HEADS, IDX_DIM = 4, 32
KV_LATENT = 128
CMP_LEN, CMP_STRIDE, CMP_HIDDEN = 32, 16, 128
N_CMP = (SEQ - CMP_LEN) // CMP_STRIDE + 1
TOPK = min(256, SEQ // 4)
CONV_DIM, CONV_WIDTH = 512, 31
ML_QK, ML_V = 64, 128
MLA_HEADS, MLA_Q_LORA, MLA_KV_LORA, MLA_NOPE, MLA_ROPE, MLA_V = 16, 512, 256, 64, 32, 64
MLA_QK = MLA_NOPE + MLA_ROPE
GRID_W = 64
FFN = 2816
KT = D_MODEL // P
QT = SEQ // P
TOK = CTX + SEQ
SCALE = HD ** -0.5

IN_LAYOUT = (
    ('dsa_q', BR), ('dsa_ckv', KV_LATENT), ('idx_q', IDX_HEADS * IDX_DIM), ('idx_k', IDX_DIM),
    ('idx_w', IDX_HEADS), ('dsa_z', BR),
    ('fox_q', BR), ('fox_k', BR), ('fox_v', BR), ('fox_f', HEADS), ('fox_z', BR),
    ('sb_q', BR), ('sb_k', BR), ('sb_v', BR), ('sb_z', BR),
    ('nsa_q', BR), ('nsa_kc', HD), ('nsa_vc', HD), ('nsa_ks', HD), ('nsa_vs', HD),
    ('nsa_kw', HD), ('nsa_vw', HD), ('nsa_g', 3 * HEADS), ('nsa_z', BR),
    ('mem_q', BR), ('mem_z', BR), ('merge', N_BRANCH * D_MODEL),
)
COL = {}
_off = 0
for _name, _n in IN_LAYOUT:
    COL[_name] = np.arange(_off, _off + _n)
    _off += _n


class Line:

    def __init__(self, eng, sem, chain):
        self.eng, self.sem, self.n, self.chain, self.seen = eng, sem, 0, chain, {}

    def wait(self, *marks):
        for m in marks:
            if m is not None and self.seen.get(m[0].name, 0) < m[1]:
                self.eng.wait_ge(m[0], m[1])
                self.seen[m[0].name] = m[1]

    def last(self):
        return (self.sem, self.n) if self.n else None

    def __call__(self, op, *args, after=(), mark=True, **kw):
        self.wait(*after)
        if self.chain:
            self.wait(self.last())
        ins = op(*args, **kw)
        if mark:
            self.n += 1
            ins.then_inc(self.sem, 1)
            return (self.sem, self.n)
        return None


class Buf:

    def __init__(self, t):
        self.t, self.free = t, []


class Ring:
    def __init__(self, bufs):
        self.bufs, self.i = bufs, 0

    def take(self):
        b = self.bufs[self.i % len(self.bufs)]
        self.i += 1
        return b


class Pack:

    def __init__(self, name):
        self.name, self.n, self.parts, self.t = name, 0, [], None

    def add(self, n, what):
        at = self.n
        self.n += n
        self.parts.append((at, n, what))
        return at

    def const(self, a):
        full = np.zeros((P, a.shape[1]), np.float32)
        full[:a.shape[0]] = a
        return self.add(a.shape[1], full)

    def param(self, name, idx, lead=0):
        idx = np.asarray(idx)
        full = np.zeros((P, idx.shape[1]), np.int64)
        full[:idx.shape[0]] = idx
        return self.add(idx.shape[1], (name, lead, full))

    def fill(self, inputs):
        out = np.zeros((P, self.n), np.float32)
        for at, n, what in self.parts:
            if isinstance(what, tuple):
                name, lead, idx = what
                a = inputs[name]
                a = a[lead] if lead is not None else a
                out[:, at:at + n] = np.where(idx < 0, np.float32(1), a.reshape(-1)[idx])
            else:
                out[:, at:at + n] = what
        return out


SLOT = 2048
NSLOT = 5


class Stream:

    def __init__(self, nc, pe, sb, sems):
        self.nc, self.pe, self.sems = nc, pe, sems
        self.slots = [sb(f"weight_slot{i}", [P, SLOT]) for i in range(NSLOT)]
        self.chunks = []
        self.pieces = []

    def piece(self, name, lead, rows, cols):
        rows, cols = np.asarray(rows), np.asarray(cols)
        nk, n = rows.shape[0], len(cols)
        size = nk * n
        assert size <= SLOT
        if not self.chunks or self.chunks[-1][0] + size > SLOT:
            self.chunks.append([0, None])
        c = len(self.chunks) - 1
        at = self.chunks[c][0]
        self.chunks[c][0] += size
        self.pieces.append((c, at, name, lead, rows, cols))
        t = self.slots[c % NSLOT][:, at:at + size].rearrange("p (k n) -> p k n", k=nk)
        loaded = (self.sems[c % NSLOT], 16 * (c // NSLOT + 1))
        self.pe.wait(loaded)
        return t, c

    def used(self, c, mark):
        self.chunks[c][1] = mark

    def issue(self, sp, dram):
        for c, (size, mark) in enumerate(self.chunks):
            if c >= NSLOT:
                sp.wait(self.chunks[c - NSLOT][1])
            sp.eng.dma_start(self.slots[c % NSLOT][:, 0:size], dram[c, :, 0:size]).then_inc(
                self.sems[c % NSLOT], 16)

    def fill(self, inputs):
        out = np.zeros((len(self.chunks), P, SLOT), np.float32)
        for c, at, name, lead, rows, cols in self.pieces:
            a = inputs[name]
            for i in lead:
                a = a[i]
            got = a[rows][:, :, cols] if a.ndim == 2 else None
            out[c, :, at:at + rows.shape[0] * len(cols)] = got.transpose(1, 0, 2).reshape(P, -1)
        return out


def rows_of(n, first=0):
    return first + np.arange(n * P).reshape(n, P)


class Core:

    def __init__(self, nc, ctx):
        self.nc, self.ctx = nc, ctx
        sem = lambda name: ctx.enter_context(nc.semaphore(name))
        self.sem = sem
        self.pe = Line(nc.tensor, sem("tensor_steps"), False)
        self.dve = Line(nc.vector, sem("vector_steps"), True)
        self.act = Line(nc.scalar, sem("scalar_steps"), True)
        self.pool = Line(nc.gpsimd, sem("gpsimd_steps"), True)
        self.sp = Line(nc.sync, sem("sync_steps"), False)
        self.psum = ctx.enter_context(nc.psum_tensor("psum", [P, 8 * BANK], F32))
        self.banks = [Buf(self.psum[:, i * BANK:(i + 1) * BANK]) for i in range(8)]
        self.turn = 0
        self.flip = 0
        self.used = {}
        self.fence = ()

    def sb(self, name, shape, stack=None, dt=F32):
        self.used[name] = self.used.get(name, 0) + 1
        if self.used[name] > 1:
            name = f"{name}_{self.used[name]}"
        return (stack or self.ctx).enter_context(self.nc.sbuf_tensor(name, shape, dt))

    def all_marks(self):
        return [m for m in (x.last() for x in (self.pe, self.dve, self.act, self.pool)) if m]

    def barrier(self):
        marks = self.all_marks()
        for line in (self.pe, self.dve, self.act, self.pool):
            line.wait(*marks)
        self.fence = tuple(marks)

    def next_banks(self, n=1):
        if self.turn % 8 + n > 8:
            self.turn += 8 - self.turn % 8
        i = self.turn % 8
        self.turn += n
        return self.claim(i, n)

    def claim(self, i, n=1):
        for b in self.banks[i:i + n]:
            self.pe.wait(*b.free)
        return i

    def bank(self, i, n=1):
        return self.psum[:, i * BANK:(i + n) * BANK]

    def release(self, i, n, *marks):
        for b in self.banks[i:i + n]:
            b.free = list(marks)

    def mm(self, out, lhsT, rhs, start, stop, mark=False, after=()):
        return self.pe(self.nc.tensor.matmul, out, lhsT, rhs, start=start, stop=stop, mark=mark,
                       after=after)

    def copy(self, out, in_, after=(), engine=None):
        if engine is None:
            self.flip += 1
            engine = self.act if self.flip % 2 else self.dve
        if engine is self.act:
            return self.act(self.nc.scalar.copy, out, in_, after=after)
        return self.dve(self.nc.vector.tensor_copy, out, in_, after=after)

    def project(self, w, chunk, m, x, spans, after=()):
        i = self.next_banks(len(spans))
        self.pe.wait(*after)
        nk = w.shape[1]
        for s, (lo, hi) in enumerate(spans):
            for k in range(nk):
                done = self.mm(self.bank(i + s)[0:m, 0:hi - lo], w[:, k, :], x[:, k, lo:hi],
                               k == 0, k == nk - 1, mark=(k == nk - 1))
        if chunk is not None:
            self.stream.used(chunk, done)
        return i, done

    def rsqrt_small(self, out, t, tmp, after=()):
        V, S = self.nc.vector, self.nc.scalar
        m = self.act(S.activation, tmp, t, ACT.Ln, after=after)
        m = self.act(S.activation, out, tmp, ACT.Exp, scale=-0.5)
        for _ in range(2):
            m = self.dve(V.tensor_tensor, tmp, out, out, ALU.mult, after=[m])
            m = self.dve(V.scalar_tensor_tensor, tmp, tmp, -0.5, t, ALU.mult, ALU.mult)
            m = self.dve(V.scalar_tensor_tensor, out, tmp, 1.5, out, ALU.add, ALU.mult)
        return m

    def token_rstd(self, sq, nk, width, ntile, cols, dim, after=()):
        V = self.nc.vector
        i = self.next_banks()
        self.pe.wait(*after)
        for t in range(ntile):
            for k in range(nk):
                done = self.mm(self.bank(i)[:, t:t + 1], sq[0:width, k, t * P:(t + 1) * P],
                               self.ones[0:width, 0:1], k == 0, k == nk - 1,
                               mark=(t == ntile - 1 and k == nk - 1))
        m = self.dve(V.tensor_scalar, self.tiny[:, 0:ntile], self.bank(i)[:, 0:ntile], 1.0 / dim, EPS,
                     ALU.mult, ALU.add, after=[done])
        self.release(i, 1, m)
        return self.rsqrt_small(cols, self.tiny[:, 0:ntile], self.tiny[:, 16:16 + ntile], after=[m])

    def spread(self, cols, ntile, after=()):
        V = self.nc.vector
        n = (ntile * P + BANK - 1) // BANK
        i = self.next_banks(n)
        for t in range(ntile):
            d = self.diag.take()
            m = self.dve(V.tensor_scalar, d.t[:, :], self.ident, cols[:, t:t + 1], None, ALU.mult,
                         after=list(d.free) + list(after))
            done = self.mm(self.bank(i, n)[:, t * P:(t + 1) * P], self.ones, d.t[:, :], True, True,
                           mark=True, after=[m])
            d.free = [done]
        return i, n, done

    def rms_features(self, x, nk, lo, hi, gain, out, sq, dim, shift=None, after=(), width=P,
                     out_free=(), func=ACT.Identity):
        V, S = self.nc.vector, self.nc.scalar
        ntile = (hi - lo) // P
        for k in range(nk):
            m = self.act(S.activation, sq[0:width, k, 0:hi - lo], x[0:width, k, lo:hi], ACT.Square,
                         after=after)
        rs = self.tiny[:, 32:32 + ntile]
        m = self.token_rstd(sq, nk, width, ntile, rs, dim, after=[m])
        i, n, done = self.spread(rs, ntile, after=[m])
        row = self.bank(i, n)
        for k in range(nk):
            m = self.dve(V.scalar_tensor_tensor, out[0:width, k, lo:hi], x[0:width, k, lo:hi], gain(k),
                         row[0:width, 0:hi - lo], ALU.mult, ALU.mult, after=[done] + list(out_free))
        self.release(i, n, m)
        if shift is not None:
            for k in range(nk):
                m = self.act(S.activation, out[0:width, k, lo:hi], out[0:width, k, lo:hi], func,
                             bias=shift(k), after=[m])
        return m


def softmax_attention(K, units, scratch, o_bank=7):
    V, S, T = K.nc.vector, K.nc.scalar, K.nc.tensor

    def scores(u):
        u.p = scratch.probs.take()
        u.c = scratch.cols.take()
        top, bias, total = (u.c.t[:, 4 * j:4 * j + 4] for j in range(3))
        for h in range(u.heads):
            K.claim(h)
            done = u.logits(h, K.bank(h)[:, 0:u.keys])
            m = K.dve(V.tensor_tensor_reduce, u.p.t[:, h, 0:u.keys], K.bank(h)[:, 0:u.keys], u.mask,
                      1.0, LOWEST, ALU.add, ALU.max, top[:, h:h + 1], after=[done] + u.p.free + u.c.free)
            K.release(h, 1, m)
        m = K.dve(V.tensor_scalar, bias[:, 0:u.heads], top[:, 0:u.heads], -SCALE, None, ALU.mult)
        for h in range(u.heads):
            e = K.act(S.activation, u.p.t[:, h, 0:u.keys], u.p.t[:, h, 0:u.keys], ACT.Exp,
                      bias=bias[:, h:h + 1], scale=SCALE, after=[m],
                      accum_out=None if u.keep is not None else total[:, h:h + 1])
        if u.keep is not None:
            for h in range(u.heads):
                e = K.dve(V.tensor_tensor_reduce, u.p.t[:, h, 0:u.keys], u.p.t[:, h, 0:u.keys], u.keep,
                          1.0, 0.0, ALU.mult, ALU.add, total[:, h:h + 1], after=[e])
            K.dve(V.tensor_scalar, total[:, 0:u.heads], total[:, 0:u.heads], 1e-30, None, ALU.max)
        u.inv = u.c.t[:, 12:12 + u.heads]
        K.dve(V.reciprocal, u.inv, total[:, 0:u.heads], after=[e])
        u.ready = e

    def turned(u, h):
        nb = (u.keys + P - 1) // P
        w = min(P, u.keys)
        i = 4 + K.t_turn % 3
        K.t_turn += 1
        K.claim(i)
        pt = scratch.turned.take()
        for b in range(nb):
            done = K.pe(T.transpose, K.bank(i)[0:w, b * P:(b + 1) * P], u.p.t[:, h, b * P:b * P + w],
                        K.ident, after=[u.ready], mark=(b == nb - 1))
        if h == u.heads - 1:
            u.p.free = [done]
        m = K.copy(pt.t[0:w, 0:nb * P], K.bank(i)[0:w, 0:nb * P], after=[done] + pt.free)
        K.release(i, 1, m)
        return pt, m, nb, w

    def weigh(u, h, pt, copied, nb, w):
        if h == 0:
            K.claim(o_bank)
        for b in range(nb):
            done = K.mm(K.bank(o_bank)[:, h * HD:(h + 1) * HD], pt.t[0:w, b * P:(b + 1) * P],
                        u.value(h, b), b == 0, b == nb - 1, mark=(b == nb - 1), after=[copied])
        pt.free = [done]
        if h == u.heads - 1:
            m = u.finish(u, K.bank(o_bank)[:, 0:u.heads * HD], done)
            u.c.free = [m]
            K.release(o_bank, 1, m)

    for i in range(len(units) + 1):
        if i < len(units):
            scores(units[i])
        if i >= 1:
            u = units[i - 1]
            waiting = None
            for h in range(u.heads):
                got = turned(u, h)
                if waiting:
                    weigh(u, *waiting)
                waiting = (h,) + got
            weigh(u, *waiting)


class Unit:

    def __init__(self, keys, logits, mask, keep, value, finish, qt):
        self.heads, self.keys, self.logits, self.mask, self.keep = HEADS, keys, logits, mask, keep
        self.value, self.finish, self.qt = value, finish, qt


class FirstBlock:
    def __init__(self, K, consts, small):
        self.K, self.c, self.small = K, consts, small

    def features(self, cols, l, x=None, name="w_in", k=KT, spans=((0, SEQ),), first=0, after=()):
        w, c = self.K.stream.piece(name, l, rows_of(k, first), cols)
        return self.K.project(w, c, len(cols), self.h if x is None else x, spans, after=after)

    def rope(self, i, done, out, tables, perm):
        K, V = self.K, self.K.nc.vector
        raw, tmp = self.raw.take(), self.rtmp.take()
        cos, sin = tables
        copied = K.copy(raw.t[:, :], K.bank(i), after=[done] + raw.free, engine=K.act)
        j = K.next_banks()
        swapped = K.mm(K.bank(j), perm, raw.t[:, :], True, True, mark=True, after=[copied])
        raw.free = [swapped]
        m = K.dve(V.tensor_tensor, out, K.bank(i), cos, ALU.mult, after=[copied])
        K.release(i, 1, m)
        m = K.dve(V.tensor_tensor, tmp.t[:, :], K.bank(j), sin, ALU.mult, after=[swapped])
        K.release(j, 1, m)
        return K.dve(V.tensor_tensor, out, out, tmp.t[:, :], ALU.add)

    def plain(self, i, done, out, scale=None):
        K, S = self.K, self.K.nc.scalar
        if scale is not None:
            m = K.act(S.activation, out, K.bank(i), ACT.Copy, scale=scale, after=[done])
        else:
            m = K.copy(out, K.bank(i), after=[done])
        K.release(i, 1, m)
        return m

    def values(self, cols, l, out, ntile=QT, x=None, name="w_in", k=KT, after=()):
        K = self.K
        x = self.h if x is None else x
        n = len(cols)
        w, c = K.stream.piece(name, l, rows_of(k), cols)
        per = BANK // n
        nb = (ntile + per - 1) // per
        i = K.next_banks(nb)
        K.pe.wait(*after)
        for t in range(ntile):
            at = t * n
            for kk in range(k):
                done = K.mm(K.bank(i, nb)[:, at:at + n], x[:, kk, t * P:(t + 1) * P], w[:, kk, :],
                            kk == 0, kk == k - 1, mark=(t == ntile - 1 and kk == k - 1))
        K.stream.used(c, done)
        m = K.copy(out, K.bank(i, nb)[:, 0:ntile * n], after=[done])
        K.release(i, nb, m)
        return m

    def gates(self, l):
        K, S = self.K, self.K.nc.scalar
        zs = ["dsa_z", "fox_z", "sb_z", "nsa_z", "mem_z"]
        groups = [np.concatenate([COL[zs[0]], COL[zs[1]]]), np.concatenate([COL[zs[2]], COL[zs[3]]]),
                  np.concatenate([COL[zs[4]], COL["nsa_g"], COL["idx_w"]])]
        half = KT // 2
        for g, cols in enumerate(groups):
            n = len(cols)
            first = K.next_banks(QT)
            for part in range(2):
                w, c = K.stream.piece("w_in", (l,), rows_of(half, part * half * P), cols)
                for t in range(QT):
                    for k in range(half):
                        kk = part * half + k
                        done = K.mm(K.bank(first + t)[:, 0:n], self.h[:, kk, t * P:(t + 1) * P],
                                    w[:, k, :], kk == 0, kk == KT - 1, mark=(k == half - 1),
                                    after=[self.h_ready])
                    if part:
                        if g < 2:
                            z = self.gate[:, 2 * g:2 * g + 2, t * BR:(t + 1) * BR]
                            m = K.act(S.activation, z,
                                      K.bank(first + t).rearrange("p (b c) -> p b c", b=2),
                                      ACT.Silu, after=[done])
                        else:
                            m = K.act(S.activation, self.gate[:, 4, t * BR:(t + 1) * BR],
                                      K.bank(first + t)[:, 0:BR], ACT.Silu, after=[done])
                            m = K.act(S.copy, self.idx_w[:, t, :],
                                      K.bank(first + t)[:, BR + 3 * HEADS:BR + 3 * HEADS + IDX_HEADS])
                            m = K.act(S.activation, self.mix[:, t, :],
                                      K.bank(first + t)[:, BR:BR + 3 * HEADS], ACT.Sigmoid)
                        K.release(first + t, 1, m)
                K.stream.used(c, done)
        self.gates_ready = m

    def turn_branch(self, b):
        K, T = self.K, self.K.nc.tensor
        i = K.next_banks(2)
        ready = K.dve.last()
        for j in range(2):
            for t in range(QT):
                done = K.pe(T.transpose, K.bank(i, 2)[:, j * SEQ + t * P:j * SEQ + (t + 1) * P],
                            self.gate[:, b, t * BR + j * P:t * BR + (j + 1) * P], K.ident,
                            after=[ready], mark=True)
        m = K.copy(self.gate[:, b, :], K.bank(i, 2), after=[done])
        K.release(i, 2, m)
        return m

    def finish_plain(self, b):
        def finish(u, o, done):
            K, V = self.K, self.K.nc.vector
            for h in range(HEADS):
                y = self.gate[:, b, u.qt * BR + h * HD:u.qt * BR + (h + 1) * HD]
                m = K.dve(V.scalar_tensor_tensor, y, o[:, h * HD:(h + 1) * HD], u.inv[:, h:h + 1], y,
                          ALU.mult, ALU.mult, after=[done, self.gates_ready])
            return m
        return finish

    def pair_logits(self, q, k, ready, extra=None, keys=None):
        K = self.K

        def logits_of(qt):
            def logits(h, out):
                lo, j = HD * (h % 2), h // 2
                n = out.shape[1]
                kt = k[lo:lo + HD, j, 0:n] if len(k.shape) == 3 else k[lo:lo + HD, 0:n]
                done = K.mm(out, q[lo:lo + HD, j, qt * P:(qt + 1) * P], kt, True, extra is None,
                            mark=extra is None, after=ready)
                if extra is not None:
                    a, b = extra
                    done = K.mm(out, a[32 * h:32 * h + 32, qt * P:(qt + 1) * P],
                                b[32 * h:32 * h + 32, 0:n], False, True, mark=True)
                return done
            return logits
        return logits_of

    def causal(self, qt):
        return self.c.causal[:, (QT - 1 - qt) * P:QT * P]

    def dsa(self, l, a):
        K, V, S = self.K, self.K.nc.vector, self.K.nc.scalar
        D = a.sub
        q, k, v = D("q", [P, 2, SEQ]), D("k", [P, 2, SEQ]), D("v", [P, QT, BR])
        c_kv, c_n = D("c_kv", [P, 1, SEQ]), D("c_n", [P, 1, SEQ])
        qi, ki = D("q_idx", [P, SEQ]), D("k_idx", [P, SEQ])
        rel, score = D("rel", [P, SEQ]), D("score", [P, SEQ])
        drop = [None] + [D(f"drop{t}", [P, (t + 1) * P]) for t in range(1, QT)]
        i, done = self.features(COL["dsa_ckv"], (l,), after=a.after)
        m = self.plain(i, done, c_kv[:, 0, :])
        K.dve.wait(m)
        n = K.rms_features(c_kv, 1, 0, SEQ, lambda kk: self.small.kv_norm[l], c_n, self.sq1, KV_LATENT,
                           after=[m])
        for j in range(2):
            i, done = self.features(COL["dsa_q"][j * P:(j + 1) * P], (l,))
            self.rope(i, done, q[:, j, :], self.rope64, self.c.perm64)
        i, done = self.features(COL["idx_q"], (l,))
        self.rope(i, done, qi[:, :], self.rope32, self.c.perm32)
        i, done = self.features(np.tile(COL["idx_k"], IDX_HEADS), (l,))
        ready_idx = self.rope(i, done, ki[:, :], self.rope32, self.c.perm32)
        for j in range(2):
            i, done = self.features(np.arange(j * P, (j + 1) * P), (l,), x=c_n, name="w_uk", k=1,
                                    after=[n])
            ready = self.rope(i, done, k[:, j, :], self.rope64, self.c.perm64)
        w, c = K.stream.piece("w_uv", (l,), rows_of(1), np.arange(BR))
        i = K.next_banks(2)
        for t in range(QT):
            done = K.mm(K.bank(i, 2)[:, t * BR:(t + 1) * BR], c_n[:, 0, t * P:(t + 1) * P], w[:, 0, :],
                        True, True, mark=True)
        K.stream.used(c, done)
        mv = K.copy(v[:, :, :].rearrange("p t c -> p (t c)"), K.bank(i, 2), after=[done])
        K.release(i, 2, mv)
        scale = IDX_DIM ** -0.5 * IDX_HEADS ** -0.5
        for t in range(1, QT):
            n = (t + 1) * P
            for h in range(IDX_HEADS):
                i = K.next_banks()
                done = K.mm(K.bank(i)[:, 0:n], qi[32 * h:32 * h + 32, t * P:(t + 1) * P],
                            ki[32 * h:32 * h + 32, 0:n], True, True, mark=True, after=[ready_idx])
                m = K.act(S.activation, rel[:, 0:n], K.bank(i)[:, 0:n], ACT.Relu,
                          after=[done, K.dve.last()])
                K.release(i, 1, m)
                wi = self.idx_w[:, t, h:h + 1]
                if h == 0:
                    K.dve(V.tensor_scalar, score[:, 0:n], rel[:, 0:n], wi, None, ALU.mult,
                          after=[m, self.gates_ready])
                else:
                    K.dve(V.scalar_tensor_tensor, score[:, 0:n], rel[:, 0:n], wi, score[:, 0:n],
                          ALU.mult, ALU.add, after=[m])
            K.dve(V.scalar_tensor_tensor, score[:, 0:n], score[:, 0:n], scale, self.causal(t),
                  ALU.mult, ALU.add)
            for _ in range(TOPK // 8):
                K.dve(V.max, self.top8[:, :], score[:, 0:n])
                K.dve(V.match_replace, score[:, 0:n], self.top8[:, :], score[:, 0:n], LOWEST)
            K.dve(V.tensor_scalar, drop[t][:, :], score[:, 0:n], LOWEST, NEG, ALU.is_gt, ALU.mult)
        logits = self.pair_logits(q, k, [ready])
        units = [Unit((t + 1) * P, logits(t), self.causal(0) if t == 0 else drop[t][:, :], None,
                      lambda h, b: v[:, b, h * HD:(h + 1) * HD], self.finish_plain(0), t)
                 for t in range(QT)]
        K.pe.wait(mv)
        softmax_attention(K, units, self.scratch)

    def log_sigmoid(self, x, e, out, width=None, after=()):
        K, V, S = self.K, self.K.nc.vector, self.K.nc.scalar
        m = K.dve(V.scalar_tensor_tensor, e, x, -1.0, x, ALU.mult, ALU.min, after=after)
        m = K.act(S.activation, e, e, ACT.Exp, after=[m])
        m = K.act(S.activation, e, e, ACT.Ln, bias=1.0)
        return K.dve(V.scalar_tensor_tensor, out, x, 0.0, e, ALU.min, ALU.subtract, after=[m])

    def fox(self, l, a):
        K, V = self.K, self.K.nc.vector
        D = a.sub
        q, k, v = D("q", [P, 2, SEQ]), D("k", [P, 2, SEQ]), D("v", [P, QT, BR])
        f, g = D("f", [P, SEQ]), D("g", [P, SEQ])
        fa, fb = D("decay_q", [P, SEQ]), D("decay_k", [P, SEQ])
        i, done = self.features(np.repeat(COL["fox_f"], 32), (l,), after=a.after)
        m = K.dve(V.tensor_scalar, f[:, :], K.bank(i), self.small.fox_bias[l], None, ALU.add,
                  after=[done])
        K.release(i, 1, m)
        self.log_sigmoid(f[:, :], g[:, :], f[:, :])
        K.dve(V.tensor_tensor_scan, g[:, :], self.ones_row[:, :], f[:, :], 0.0, ALU.mult, ALU.add)
        K.dve(V.tensor_scalar, fa[:, :], g[:, :], self.c.fox[:, 0:1], self.c.fox[:, 1:2], ALU.mult,
              ALU.add)
        mf = K.dve(V.tensor_scalar, fb[:, :], g[:, :], self.c.fox[:, 2:3], self.c.fox[:, 3:4],
                   ALU.mult, ALU.add)
        marks = [mf]
        for j in range(2):
            for name, dst in (("fox_q", q), ("fox_k", k)):
                i, done = self.features(COL[name][j * P:(j + 1) * P], (l,))
                marks.append(self.plain(i, done, dst[:, j, :]))
        marks.append(self.values(COL["fox_v"], (l,), v[:, :, :].rearrange("p t c -> p (t c)")))
        logits = self.pair_logits(q, k, marks, extra=(fa, fb))
        units = [Unit((t + 1) * P, logits(t), self.causal(t), None,
                      lambda h, b: v[:, b, h * HD:(h + 1) * HD], self.finish_plain(1), t)
                 for t in range(QT)]
        softmax_attention(K, units, self.scratch)

    def sb_attention(self, l, a):
        K, V, S = self.K, self.K.nc.vector, self.K.nc.scalar
        D = a.sub
        q, k, v = D("q", [P, 2, SEQ]), D("k", [P, 2, SEQ]), D("v", [P, QT, BR])
        lk = [D(f"log_keep{b}", [P, SEQ - b * P]) for b in range(QT)]
        e, z = D("e", [P, SEQ]), D("z", [P, SEQ])
        wt = [D(f"weight{b}", [P, SEQ - b * P]) for b in range(QT)]
        marks = []
        for j in range(2):
            i, done = self.features(COL["sb_q"][j * P:(j + 1) * P], (l,), after=a.after)
            marks.append(self.plain(i, done, q[:, j, :], scale=SCALE))
            i, done = self.features(COL["sb_k"][j * P:(j + 1) * P], (l,))
            marks.append(self.plain(i, done, k[:, j, :]))
        marks.append(self.values(COL["sb_v"], (l,), v[:, :, :].rearrange("p t c -> p (t c)")))
        read = []
        for h in range(HEADS):
            lo, j = HD * (h % 2), h // 2
            for b in range(QT):
                n = SEQ - b * P
                i = K.next_banks()
                done = K.mm(K.bank(i)[:, 0:n], k[lo:lo + HD, j, b * P:(b + 1) * P],
                            q[lo:lo + HD, j, b * P:SEQ], True, True, mark=True, after=marks)
                m = K.dve(V.tensor_scalar, z[:, 0:n], K.bank(i)[:, 0:n], -1.0, None, ALU.mult,
                          after=[done])
                K.release(i, 1, m)
                m = self.log_sigmoid(z[:, 0:n], e[:, 0:n], lk[b][:, :], after=read)
                m = K.dve(V.tensor_tensor, lk[b][:, 0:P], lk[b][:, 0:P], self.c.before01, ALU.mult)
            for b in range(QT):
                n = SEQ - b * P
                i = K.next_banks()
                bank = K.bank(i)
                K.mm(bank[:, 0:n], k[lo:lo + HD, j, b * P:(b + 1) * P], q[lo:lo + HD, j, b * P:SEQ],
                     True, False)
                K.mm(bank[:, 0:P], K.ident, self.c.before_add, False, False)
                K.mm(bank[:, 0:n], self.c.from_here, lk[b][:, :], False, b == QT - 1,
                     mark=True, after=[m])
                for b2 in range(b + 1, QT):
                    K.mm(bank[:, (b2 - b) * P:n], K.ones, lk[b2][:, :], False, b2 == QT - 1, mark=True)
                done = K.pe.last()
                w = K.act(S.activation, wt[b][:, :], bank[:, 0:n], ACT.Exp, after=[done] + read)
                K.release(i, 1, w)
            i = K.next_banks()
            for t in range(QT):
                for b in range(t + 1):
                    done = K.mm(K.bank(i)[:, t * HD:(t + 1) * HD], wt[b][:, (t - b) * P:(t - b + 1) * P],
                                v[:, b, h * HD:(h + 1) * HD], b == 0, b == t, mark=(b == t),
                                after=[w])
            read = [done]
            y = self.gate[:, 2, :].rearrange("p (t c) -> p t c", t=QT)[:, :, h * HD:(h + 1) * HD]
            m = K.dve(V.tensor_tensor, y,
                      K.bank(i)[:, 0:QT * HD].rearrange("p (t c) -> p t c", t=QT), y, ALU.mult,
                      after=[done, self.gates_ready])
            K.release(i, 1, m)

    def compress(self, l, a, x, which):
        K, V, S = self.K, self.K.nc.vector, self.K.nc.scalar
        blocks = a.sub("blocks_" + which, [P, CMP_LEN // 2, N_CMP])
        hid = a.sub("hidden_" + which, [P, N_CMP])
        pe_cols = self.small.pe[which][l]
        for g in range(2):
            src = bass.AP(tensor=x.tensor, offset=x[HD * g:HD * g + HD, g:g + 1].offset,
                          ap=[[x.ap[0][0], HD], [2, CMP_LEN // 2], [CMP_STRIDE, N_CMP]])
            p = pe_cols[HD * g:HD * g + HD, :]
            pe_b = bass.AP(tensor=p.tensor, offset=p.offset,
                           ap=[[p.ap[0][0], HD], [1, CMP_LEN // 2], [0, N_CMP]])
            m = K.dve(V.tensor_tensor, blocks[HD * g:HD * g + HD, :, :], src, pe_b, ALU.add,
                      after=[K.act.last()])
        rows = ((2 * np.arange(CMP_LEN // 2)[:, None] + np.arange(P)[None, :] // HD) * HD
                + np.arange(P)[None, :] % HD)
        w, c = K.stream.piece("nsa_wc1_" + which, (l,), rows, np.arange(CMP_HIDDEN))
        i = K.next_banks()
        for j in range(CMP_LEN // 2):
            done = K.mm(K.bank(i)[:, 0:N_CMP], w[:, j, :], blocks[:, j, :], j == 0,
                        j == CMP_LEN // 2 - 1, mark=(j == CMP_LEN // 2 - 1), after=[m])
        K.stream.used(c, done)
        m = K.act(S.activation, hid[:, :], K.bank(i)[:, 0:N_CMP], ACT.Silu, after=[done])
        K.release(i, 1, m)
        return hid, m

    def nsa(self, l, a):
        K, V, S = self.K, self.K.nc.vector, self.K.nc.scalar
        D = a.sub
        q = D("q", [P, 2, SEQ])
        twice = {n: D(n, [P, SEQ]) for n in ("nsa_kc", "nsa_vc", "nsa_ks", "nsa_kw")}
        v = D("v", [P, QT, 2 * HD])
        kct, vc = D("k_cmp", [P, N_CMP]), D("v_cmp", [N_CMP, HD])
        acc = D("mixed", [P, QT, BR])
        coef = D("coef", [P, HEADS])
        for n in twice:
            i, done = self.features(np.tile(COL[n], 2), (l,), after=a.after)
            if n == "nsa_vc":
                self.plain(i, done, twice[n][:, :])
            else:
                self.rope(i, done, twice[n][:, :], self.rope64, self.c.perm64)
        for j in range(2):
            i, done = self.features(COL["nsa_q"][j * P:(j + 1) * P], (l,))
            ready = self.rope(i, done, q[:, j, :], self.rope64, self.c.perm64)
        mv = self.values(np.concatenate([COL["nsa_vs"], COL["nsa_vw"]]), (l,),
                         v[:, :, :].rearrange("p t c -> p (t c)"))
        hid, m = self.compress(l, a, twice["nsa_kc"][:, :], "k")
        w, c = K.stream.piece("nsa_wc2_k", (l,), rows_of(1), np.tile(np.arange(HD), 2))
        i = K.next_banks()
        done = K.mm(K.bank(i)[:, 0:N_CMP], w[:, 0, :], hid[:, :], True, True, mark=True, after=[m])
        K.stream.used(c, done)
        m1 = K.copy(kct[:, :], K.bank(i)[:, 0:N_CMP], after=[done])
        K.release(i, 1, m1)
        hid, m = self.compress(l, a, twice["nsa_vc"][:, :], "v")
        w, c = K.stream.piece("nsa_wc2_v", (l,), rows_of(1), np.arange(HD))
        i = K.next_banks()
        done = K.mm(K.bank(i)[0:N_CMP, 0:HD], hid[:, :], w[:, 0, :], True, True, mark=True, after=[m])
        K.stream.used(c, done)
        m2 = K.copy(vc[:, :], K.bank(i)[0:N_CMP, 0:HD], after=[done])
        K.release(i, 1, m2)
        ks, kw = twice["nsa_ks"], twice["nsa_kw"]

        def finish(which):
            def end(u, o, done):
                m = K.dve(V.tensor_tensor, coef[:, :], u.inv,
                          self.mix[:, u.qt, which * HEADS:(which + 1) * HEADS], ALU.mult,
                          after=[self.gates_ready])
                for h in range(HEADS):
                    y = acc[:, u.qt, h * HD:(h + 1) * HD]
                    oh, ch = o[:, h * HD:(h + 1) * HD], coef[:, h:h + 1]
                    if which == 0:
                        m = K.dve(V.tensor_scalar, y, oh, ch, None, ALU.mult, after=[done])
                    else:
                        m = K.dve(V.scalar_tensor_tensor, y, oh, ch, y, ALU.mult, ALU.add,
                                  after=[done])
                if which == 2:
                    z = self.gate[:, 3, u.qt * BR:(u.qt + 1) * BR]
                    K.dve(V.tensor_tensor, z, acc[:, u.qt, :], z, ALU.mult)
                return m
            return end

        cmp_l = self.pair_logits(q, kct, [ready, m1, m2, mv])
        slc_l = self.pair_logits(q, ks, [ready])
        win_l = self.pair_logits(q, kw, [ready])
        units = []
        for t in range(QT):
            units.append(Unit(N_CMP, cmp_l(t), self.c.cmp_add[:, t * N_CMP:(t + 1) * N_CMP],
                              self.c.cmp_keep[:, t * N_CMP:(t + 1) * N_CMP],
                              lambda h, b: vc[:, :], finish(0), t))
            units.append(Unit((t + 1) * P, slc_l(t), self.causal(t), None,
                              lambda h, b: v[:, b, 0:HD], finish(1), t))
            units.append(Unit((t + 1) * P, win_l(t), self.causal(t), None,
                              lambda h, b: v[:, b, HD:2 * HD], finish(2), t))
        softmax_attention(K, units, self.scratch)

    def memory(self, l, a):
        K = self.K
        D = a.sub
        nt = N_MEM // P
        q, k, v = D("q", [P, 2, SEQ]), D("k", [P, 2, N_MEM]), D("v", [P, nt, BR])
        mem = D("mem_t", [P, KT, N_MEM])
        K.act.eng.dma_start(mem[:, :, :], self.dram_mem).then_inc(self.mem_sem, 16)
        loaded = (self.mem_sem, 16 * (l + 1))
        marks = []
        for j in range(2):
            i, done = self.features(COL["mem_q"][j * P:(j + 1) * P], (l,), after=a.after)
            marks.append(self.plain(i, done, q[:, j, :]))
        K.dve.wait(loaded)
        K.act.wait(loaded)
        n = K.rms_features(mem, KT, 0, N_MEM, lambda kk: self.small.mem_norm[l][kk], mem, self.sq8,
                           D_MODEL)
        for j in range(2):
            i, done = self.features(np.arange(j * P, (j + 1) * P), (l,), x=mem, name="w_mem_kv",
                                    spans=((0, N_MEM),), after=[n])
            m = K.copy(k[:, j, :], K.bank(i)[:, 0:N_MEM], after=[done])
            K.release(i, 1, m)
            marks.append(m)
        marks.append(self.values(BR + np.arange(BR), (l,), v[:, :, :].rearrange("p t c -> p (t c)"),
                                 ntile=nt, x=mem, name="w_mem_kv"))
        logits = self.pair_logits(q, k, marks)
        units = [Unit(N_MEM, logits(t), self.c.causal[:, 0:N_MEM], None,
                      lambda h, b: v[:, b, h * HD:(h + 1) * HD], self.finish_plain(4), t)
                 for t in range(QT)]
        softmax_attention(K, units, self.scratch)

    def merge(self, l, st):
        K, V, S = self.K, self.K.nc.vector, self.K.nc.scalar
        merged = K.sb("merged", [P, KT, SEQ], st)
        sig = Ring([Buf(K.sb(f"sig{i}", [P, SEQ], st)) for i in range(2)])
        part = K.sb("part", [P, SEQ], st)
        for d in range(KT):
            for b in range(N_BRANCH):
                i, done = self.features(COL["merge"][b * D_MODEL + d * P:b * D_MODEL + (d + 1) * P], (l,))
                s = sig.take()
                g = K.act(S.activation, s.t[:, :], K.bank(i), ACT.Sigmoid, after=[done] + s.free)
                K.release(i, 1, g)
                y = self.gate[:, b, :].rearrange("p (j n) -> p j n", j=2)
                i, done = self.features(np.arange(d * P, (d + 1) * P), (l, b), x=y, name="w_branch", k=2)
                dst = merged[:, d, :] if b == 0 else part[:, :]
                m = K.dve(V.tensor_tensor, dst, K.bank(i), s.t[:, :], ALU.mult, after=[done, g])
                K.release(i, 1, m)
                s.free = [m]
                if b:
                    m = K.dve(V.tensor_tensor, merged[:, d, :], merged[:, d, :], part[:, :], ALU.add)
        for d in range(KT):
            i, done = self.features(np.arange(d * P, (d + 1) * P), (l,), x=merged, name="w_out",
                                    after=[m])
            r = K.dve(V.tensor_tensor, self.x[:, d, :], K.bank(i), self.x[:, d, :], ALU.add,
                      after=[done])
            K.release(i, 1, r)
        return r

    def tables(self, st):
        K, V, S = self.K, self.K.nc.vector, self.K.nc.scalar
        pos_i = K.sb("pos_i", [P, SEQ], st, I32)
        pos, ang, turn, red = (K.sb(n, [P, SEQ], st) for n in ("pos", "angle", "turns", "reduced"))
        K.sp.eng.dma_start(pos_i[:, :], self.dram_pos.partition_broadcast(P)).then_inc(self.pos_sem, 16)
        K.dve(V.tensor_copy, pos[:, :], pos_i[:, :], after=[(self.pos_sem, 16), self.consts_loaded])
        two_pi = 2.0 * np.pi
        c1 = 6.28125
        c2 = float(np.float32(np.round((two_pi - c1) * 2.0 ** 20) / 2.0 ** 20))
        c3 = float(np.float32(two_pi - c1 - c2))
        magic = 1.5 * 2.0 ** 23
        for (cos, sin), inv, sign in ((self.rope64, self.c.inv64, self.c.sign64),
                                      (self.rope32, self.c.inv32, self.c.sign32)):
            K.dve(V.tensor_scalar, ang[:, :], pos[:, :], inv, None, ALU.mult,
                  after=[K.act.last()])
            K.dve(V.tensor_scalar, turn[:, :], ang[:, :], float(1.0 / two_pi), magic, ALU.mult, ALU.add)
            K.dve(V.tensor_scalar, turn[:, :], turn[:, :], magic, None, ALU.subtract)
            for part, src in ((c1, ang), (c2, red), (c3, red)):
                K.dve(V.scalar_tensor_tensor, red[:, :], turn[:, :], -part, src[:, :], ALU.mult, ALU.add)
            pi = float(np.nextafter(np.float32(np.pi), np.float32(0)))
            m = K.dve(V.tensor_scalar, red[:, :], red[:, :], pi, -pi, ALU.min, ALU.max)
            m = K.act(S.activation, sin[:, :], red[:, :], ACT.Sin, after=[m])
            K.dve(V.tensor_scalar, sin[:, :], sin[:, :], sign, None, ALU.mult, after=[m])
            K.dve(V.scalar_tensor_tensor, red[:, :], red[:, :], -1.0, red[:, :], ALU.mult, ALU.min)
            m = K.dve(V.tensor_scalar, red[:, :], red[:, :], float(np.pi / 2), None, ALU.add)
            m = K.act(S.activation, cos[:, :], red[:, :], ACT.Sin, after=[m])
        K.dve.wait(m)

    def run(self):
        K, nc = self.K, self.K.nc
        V = nc.vector
        outer = ExitStack()
        cos64, sin64, cos32, sin32 = (K.sb(n, [P, SEQ], outer) for n in ("cos64", "sin64", "cos32", "sin32"))
        self.rope64, self.rope32 = (cos64[:, :], sin64[:, :]), (cos32[:, :], sin32[:, :])
        self.ones_row = K.sb("ones_row", [P, SEQ], outer)
        K.dve(V.memset, self.ones_row[:, :], 1.0)
        st = ExitStack()
        self.tables(st)
        K.barrier()
        st.close()
        for l in range(DEPTH):
            with ExitStack() as st:
                self.h = K.sb("h", [P, KT, SEQ], st)
                self.gate = K.sb("gate", [P, N_BRANCH, QT * BR], st)
                self.idx_w = K.sb("idx_w", [P, QT, IDX_HEADS], st)
                self.mix = K.sb("mix", [P, QT, 3 * HEADS], st)
                with ExitStack() as s2:
                    self.sq8 = K.sb("squares", [P, KT, SEQ], s2)
                    self.h_ready = K.rms_features(self.x, KT, 0, SEQ, lambda k: self.small.norm_g[l][k],
                                                  self.h, self.sq8, D_MODEL)
                    self.gates(l)
                    K.barrier()
                with ExitStack() as s2:
                    self.raw = Ring([Buf(K.sb(f"raw{i}", [P, SEQ], s2)) for i in range(2)])
                    self.rtmp = Ring([Buf(K.sb(f"rtmp{i}", [P, SEQ], s2)) for i in range(1)])
                    self.sq1 = K.sb("sq1", [P, 1, SEQ], s2)
                    self.top8 = K.sb("top8", [P, 8], s2)
                    self.scratch = Scratch(K, s2)
                    arenas = [Arena(K, s2, "big", 32 * 1024), Arena(K, s2, "small", 29 * 1024)]
                    for n, (b, branch) in enumerate(((0, self.dsa), (1, self.fox), (3, self.nsa),
                                                     (2, self.sb_attention))):
                        a = arenas[n % 2]
                        a.open()
                        branch(l, a)
                        self.turn_branch(b)
                        a.close()
                    K.barrier()
                with ExitStack() as s2:
                    self.sq8 = K.sb("squares", [P, KT, N_MEM], s2)
                    self.scratch = Scratch(K, s2)
                    a = Arena(K, s2, "mem", 20 * 1024)
                    a.after = list(K.fence)
                    a.open()
                    self.memory(l, a)
                    self.turn_branch(4)
                    K.barrier()
                with ExitStack() as s2:
                    self.merge(l, s2)
                    K.barrier()
        with ExitStack() as st:
            sq = K.sb("squares", [P, KT, SEQ], st)
            K.rms_features(self.x, KT, 0, SEQ, lambda k: self.small.final_norm[k], self.x, sq, D_MODEL)
            K.barrier()
        outer.close()


class Scratch:

    def __init__(self, K, st, heads=HEADS, keys=SEQ, turned=4):
        self.probs = Ring([Buf(K.sb(f"probs{i}", [P, heads, keys], st)) for i in range(2)])
        self.turned = Ring([Buf(K.sb(f"turned{i}", [P, keys], st)) for i in range(turned)])
        self.cols = Ring([Buf(K.sb(f"softmax_cols{i}", [P, 16], st)) for i in range(3)])


class Arena:

    def __init__(self, K, st, name, size):
        self.K, self.t, self.size = K, K.sb("arena_" + name, [P, size // 4], st), size // 4
        self.after = []

    def open(self):
        self.at = 0
        for line in (self.K.dve, self.K.act, self.K.pool, self.K.pe):
            line.wait(*self.after)

    def sub(self, name, shape):
        n = int(np.prod(shape[1:]))
        if not self.at + n <= self.size:
            raise ValueError(name)
        t = self.t[0:shape[0], self.at:self.at + n]
        self.at += n
        if len(shape) == 3:
            return t.rearrange("p (a b) -> p a b", a=shape[1])
        return t

    def close(self):
        self.after = self.K.all_marks()


AB_COL, _o = {}, 0
for _name, _n in (("a", CONV_DIM), ("g", CONV_DIM), ("q", HEADS * ML_QK), ("k", HEADS * ML_QK),
                  ("v", HEADS * ML_V), ("o", HEADS * ML_V), ("gates", 4 * HEADS)):
    AB_COL[_name] = np.arange(_o, _o + _n)
    _o += _n
TT = TOK // P
CT = CTX // P
PAD = (CONV_WIDTH - 1) // 2
FT = FFN // P
BOTH = ((0, CTX), (CTX, TOK))
LATENT = ((CTX, TOK),)


class SecondBlock:

    def __init__(self, K, consts, small):
        self.K, self.c, self.small = K, consts, small

    def wide(self, w, chunk, x, spans, m=P, after=(), keep=None, k0=0, k1=None, last=True):
        K = self.K
        nk = w.shape[1]
        i = K.next_banks(2) if keep is None else keep
        K.pe.wait(*after)
        for lo, hi in spans:
            for k in range(nk):
                first, end = k == 0 and k0 == 0, k == nk - 1 and last
                done = K.mm(K.bank(i, 2)[0:m, BANK - CTX + lo:BANK - CTX + hi], w[:, k, :],
                            x[:, k0 + k, lo:hi], first, end, mark=(k == nk - 1))
        K.stream.used(chunk, done)
        return i, done

    def pair(self, i, lo=0, hi=TOK, m=P):
        return self.K.bank(i, 2)[0:m, BANK - CTX + lo:BANK - CTX + hi]

    def modulation(self, l):
        K, V = self.K, self.K.nc.vector
        n = 6 * KT
        i = K.next_banks()
        for j in range(n):
            w, c = K.stream.piece("ada_w_2", (l,), rows_of(KT), np.arange(j * P, (j + 1) * P))
            for k in range(KT):
                done = K.mm(K.bank(i)[:, 2 * j:2 * j + 2], w[:, k, :], self.silu_c[:, k, :], k == 0,
                            k == KT - 1, mark=(k == KT - 1), after=[self.silu_ready])
            K.stream.used(c, done)
        b = self.small.ada_b[l]
        bias = bass.AP(tensor=b.tensor, offset=b.offset, ap=[[b.ap[0][0], P], [1, n], [0, 2]])
        mods = self.mods[l]
        m = K.dve(V.tensor_tensor, mods[:, :, :], K.bank(i)[:, 0:2 * n].rearrange("p (j s) -> p j s", s=2),
                  bias, ALU.add, after=[done])
        K.release(i, 1, m)
        for s in (1, 4):
            part = mods[:, s * KT:(s + 1) * KT, :]
            m = K.dve(V.tensor_scalar, part, part, 1.0, None, ALU.add)
        self.mods_ready = m

    def mod(self, l, which, k, side):
        return self.mods[l][:, which * KT + k, side:side + 1]

    def modulate(self, l, shift, scale, h, sq, with_ctx=True):
        K = self.K
        K.act.wait(self.mods_ready)
        sides = [(0, self.x, CTX, SEQ)] + ([(1, self.xc, 0, CTX)] if with_ctx else [])
        for side, x, at, n in sides:
            m = K.rms_features(x, KT, 0, n, lambda k: self.mod(l, scale, k, side),
                               h[:, :, at:at + n], sq, D_MODEL,
                               shift=lambda k: self.mod(l, shift, k, side), after=[K.dve.last()])
        return m

    def residual(self, i, done, l, which, d, with_ctx=True):
        K, V = self.K, self.K.nc.vector
        m = K.dve(V.scalar_tensor_tensor, self.x[:, d, :], self.pair(i, CTX, TOK),
                  self.mod(l, which, d, 0), self.x[:, d, :], ALU.mult, ALU.add, after=[done])
        if with_ctx:
            m = K.dve(V.scalar_tensor_tensor, self.xc[:, d, :], self.pair(i, 0, CTX),
                      self.mod(l, which, d, 1), self.xc[:, d, :], ALU.mult, ALU.add)
        K.release(i, 2, m)
        return m

    def conformer(self, l, st):
        K, V, S, T = self.K, self.K.nc.vector, self.K.nc.scalar, self.K.nc.tensor
        y = K.sb("mixed_features", [P, 2 * HEADS, TOK], st)
        q, k = K.sb("ml_q", [P, 2, TOK], st), K.sb("ml_k", [P, 2, TOK], st)
        v = K.sb("ml_v", [P, TT, HEADS, ML_V + 1], st)
        rows_r = K.sb("ml_rows", [64, TOK], st)
        cols = K.sb("ml_cols", [P, TT, P], st)
        with ExitStack() as s1:
            h = K.sb("h2", [P, KT, TOK], s1)
            with ExitStack() as s2:
                sq = K.sb("squares2", [P, KT, SEQ], s2)
                ready = self.modulate(l, 0, 1, h, sq)
                K.barrier()
            lat0 = 3 * PAD + CTX
            up = K.sb("padded", [P, 4, CTX + SEQ + 4 * PAD], s1)
            sig = K.sb("sig2", [P, TOK], s1)
            pre, tmp = K.sb("gate_pre", [P, TOK], s1), K.sb("gate_tmp", [P, TOK], s1)
            stack = K.sb("gate_stack", [P, TOK], s1)
            b, cmx = K.sb("gate_sum", [64, TOK], s1), K.sb("gate_max", [64, TOK], s1)
            one = K.sb("one_row", [64, TOK], s1)
            mz = K.pool(K.nc.gpsimd.memset, up[:, :, :], 0.0)
            m1 = K.pool(K.nc.gpsimd.memset, v[:, :, :, ML_V:ML_V + 1], 1.0)
            m2 = K.pool(K.nc.gpsimd.memset, one[:, :], 1.0)
            for c in range(4):
                w, ch = K.stream.piece("ab_w_in_2", (0,), rows_of(KT), AB_COL["g"][c * P:(c + 1) * P])
                i, done = self.wide(w, ch, h, BOTH, after=[ready])
                g = K.act(S.activation, sig[:, :], self.pair(i), ACT.Sigmoid,
                          after=[done, K.dve.last()])
                K.release(i, 2, g)
                w, ch = K.stream.piece("ab_w_in_2", (0,), rows_of(KT), AB_COL["a"][c * P:(c + 1) * P])
                i, done = self.wide(w, ch, h, BOTH)
                K.dve(V.tensor_tensor, up[:, c, PAD:PAD + CTX], self.pair(i, 0, CTX), sig[:, 0:CTX],
                      ALU.mult, after=[done, g, mz])
                m = K.dve(V.tensor_tensor, up[:, c, lat0:lat0 + SEQ], self.pair(i, CTX, TOK),
                          sig[:, CTX:TOK], ALU.mult)
                K.release(i, 2, m)
            g4 = AB_COL["gates"].reshape(4, HEADS)[[0, 2, 1, 3]]
            w, ch = K.stream.piece("ab_w_in_2", (0,), rows_of(KT), np.tile(g4, (1, 32 // HEADS)).ravel())
            i, done = self.wide(w, ch, h, BOTH)
            m = K.dve(V.tensor_scalar, pre[:, :], self.pair(i), self.small.gate_bias, None, ALU.add,
                      after=[done])
            K.release(i, 2, m)
            fg, e = pre[64:128, :], tmp[64:128, :]
            K.dve(V.scalar_tensor_tensor, e, fg, -1.0, fg, ALU.mult, ALU.min)
            K.act(S.activation, e, e, ACT.Exp, after=[K.dve.last()])
            m = K.act(S.activation, e, e, ACT.Ln, bias=1.0)
            lf = tmp[0:64, :]
            K.dve(V.scalar_tensor_tensor, lf, fg, 0.0, e, ALU.min, ALU.subtract, after=[m])

            def scans(out, data, op, init):
                K.dve(V.tensor_tensor_scan, out[0:32, :], one[0:32, :], data[0:32, :], init, ALU.mult,
                      op, after=[m2])
                K.dve(V.tensor_tensor_scan, out[32:64, 0:CTX][:, ::-1], one[32:64, 0:CTX],
                      data[32:64, 0:CTX][:, ::-1], init, ALU.mult, op)
                K.dve(V.tensor_tensor_scan, out[32:64, CTX:TOK][:, ::-1], one[32:64, 0:SEQ],
                      data[32:64, CTX:TOK][:, ::-1], out[32:64, 0:1], ALU.mult, op)

            scans(b, lf, ALU.add, 0.0)
            K.dve(V.tensor_tensor, stack[0:64, :], pre[0:64, :], b[:, :], ALU.subtract)
            scans(cmx, stack, ALU.max, LOWEST)
            K.dve(V.tensor_tensor, cmx[:, :], cmx[:, :], b[:, :], ALU.add)
            K.dve(V.tensor_scalar, cmx[:, :], cmx[:, :], 0.0, None, ALU.max)
            rows_ready = K.dve(V.tensor_tensor, rows_r[:, :], b[:, :], cmx[:, :], ALU.subtract)
            m = K.act(S.activation, stack[64:128, :], cmx[:, :], ACT.Exp, scale=-1.0,
                      after=[rows_ready])
            i = K.next_banks(2)
            for t in range(TT):
                done = K.pe(T.transpose, K.bank(i, 2)[:, t * P:(t + 1) * P],
                            stack[:, t * P:(t + 1) * P], K.ident, after=[m], mark=True)
            m = K.act(S.copy, cols[:, :, :].rearrange("p t c -> p (t c)"), K.bank(i, 2)[:, 0:TOK],
                      after=[done])
            K.release(i, 2, m)
            cols_ready = m
            for name, dst, scale in (("q", q, 1.0), ("k", k, ML_QK ** -0.5)):
                for j in range(2):
                    w, ch = K.stream.piece("ab_w_in_2", (0,), rows_of(KT),
                                           AB_COL[name][j * P:(j + 1) * P])
                    i, done = self.wide(w, ch, h, BOTH)
                    m = K.act(S.activation, dst[:, j, :], self.pair(i), ACT.Copy, scale=scale,
                              after=[done])
                    K.release(i, 2, m)
            half = KT // 2
            for c in range(2):
                first = K.next_banks(3)
                for part in range(2):
                    w, ch = K.stream.piece("ab_w_in_2", (0,), rows_of(half, part * half * P),
                                           AB_COL["v"])
                    for t in range(3):
                        tt = 3 * c + t
                        for kk in range(half):
                            kg = part * half + kk
                            done = K.mm(K.bank(first + t), h[:, kg, tt * P:(tt + 1) * P], w[:, kk, :],
                                        kg == 0, kg == KT - 1, mark=(kk == half - 1))
                        if part:
                            m = K.act(S.copy, v[:, tt, :, 0:ML_V],
                                      K.bank(first + t).rearrange("p (h d) -> p h d", h=HEADS),
                                      after=[done])
                            K.release(first + t, 1, m)
                    K.stream.used(ch, done)
            for c in range(4):
                w, ch = K.stream.piece("ab_w_in_2", (0,), rows_of(KT), AB_COL["o"][c * P:(c + 1) * P])
                i, done = self.wide(w, ch, h, BOTH)
                m = K.act(S.activation, y[:, 4 + c, :], self.pair(i), ACT.Sigmoid, after=[done])
                K.release(i, 2, m)
            for c in range(4):
                i = K.next_banks(2)
                K.dve.wait(*K.banks[i].free, *K.banks[i + 1].free)
                cw = self.small.conv_w[c]
                for lo, n, at in ((0, CTX, 0), (CTX, SEQ, lat0 - PAD)):
                    acc = self.pair(i, lo, lo + n)
                    K.dve(V.tensor_scalar, acc, up[:, c, at:at + n], cw[:, 0:1], self.small.conv_b[c],
                          ALU.mult, ALU.add)
                    for j in range(1, CONV_WIDTH):
                        m = K.dve(V.scalar_tensor_tensor, acc, up[:, c, at + j:at + j + n],
                                  cw[:, j:j + 1], acc, ALU.mult, ALU.add)
                m = K.act(S.copy, y[:, c, :], self.pair(i), after=[m])
                K.release(i, 2, m)
            K.barrier()
        with ExitStack() as s1:
            sq = K.sb("squares3", [P, 4, TOK], s1)
            i = K.next_banks(2)
            for lo, hi in BOTH:
                for c in range(4):
                    done = K.mm(self.pair(i, lo, hi), K.ones, y[:, c, lo:hi], c == 0, c == 3,
                                mark=(c == 3))
            for c in range(4):
                m = K.dve(V.scalar_tensor_tensor, y[:, c, :], self.pair(i), -1.0 / CONV_DIM, y[:, c, :],
                          ALU.mult, ALU.add, after=[done])
            K.release(i, 2, m)
            K.rms_features(y[:, 0:4, :], 4, 0, TOK, lambda c: self.small.ln_g[c], y[:, 0:4, :], sq,
                           CONV_DIM, shift=lambda c: self.small.ln_b[c], after=[m], func=ACT.Silu)
            K.barrier()
        with ExitStack() as s1:
            self.mlstm(l, s1, y, q, k, v, rows_r, cols, cols_ready, rows_ready)
            K.barrier()
        for d in range(KT):
            w, ch = K.stream.piece("ab_w_out_2", (0,), rows_of(KT), np.arange(d * P, (d + 1) * P))
            i, done = self.wide(w, ch, y, BOTH)
            self.residual(i, done, l, 2, d)

    def mlstm(self, l, st, y, q, k, v, rows_r, cols, cols_ready, rows_ready):
        K, V, S, T = self.K, self.K.nc.vector, self.K.nc.scalar, self.K.nc.tensor
        hs = K.sb("ml_out", [P, TT, HEADS * ML_V], st)
        weights = Ring([Buf(K.sb(f"ml_weights{i}", [P, TT, TOK], st)) for i in range(2)])
        rowdiag = Ring([Buf(K.sb(f"ml_diag{i}", [P, TT, P], st)) for i in range(2)])
        den = K.sb("ml_den", [P, 16], st)
        todo = [(d, h) for h in range(HEADS) for d in range(2)]

        def seen_by(d, kb):
            if d == 0:
                return [(kb + 1, TT)] if kb + 1 < TT else []
            if kb < CT:
                return ([(0, kb)] if kb else []) + [(CT, TT)]
            return [(CT, kb)] if kb > CT else []

        def rows_of_head(d, h):
            r = 32 * d + h
            one = K.ident[0:64, r:r + 1]
            sel = bass.AP(tensor=one.tensor, offset=one.offset, ap=[[one.ap[0][0], 64], [0, P]])
            i = 0
            K.claim(i, 2)
            for lo, hi in BOTH:
                done = K.mm(self.pair(i, lo, hi), sel, rows_r[0:64, lo:hi], True, True, mark=True,
                            after=[rows_ready])
            rd = rowdiag.take()
            mask = self.c.ml_mask[d]
            mask6 = bass.AP(tensor=mask.tensor, offset=mask.offset,
                            ap=[[mask.ap[0][0], P], [0, TT], [1, P]])
            m = K.dve(V.tensor_tensor, rd.t[:, :, :], self.pair(i).rearrange("p (t c) -> p t c", t=TT),
                      mask6, ALU.add, after=[done] + rd.free)
            return i, rd, m

        def make(d, h):
            i, rd, m = rows_of_head(d, h)
            w = weights.take()
            lo_p, j = ML_QK * (h % 2), h // 2
            for kb in range(TT):
                u = cols[:, kb, 32 * d + h:32 * d + h + 1]
                K.act(S.activation, w.t[:, kb, kb * P:(kb + 1) * P], rd.t[:, kb, :], ACT.Exp, bias=u,
                      after=[m, cols_ready] + w.free)
                for a, b in seen_by(d, kb):
                    K.act(S.activation, w.t[:, kb, a * P:b * P], self.pair(i, a * P, b * P), ACT.Exp,
                          bias=u)
            e = K.act.last()
            rd.free = [e]
            K.release(i, 2, e)
            for kb in range(TT):
                s = 2 + 2 * (kb % 2)
                K.claim(s, 2)
                ranges = sorted(seen_by(d, kb) + [(kb, kb + 1)])
                joined = [list(ranges[0])]
                for a, b in ranges[1:]:
                    if a == joined[-1][1]:
                        joined[-1][1] = b
                    else:
                        joined.append([a, b])
                for a, b in joined:
                    for lo, hi in BOTH:
                        x0, x1 = max(a * P, lo), min(b * P, hi)
                        if x0 < x1:
                            done = K.mm(self.pair(s, x0, x1), k[lo_p:lo_p + ML_QK, j, kb * P:(kb + 1) * P],
                                        q[lo_p:lo_p + ML_QK, j, x0:x1], True, True, mark=True)
                for a, b in joined:
                    m = K.dve(V.tensor_tensor, w.t[:, kb, a * P:b * P], self.pair(s, a * P, b * P),
                              w.t[:, kb, a * P:b * P], ALU.mult, after=[done, e])
                K.release(s, 2, m)
            return w, m

        def read(d, h, w, ready):
            n = ML_V + 1
            K.claim(6, 2)
            place = lambda t: 6 * BANK + (t // 3) * BANK + (t % 3) * n
            for t in range(TT):
                kbs = [kb for kb in range(TT) if kb == t or any(a <= t < b for a, b in seen_by(d, kb))]
                for kb in kbs:
                    done = K.mm(K.psum[:, place(t):place(t) + n], w.t[:, kb, t * P:(t + 1) * P],
                                v[:, kb, h, :], kb == kbs[0], kb == kbs[-1], mark=(kb == kbs[-1]),
                                after=[ready])
            w.free = [done]
            o2 = K.bank(6, 2).rearrange("p (b c) -> p b c", b=2)
            dcol = o2[:, :, 0:3 * n].rearrange("p b (t c) -> p b t c", t=3)[:, :, :, ML_V]
            d6 = den[:, 0:TT].rearrange("p (b t) -> p b t", b=2)
            K.dve(V.tensor_scalar, d6, dcol, -1.0, None, ALU.mult, after=[done])
            K.dve(V.tensor_tensor, d6, dcol, d6, ALU.max)
            K.dve(V.tensor_tensor, den[:, 0:TT], den[:, 0:TT], cols[:, :, 64 + 32 * d + h], ALU.max)
            K.dve(V.reciprocal, den[:, 0:TT], den[:, 0:TT])
            for t in range(TT):
                o = hs[:, t, h * ML_V:(h + 1) * ML_V]
                num = K.psum[:, place(t):place(t) + ML_V]
                if d == 0:
                    m = K.dve(V.tensor_scalar, o, num, den[:, t:t + 1], None, ALU.mult)
                else:
                    m = K.dve(V.scalar_tensor_tensor, o, num, den[:, t:t + 1], o, ALU.mult, ALU.add)
            K.release(6, 2, m)

        before = None
        for d, h in todo:
            w, m = make(d, h)
            if before:
                read(*before)
            before = (d, h, w, m)
        read(*before)
        n = TT * HEADS
        ss, tmp2, rs = (K.sb(f"ml_small{i}", [P, n], st) for i in range(3))
        sqr = K.sb("ml_squares", [P, ML_V], st)
        last = K.dve.last()
        for t in range(TT):
            for h in range(HEADS):
                m = K.act(S.activation, sqr[:, :], hs[:, t, h * ML_V:(h + 1) * ML_V], ACT.Square,
                          accum_out=ss[:, t * HEADS + h:t * HEADS + h + 1], after=[last])
        m = K.dve(V.tensor_scalar, ss[:, :], ss[:, :], 1.0 / ML_V, EPS, ALU.mult, ALU.add, after=[m])
        K.rsqrt_small(rs[:, :], ss[:, :], tmp2[:, :], after=[m])
        rsb = bass.AP(tensor=rs[:, :].tensor, offset=rs[:, :].offset, ap=[[n, P], [1, n], [0, ML_V]])
        hv = hs[:, :, :].rearrange("p t c -> p (t c)").rearrange("p (n d) -> p n d", d=ML_V)
        m = K.dve(V.tensor_tensor, hv, hv, rsb, ALU.mult)
        for h in range(HEADS):
            i = 2 * (h % 3)
            K.claim(i, 2)
            for t in range(TT):
                done = K.pe(T.transpose, self.pair(i, t * P, (t + 1) * P),
                            hs[:, t, h * ML_V:(h + 1) * ML_V], K.ident, after=[m], mark=True)
            g = K.dve(V.scalar_tensor_tensor, y[:, HEADS + h, :], self.pair(i), self.small.head_gain[h],
                      y[:, HEADS + h, :], ALU.mult, ALU.mult, after=[done])
            K.release(i, 2, g)

    def latent_attention(self, l, st):
        K, V, S, T = self.K, self.K.nc.vector, self.K.nc.scalar, self.K.nc.tensor
        H = MLA_HEADS
        room = K.sb("mla_latents", [P, QT * H * MLA_V], st)
        cq = room[:, 0:4 * SEQ].rearrange("p (j n) -> p j n", j=4)
        ckv = room[:, 4 * SEQ:4 * SEQ + 2 * TOK].rearrange("p (j n) -> p j n", j=2)
        out = room[:, :].rearrange("p (t c) -> p t c", t=QT)
        kr = K.sb("k_rope", [P, TT, MLA_ROPE], st)
        sk, sq_ = K.sb("sum_k", [P, TT * H], st), K.sb("sum_q", [P, QT * H], st)
        rk, rq = K.sb("rstd_k", [P, TT * H], st), K.sb("rstd_q", [P, QT * H], st)
        small = K.sb("mla_small", [P, TT * H], st)
        with ExitStack() as s2:
            h = K.sb("h2", [P, KT, TOK], s2)
            with ExitStack() as s3:
                sq = K.sb("squares2", [P, KT, SEQ], s3)
                ready = self.modulate(l, 0, 1, h, sq)
                K.barrier()
            for j in range(4):
                w, ch = K.stream.piece("mla_w_in_2", (0,), rows_of(KT), np.arange(j * P, (j + 1) * P))
                i, done = self.wide(w, ch, h, LATENT, after=[ready])
                m = K.copy(cq[:, j, :], self.pair(i, CTX, TOK), after=[done])
                K.release(i, 2, m)
            mq = [K.act.last(), K.dve.last()]
            for j in range(2):
                w, ch = K.stream.piece("mla_w_in_2", (0,), rows_of(KT),
                                       MLA_Q_LORA + np.arange(j * P, (j + 1) * P))
                i, done = self.wide(w, ch, h, BOTH)
                m = K.copy(ckv[:, j, :], self.pair(i), after=[done])
                K.release(i, 2, m)
            w, ch = K.stream.piece("mla_w_in_2", (0,), rows_of(KT),
                                   MLA_Q_LORA + MLA_KV_LORA + np.arange(MLA_ROPE))
            i = K.next_banks()
            for t in range(TT):
                for kk in range(KT):
                    done = K.mm(K.bank(i)[:, t * MLA_ROPE:(t + 1) * MLA_ROPE],
                                h[:, kk, t * P:(t + 1) * P], w[:, kk, :], kk == 0, kk == KT - 1,
                                mark=(kk == KT - 1))
            K.stream.used(ch, done)
            m = K.act(S.copy, kr[:, :, :].rearrange("p t c -> p (t c)"),
                      K.bank(i)[:, 0:TT * MLA_ROPE], after=[done])
            K.release(i, 1, m)
            K.barrier()
        kt = K.sb("mla_k", [P, TT, H, MLA_QK], st)
        v = K.sb("mla_v", [P, TT, H, MLA_V], st)
        qt = K.sb("mla_q", [P, QT, H, MLA_QK], st)
        with ExitStack() as s1:
            sq = K.sb("squares4", [P, 4, TOK], s1)
            nq = K.rms_features(cq, 4, 0, SEQ, lambda j: self.small.q_norm[j], cq, sq, MLA_Q_LORA)
            nk = K.rms_features(ckv, 2, 0, TOK, lambda j: self.small.kv_norm2[j], ckv, sq, MLA_KV_LORA,
                                after=[nq])
            flat = qt[:, :, :, :].rearrange("p t h d -> p t (h d)")
            for c in range(3):
                w, ch = K.stream.piece("mla_w_uq_2", (0,), rows_of(4), np.arange(c * BANK, (c + 1) * BANK))
                for t in range(QT):
                    i = K.next_banks()
                    for j in range(4):
                        done = K.mm(K.bank(i), cq[:, j, t * P:(t + 1) * P], w[:, j, :], j == 0, j == 3,
                                    mark=(j == 3), after=[nq])
                    m = K.copy(flat[:, t, c * BANK:(c + 1) * BANK], K.bank(i), after=[done])
                    K.release(i, 1, m)
                K.stream.used(ch, done)
            mq = [K.act.last(), K.dve.last()]
            for c in range(4):
                w, ch = K.stream.piece("mla_w_ukv_2", (0,), rows_of(2), np.arange(c * BANK, (c + 1) * BANK))
                for t in range(TT):
                    i = K.next_banks()
                    for j in range(2):
                        done = K.mm(K.bank(i), ckv[:, j, t * P:(t + 1) * P], w[:, j, :], j == 0, j == 1,
                                    mark=(j == 1), after=[nk])
                    kv = K.bank(i).rearrange("p (h d) -> p h d", h=4)
                    m = K.act(S.copy, kt[:, t, 4 * c:4 * c + 4, 0:MLA_NOPE], kv[:, :, 0:MLA_NOPE],
                              after=[done])
                    m = K.dve(V.tensor_copy, v[:, t, 4 * c:4 * c + 4, :], kv[:, :, MLA_NOPE:], after=[m])
                    K.release(i, 1, m)
                K.stream.used(ch, done)
            mk = [K.act.last(), K.dve.last()]
            sqb = K.sb("mla_sq", [P, H * MLA_QK], s1)
            sr = K.sb("mla_sr", [P, TT], s1)
            for t in range(QT):
                m = K.act(S.activation, sqb[:, :], flat[:, t, :], ACT.Square, after=mq + [K.dve.last()])
                K.dve(V.tensor_reduce, sq_[:, t * H:(t + 1) * H],
                      sqb[:, :].rearrange("p (h d) -> p h d", h=H), AX_X, ALU.add, after=[m])
            for t in range(TT):
                n = H * MLA_NOPE
                sv = sqb[:, 0:n].rearrange("p (h d) -> p h d", h=H)
                m = K.act(S.activation, sv, kt[:, t, :, 0:MLA_NOPE], ACT.Square,
                          after=mk + [K.dve.last()])
                K.dve(V.tensor_reduce, sk[:, t * H:(t + 1) * H], sv, AX_X, ALU.add, after=[m])
                m = K.act(S.activation, sqb[:, 0:MLA_ROPE], kr[:, t, :], ACT.Square,
                          accum_out=sr[:, t:t + 1], after=[K.dve.last()])
                K.dve(V.tensor_scalar, sk[:, t * H:(t + 1) * H], sk[:, t * H:(t + 1) * H],
                      sr[:, t:t + 1], None, ALU.add, after=[m])
            for s, r, n in ((sq_, rq, QT * H), (sk, rk, TT * H)):
                m = K.dve(V.tensor_scalar, s[:, :], s[:, :], 1.0 / MLA_QK, EPS, ALU.mult, ALU.add)
                K.rsqrt_small(r[:, :], s[:, :], small[:, 0:n], after=[m])
            m = K.dve(V.tensor_scalar, rq[:, :], rq[:, :], MLA_QK ** -0.5, None, ALU.mult)
            half = MLA_ROPE // 2
            t1 = K.sb("rot1", [P, H, half], s1)
            t2 = K.sb("rot2", [P, H, half], s1)

            def rotate(x, heads, cos, sin):
                xp = x.rearrange("p h (i two) -> p h i two", two=2)
                even, odd = xp[:, :, :, 0], xp[:, :, :, 1]
                rep = lambda a: bass.AP(tensor=a.tensor, offset=a.offset,
                                        ap=[[a.ap[0][0], P], [0, heads], [1, half]])
                a, b = t1[:, 0:heads, :], t2[:, 0:heads, :]
                K.dve(V.tensor_tensor, a, even, rep(sin), ALU.mult)
                K.dve(V.tensor_tensor, b, odd, rep(sin), ALU.mult)
                K.dve(V.tensor_tensor, even, even, rep(cos), ALU.mult)
                K.dve(V.tensor_tensor, even, even, b, ALU.subtract)
                K.dve(V.tensor_tensor, odd, odd, rep(cos), ALU.mult)
                K.dve(V.tensor_tensor, odd, odd, a, ALU.add)

            def gain(x, heads, g):
                gb = bass.AP(tensor=g.tensor, offset=g.offset,
                             ap=[[g.ap[0][0], P], [0, heads], [1, MLA_ROPE]])
                K.dve(V.tensor_tensor, x, x, gb, ALU.mult)

            for t in range(QT):
                cos = self.c.mla_cos[:, t * half:(t + 1) * half]
                sin = self.c.mla_sin[:, t * half:(t + 1) * half]
                x = qt[:, t, :, MLA_NOPE:]
                gain(x, H, self.small.q_gain_row)
                rotate(x, H, cos, sin)
                x = kr[:, CT + t:CT + t + 1, :]
                gain(x, 1, self.small.k_gain_row)
                rotate(x, 1, cos, sin)
            gain(kr[:, 0:CT, :], CT, self.small.k_gain_row)
            for t in range(TT):
                r = rk[:, t * H:(t + 1) * H]
                rb = lambda n: bass.AP(tensor=r.tensor, offset=r.offset,
                                       ap=[[r.ap[0][0], P], [1, H], [0, n]])
                K.dve(V.tensor_tensor, kt[:, t, :, 0:MLA_NOPE], kt[:, t, :, 0:MLA_NOPE], rb(MLA_NOPE),
                      ALU.mult)
                kb = kr[:, t, :]
                kbb = bass.AP(tensor=kb.tensor, offset=kb.offset,
                              ap=[[kb.ap[0][0], P], [0, H], [1, MLA_ROPE]])
                K.dve(V.tensor_tensor, kt[:, t, :, MLA_NOPE:], kbb, rb(MLA_ROPE), ALU.mult)
            K.barrier()
        with ExitStack() as s1:
            self.heads_attention(s1, kt, v, qt, rq, out)
            K.barrier()
        with ExitStack() as s1:
            yt = K.sb("mla_out_t", [P, KT, SEQ], s1)
            for j in range(KT):
                i = K.next_banks()
                for t in range(QT):
                    done = K.pe(T.transpose, K.bank(i)[:, t * P:(t + 1) * P],
                                out[:, t, j * P:(j + 1) * P], K.ident, mark=True)
                m = K.copy(yt[:, j, :], K.bank(i), after=[done])
                K.release(i, 1, m)
            marks = [K.act.last(), K.dve.last()]
            ytw = yt[:, :, :]
            for d in range(KT):
                w, ch = K.stream.piece("mla_w_out_2", (0,), rows_of(KT), np.arange(d * P, (d + 1) * P))
                i = K.next_banks(2)
                K.pe.wait(*marks)
                for kk in range(KT):
                    done = K.mm(self.pair(i, CTX, TOK), w[:, kk, :], ytw[:, kk, :], kk == 0, kk == KT - 1,
                                mark=(kk == KT - 1))
                K.stream.used(ch, done)
                self.residual(i, done, l, 2, d, with_ctx=False)
            K.barrier()

    def heads_attention(self, st, kt, v, qt, rq, out):
        K, V, S, T = self.K, self.K.nc.vector, self.K.nc.scalar, self.K.nc.tensor
        H = MLA_HEADS
        kf = Ring([Buf(K.sb(f"k_feat{i}", [MLA_QK, TOK], st)) for i in range(4)])
        qf = Ring([Buf(K.sb(f"q_feat{i}", [MLA_QK, SEQ], st)) for i in range(4)])
        probs = Ring([Buf(K.sb(f"mla_probs{i}", [P, 2, TOK], st)) for i in range(2)])
        turned = Ring([Buf(K.sb(f"mla_turned{i}", [P, 3 * P], st)) for i in range(4)])
        colr = Ring([Buf(K.sb(f"mla_cols{i}", [P, 8], st)) for i in range(3)])
        tb = [0]

        def t_bank():
            i = 4 + tb[0] % 3
            tb[0] += 1
            K.claim(i)
            return i

        def to_features(src, ntile, dst, gain):
            for t0 in range(0, ntile, 3):
                n = min(3, ntile - t0)
                i = t_bank()
                for t in range(n):
                    done = K.pe(T.transpose, K.bank(i)[0:MLA_QK, t * P:(t + 1) * P], src(t0 + t),
                                K.ident, mark=True)
                m = K.act(S.activation, dst.t[:, t0 * P:(t0 + n) * P], K.bank(i)[0:MLA_QK, 0:n * P],
                          ACT.Copy, scale=gain, after=[done] + dst.free)
                K.release(i, 1, m)
            return m

        def prepare(hp):
            got = []
            for h in (2 * hp, 2 * hp + 1):
                a, b = kf.take(), qf.take()
                m1 = to_features(lambda t: kt[:, t, h, :], TT, a, self.small.k_gain_col)
                m2 = to_features(lambda t: qt[:, t, h, :], QT, b, self.small.q_gain_col)
                got.append((h, a, b, m2))
            return got

        def scores(heads, t):
            u = Names()
            u.heads, u.t, u.p, u.c = heads, t, probs.take(), colr.take()
            top, bias, total, u.inv = (u.c.t[:, 2 * j:2 * j + 2] for j in range(4))
            K.claim(0, 4)
            for n, (h, a, b, ready) in enumerate(heads):
                for lo, hi in ((0, BANK), (BANK, TOK)):
                    done = K.mm(K.psum[:, 2 * n * BANK + lo:2 * n * BANK + hi],
                                b.t[:, t * P:(t + 1) * P], a.t[:, lo:hi], True, True, mark=True,
                                after=[ready])
            for n, (h, a, b, ready) in enumerate(heads):
                a.free, b.free = [done], [done]
            l2 = K.bank(0, 4).rearrange("p (h c) -> p h c", h=2)[:, :, 0:TOK]
            K.dve(V.tensor_reduce, top, l2, AX_X, ALU.max, after=[done] + u.c.free)
            h0 = heads[0][0]
            s2 = rq[:, t * H + h0:t * H + h0 + 2]
            m = K.dve(V.scalar_tensor_tensor, bias, top, -1.0, s2, ALU.mult, ALU.mult)
            for n in range(2):
                e = K.act(S.activation, u.p.t[:, n, :], l2[:, n, :], ACT.Exp, bias=bias[:, n:n + 1],
                          scale=s2[:, n:n + 1], accum_out=total[:, n:n + 1], after=[m] + u.p.free)
            K.release(0, 4, e)
            K.dve(V.reciprocal, u.inv, total, after=[e])
            u.ready = e
            return u

        def turn(u, n):
            got = []
            for part in range(2):
                i, pt = t_bank(), turned.take()
                for b in range(3):
                    kb = 3 * part + b
                    done = K.pe(T.transpose, K.bank(i)[:, b * P:(b + 1) * P],
                                u.p.t[:, n, kb * P:(kb + 1) * P], K.ident, after=[u.ready], mark=True)
                m = K.copy(pt.t[:, :], K.bank(i)[:, 0:3 * P], after=[done] + pt.free)
                K.release(i, 1, m)
                got.append((pt, m))
            if n == 1:
                u.p.free = [done]
            return got

        def weigh(u, n, parts):
            if n == 0:
                K.claim(7)
            h = u.heads[n][0]
            for kb in range(TT):
                pt, m = parts[kb // 3]
                done = K.mm(K.bank(7)[:, n * MLA_V:(n + 1) * MLA_V], pt.t[:, (kb % 3) * P:(kb % 3 + 1) * P],
                            v[:, kb, h, :], kb == 0, kb == TT - 1, mark=(kb % 3 == 2), after=[m])
                if kb % 3 == 2:
                    pt.free = [done]
            if n == 1:
                for n2 in range(2):
                    h2 = u.heads[n2][0]
                    m = K.dve(V.tensor_scalar, out[:, u.t, h2 * MLA_V:(h2 + 1) * MLA_V],
                              K.bank(7)[:, n2 * MLA_V:(n2 + 1) * MLA_V], u.inv[:, n2:n2 + 1], None,
                              ALU.mult, after=[done])
                u.c.free = [m]
                K.release(7, 1, m)

        def second_half(u):
            a = turn(u, 0)
            b = turn(u, 1)
            weigh(u, 0, a)
            weigh(u, 1, b)

        before = None
        for hp in range(H // 2):
            heads = prepare(hp)
            for t in range(QT):
                u = scores(heads, t)
                if before:
                    second_half(before)
                before = u
        second_half(before)

    def feed_forward(self, l, with_ctx):
        K, V, S = self.K, self.K.nc.vector, self.K.nc.scalar
        spans = BOTH if with_ctx else LATENT
        lo0 = 0 if with_ctx else CTX
        with ExitStack() as st:
            act = K.sb("ffn_act", [P, FT, TOK if with_ctx else SEQ], st)
            with ExitStack() as s1:
                h = K.sb("h2", [P, KT, TOK], s1)
                with ExitStack() as s2:
                    sq = K.sb("squares2", [P, KT, SEQ], s2)
                    ready = self.modulate(l, 3, 4, h, sq, with_ctx)
                    K.barrier()
                gap = 2
                row = [Buf(K.sb(f"ffn_row{i}", [P, TOK + 2 * gap], s1)) for i in range(2)]
                for r in row:
                    mz = K.pool(K.nc.gpsimd.memset, r.t[:, :], 0.0)
                rows = Ring(row)
                n = TOK + gap - lo0 if with_ctx else SEQ
                base = 0 if with_ctx else CTX + gap
                for f in range(FT):
                    cw = self.small.ffn_w[l][f]
                    w, ch = K.stream.piece("ffn_w_in_2", (l,), rows_of(KT), np.arange(f * P, (f + 1) * P))
                    i, done = self.wide(w, ch, h, spans, after=[ready])
                    r = rows.take()
                    if with_ctx:
                        K.act(S.copy, r.t[:, 1:1 + CTX], self.pair(i, 0, CTX), after=[done, mz] + r.free)
                    m = K.act(S.copy, r.t[:, 1 + CTX + gap:1 + TOK + gap], self.pair(i, CTX, TOK),
                              after=[done, mz] + r.free)
                    t = K.bank(i, 2)[:, 0:n]
                    K.dve(V.tensor_scalar, t, r.t[:, base:base + n], cw[:, 0:1], self.small.ffn_b[l][f],
                          ALU.mult, ALU.add, after=[m])
                    for j in (1, 2):
                        m = K.dve(V.scalar_tensor_tensor, t, r.t[:, base + j:base + j + n],
                                  cw[:, j:j + 1], t, ALU.mult, ALU.add)
                    r.free = [m]
                    a = act[:, f, :]
                    if with_ctx:
                        K.act(S.activation, a[:, 0:CTX], t[:, 0:CTX], ACT.Gelu_apprx_tanh, after=[m])
                        g = K.act(S.activation, a[:, CTX:TOK], t[:, CTX + gap:TOK + gap],
                                  ACT.Gelu_apprx_tanh)
                    else:
                        g = K.act(S.activation, a, t, ACT.Gelu_apprx_tanh, after=[m])
                    K.release(i, 2, g)
                    w, ch = K.stream.piece("ffn_w_in_2", (l,), rows_of(KT),
                                           FFN + np.arange(f * P, (f + 1) * P))
                    i, done = self.wide(w, ch, h, spans)
                    m = K.dve(V.tensor_tensor, a, self.pair(i, lo0, TOK), a, ALU.mult, after=[done, g])
                    K.release(i, 2, m)
                K.barrier()
            half = FT // 2
            for d in range(KT):
                i = K.next_banks(2)
                for part in range(2):
                    w, ch = K.stream.piece("ffn_w_out_2", (l,), rows_of(half, part * half * P),
                                           np.arange(d * P, (d + 1) * P))
                    for lo, hi in spans:
                        for kk in range(half):
                            kg = part * half + kk
                            done = K.mm(self.pair(i, lo, hi), w[:, kk, :], act[:, kg, lo - lo0:hi - lo0],
                                        kg == 0, kg == FT - 1, mark=(kk == half - 1))
                    K.stream.used(ch, done)
                self.residual(i, done, l, 5, d, with_ctx)
            K.barrier()

    def run(self):
        K, S = self.K, self.K.nc.scalar
        st = ExitStack()
        self.xc = K.sb("context", [P, KT, CTX], st)
        K.act.eng.dma_start(self.xc[:, :, :], self.dram_ctx).then_inc(self.ctx_sem, 16)
        for line in (K.pe, K.dve, K.act):
            line.wait((self.ctx_sem, 32))
        self.silu_c = K.sb("silu_c", [P, KT, 2], st)
        for side in range(2):
            self.silu_ready = K.act(S.activation, self.silu_c[:, :, side], self.small.c_sides[side],
                                    ACT.Silu)
        self.mods = [K.sb(f"mods{l}", [P, 6 * KT, 2], st) for l in range(DEPTH)]
        for l in range(DEPTH):
            self.modulation(l)
            with ExitStack() as s1:
                if l == 0:
                    self.conformer(l, s1)
                else:
                    self.latent_attention(l, s1)
                K.barrier()
            self.feed_forward(l, l < DEPTH - 1)
        st.close()


class Names:
    pass


def pack_constants():
    common, first = Pack("common"), Pack("first")
    at = {}
    i, j = np.arange(P)[:, None], np.arange(P)[None, :]
    at["ident"] = common.const(np.eye(P))
    at["ones"] = common.const(np.ones((P, P)))
    causal = np.zeros((P, SEQ))
    causal[:, SEQ - P:] = np.where(j <= i, 0.0, NEG)
    at["causal"] = first.const(causal)
    at["before01"] = first.const((i < j) * 1.0)
    at["before_add"] = first.const(np.where(i < j, 0.0, NEG))
    at["from_here"] = first.const((i >= j) * 1.0)

    def partner(dim):
        half = dim // 2
        f = np.arange(P) % dim
        return np.arange(P) + np.where(f < half, half, -half)

    for dim in (64, 32):
        half = dim // 2
        perm = np.zeros((P, P))
        perm[partner(dim), np.arange(P)] = 1.0
        at[f"perm{dim}"] = first.const(perm)
        f = np.arange(P) % dim
        inv = (10000.0 ** (-2.0 * (f % half) / dim)).astype(np.float32)
        at[f"inv{dim}"] = first.const(inv[:, None])
        at[f"sign{dim}"] = first.const(np.where(f < half, -1.0, 1.0)[:, None])
    n = np.arange(N_CMP)[None, None, :]
    t = np.arange(QT)[None, :, None] * P + np.arange(P)[:, None, None]
    seen = n * CMP_STRIDE + CMP_LEN - 1 <= t
    at["cmp_add"] = first.const(np.where(seen, 0.0, NEG).reshape(P, -1))
    at["cmp_keep"] = first.const((seen * 1.0).reshape(P, -1))
    r = np.arange(P) % 32
    at["fox"] = first.const(np.stack([(r == 0) / SCALE, (r == 1) * 1.0, (r == 1) / -SCALE,
                                      (r == 0) * 1.0], 1))
    p = np.arange(P)[:, None]
    for l in range(DEPTH):
        feature = np.arange(KT)[None, :] * P + p
        at["norm_g", l] = first.param("norm_g", feature, l)
        at["mem_norm", l] = first.param("mem_norm", feature, l)
        at["kv_norm", l] = first.param("kv_norm", p, l)
        at["fox_bias", l] = first.param("fox_bias", p // 32, l)
        pe = (2 * np.arange(CMP_LEN // 2)[None, :] + p // HD) * HD + p % HD
        at["pe_k", l] = first.param("nsa_pe_k", pe, l)
        at["pe_v", l] = first.param("nsa_pe_v", pe, l)
    at["final_norm"] = first.param("final_norm", np.arange(KT)[None, :] * P + p, None)
    second = Pack("second")
    at["le"] = second.const(np.where(i <= j, 0.0, NEG))
    at["ge"] = second.const(np.where(i >= j, 0.0, NEG))
    tok = np.arange(SEQ)
    half = MLA_ROPE // 2
    inv = (10000.0 ** (-np.arange(0, half, 2) / half)).astype(np.float32)
    ang = np.concatenate([(tok // GRID_W).astype(np.float32)[:, None] * inv,
                          (tok % GRID_W).astype(np.float32)[:, None] * inv], 1)
    by_tile = lambda a: a.reshape(QT, P, half).transpose(1, 0, 2).reshape(P, -1)
    at["mla_cos"] = second.const(by_tile(np.cos(ang)))
    at["mla_sin"] = second.const(by_tile(np.sin(ang)))
    at["c"], at["c_ctx"] = (second.param(n, feature, None) for n in ("c_2", "c_ctx_2"))
    at["gate_bias"] = second.param("ab_gate_bias_2",
                                   HEADS * np.array([0, 2, 1, 3])[p // 32] + p % HEADS, 0)
    for c in range(4):
        at["conv_w", c] = second.param("ab_conv_w_2",
                                       np.arange(CONV_WIDTH)[None, :] * CONV_DIM + c * P + p, 0)
    four = np.arange(4)[None, :] * P + p
    for n in ("ab_conv_b_2", "ab_ln_g_2", "ab_ln_b_2", "ab_head_gain_2", "mla_q_norm_2"):
        at[n] = second.param(n, four, 0)
    at["mla_kv_norm_2"] = second.param("mla_kv_norm_2", four[:, 0:2], 0)
    for n in ("mla_q_gain_2", "mla_k_gain_2"):
        at[n] = second.param(n, np.where(p < MLA_NOPE, p, -1), 0)
        at[n, "row"] = second.param(n, MLA_NOPE + np.arange(MLA_ROPE)[None, :] + 0 * p, 0)
    for l in range(DEPTH):
        at["ada_b", l] = second.param("ada_b_2", np.arange(6 * KT)[None, :] * P + p, l)
        taps = (np.arange(FT)[None, :, None] * P + p[:, :, None]
                + np.arange(3)[None, None, :] * FFN).reshape(P, -1)
        at["ffn_w", l] = second.param("ffn_conv_w_2", taps, l)
        at["ffn_b", l] = second.param("ffn_conv_b_2", np.arange(FT)[None, :] * P + p, l)
    return common, first, second, at


def name_second(at, second):
    c, s = Names(), Names()
    col = lambda n, w=1, lo=0: second[:, at[n] + lo:at[n] + lo + w]
    c.ml_mask = [col("le", P), col("ge", P)]
    half = MLA_ROPE // 2
    c.mla_cos, c.mla_sin = col("mla_cos", QT * half), col("mla_sin", QT * half)
    s.c_sides = [col("c", KT), col("c_ctx", KT)]
    s.gate_bias = col("gate_bias")
    s.conv_w = [col(("conv_w", k), CONV_WIDTH) for k in range(4)]
    s.conv_b, s.ln_g, s.ln_b, s.head_gain, s.q_norm = (
        [col(n, 1, k) for k in range(4)]
        for n in ("ab_conv_b_2", "ab_ln_g_2", "ab_ln_b_2", "ab_head_gain_2", "mla_q_norm_2"))
    s.kv_norm2 = [col("mla_kv_norm_2", 1, k) for k in range(2)]
    s.q_gain_col, s.k_gain_col = (col(n)[0:MLA_QK, :] for n in ("mla_q_gain_2", "mla_k_gain_2"))
    s.q_gain_row, s.k_gain_row = (col((n, "row"), MLA_ROPE) for n in ("mla_q_gain_2", "mla_k_gain_2"))
    s.ada_b = [col(("ada_b", l), 6 * KT) for l in range(DEPTH)]
    s.ffn_w = [[col(("ffn_w", l), 3, 3 * f) for f in range(FT)] for l in range(DEPTH)]
    s.ffn_b = [[col(("ffn_b", l), 1, f) for f in range(FT)] for l in range(DEPTH)]
    return c, s


def name_constants(at, common, first):
    c, s = Names(), Names()
    c.causal = first[:, at["causal"]:at["causal"] + SEQ]
    sq = lambda t, n: t[:, at[n]:at[n] + P]
    c.before01, c.before_add, c.from_here = (sq(first, n) for n in ("before01", "before_add", "from_here"))
    c.perm64, c.perm32 = sq(first, "perm64"), sq(first, "perm32")
    col = lambda t, n, w=1: t[:, at[n]:at[n] + w]
    c.inv64, c.inv32, c.sign64, c.sign32 = (col(first, n) for n in ("inv64", "inv32", "sign64", "sign32"))
    c.cmp_add, c.cmp_keep = (col(first, n, QT * N_CMP) for n in ("cmp_add", "cmp_keep"))
    c.fox = col(first, "fox", 4)
    tiles = lambda n: [first[:, at[n] + k:at[n] + k + 1] for k in range(KT)]
    s.norm_g = [tiles(("norm_g", l)) for l in range(DEPTH)]
    s.mem_norm = [tiles(("mem_norm", l)) for l in range(DEPTH)]
    s.kv_norm = [col(first, ("kv_norm", l)) for l in range(DEPTH)]
    s.fox_bias = [col(first, ("fox_bias", l)) for l in range(DEPTH)]
    s.pe = {w: [col(first, ("pe_" + w, l), CMP_LEN // 2) for l in range(DEPTH)] for w in "kv"}
    s.final_norm = tiles("final_norm")
    return c, s


def build(nc):
    common, first, second, at = pack_constants()
    dram = lambda name, shape, dt=F32, kind="ExternalInput": nc.dram_tensor(name, shape, dt, kind=kind).ap()
    with ExitStack() as ctx:
        K = Core(nc, ctx)
        d_common, d_first = dram("common_dram", (P, common.n)), dram("first_dram", (P, first.n))
        d_x, d_mem = dram("x_dram", (P, KT, SEQ)), dram("mem_dram", (P, KT, N_MEM))
        d_pos = dram("positions_dram", (SEQ,), I32)
        d_out = dram("out_dram", (P, KT, SEQ), kind="ExternalOutput")
        K.stream = Stream(nc, K.pe, K.sb, [K.sem(f"weights_in_slot{i}") for i in range(NSLOT)])
        t_common = K.sb("common", [P, common.n])
        K.ident, K.ones = t_common[:, 0:P], t_common[:, P:2 * P]
        K.tiny = K.sb("tiny", [P, 64])
        K.diag = Ring([Buf(K.sb(f"diag{i}", [P, P])) for i in range(2)])
        K.t_turn = 0
        d_second, d_ctx = dram("second_dram", (P, second.n)), dram("context_dram", (P, KT, CTX))
        x = K.sb("x", [P, KT, SEQ])
        loaded, stored = K.sem("constants_in"), K.sem("output_stored")
        with ExitStack() as st:
            t_first = K.sb("first", [P, first.n], st)
            c, small = name_constants(at, t_common, t_first)
            for t, d in ((t_common, d_common), (t_first, d_first), (x, d_x)):
                nc.sync.dma_start(t[:], d).then_inc(loaded, 16)
            for line in (K.pe, K.dve, K.act):
                line.wait((loaded, 48))
            B = FirstBlock(K, c, small)
            B.x, B.dram_mem, B.dram_pos = x, d_mem, d_pos
            B.mem_sem, B.pos_sem, B.consts_loaded = K.sem("mem_in"), K.sem("positions_in"), (loaded, 48)
            B.run()
        with ExitStack() as st:
            t_second = K.sb("second", [P, second.n], st)
            ctx_sem = K.sem("context_in")
            nc.scalar.dma_start(t_second[:], d_second).then_inc(ctx_sem, 16)
            c, small = name_second(at, t_second)
            B = SecondBlock(K, c, small)
            B.x, B.dram_ctx, B.ctx_sem = x, d_ctx, ctx_sem
            B.run()
        d_stream = dram("stream_dram", (len(K.stream.chunks), P, SLOT))
        K.stream.issue(K.sp, d_stream)
        K.sp.wait(*K.all_marks())
        nc.sync.dma_start(d_out, x[:, :, :]).then_inc(stored, 16)
        nc.sync.wait_ge(stored, 16)
    return K.stream, [common, first, second]


def feature_major(a):
    return np.ascontiguousarray(a.reshape(a.shape[0], -1, P).transpose(2, 1, 0))


def kernel(**inputs):
    import concourse.bacc as bacc
    from concourse.bass_utils import run_bass_kernel_spmd

    inputs = {k: np.asarray(v) for k, v in inputs.items()}
    nc = bacc.Bacc("TRN2", target_bir_lowering=False, num_devices=1,
                   dynamic_dma_scratch_size=1024)
    stream, packs = build(nc)
    arrays = {"common_dram": packs[0].fill(inputs), "first_dram": packs[1].fill(inputs),
              "second_dram": packs[2].fill(inputs), "context_dram": feature_major(inputs["ctx_2"][0]),
              "x_dram": feature_major(inputs["x"][0]), "mem_dram": feature_major(inputs["mem"][0]),
              "positions_dram": inputs["positions"][0], "stream_dram": stream.fill(inputs)}
    got = run_bass_kernel_spmd(nc, [arrays], core_ids=[0]).results[0]["out_dram"]
    return np.ascontiguousarray(got.transpose(2, 1, 0)).reshape(1, SEQ, D_MODEL)
```

```python
from contextlib import ExitStack

import numpy as np

import concourse.bass as bass
from concourse import mybir

F32 = mybir.dt.float32
I32 = mybir.dt.int32
ALU = mybir.AluOpType
ACT = mybir.ActivationFunctionType
AX_X = mybir.AxisListType.X
P = 128
BANK = 512
NEG = -1.0e30
LOWEST = -3.0e38
EPS = 1e-6

D_MODEL, SEQ, DEPTH, N_MEM, CTX = 1024, 512, 2, 256, 256
HEADS, HD = 4, 64
BR = HEADS * HD
N_BRANCH = 5
IDX_HEADS, IDX_DIM = 4, 32
KV_LATENT = 128
CMP_LEN, CMP_STRIDE, CMP_HIDDEN = 32, 16, 128
N_CMP = (SEQ - CMP_LEN) // CMP_STRIDE + 1
TOPK = min(256, SEQ // 4)
CONV_DIM, CONV_WIDTH = 512, 31
ML_QK, ML_V = 64, 128
MLA_HEADS, MLA_Q_LORA, MLA_KV_LORA, MLA_NOPE, MLA_ROPE, MLA_V = 16, 512, 256, 64, 32, 64
MLA_QK = MLA_NOPE + MLA_ROPE
GRID_W = 64
FFN = 2816
KT = D_MODEL // P
QT = SEQ // P
TOK = CTX + SEQ
SCALE = HD ** -0.5

IN_LAYOUT = (
    ('dsa_q', BR), ('dsa_ckv', KV_LATENT), ('idx_q', IDX_HEADS * IDX_DIM), ('idx_k', IDX_DIM),
    ('idx_w', IDX_HEADS), ('dsa_z', BR),
    ('fox_q', BR), ('fox_k', BR), ('fox_v', BR), ('fox_f', HEADS), ('fox_z', BR),
    ('sb_q', BR), ('sb_k', BR), ('sb_v', BR), ('sb_z', BR),
    ('nsa_q', BR), ('nsa_kc', HD), ('nsa_vc', HD), ('nsa_ks', HD), ('nsa_vs', HD),
    ('nsa_kw', HD), ('nsa_vw', HD), ('nsa_g', 3 * HEADS), ('nsa_z', BR),
    ('mem_q', BR), ('mem_z', BR), ('merge', N_BRANCH * D_MODEL),
)
COL = {}
_off = 0
for _name, _n in IN_LAYOUT:
    COL[_name] = np.arange(_off, _off + _n)
    _off += _n


class Line:

    def __init__(self, eng, sem, chain):
        self.eng, self.sem, self.n, self.chain, self.seen = eng, sem, 0, chain, {}

    def wait(self, *marks):
        for m in marks:
            if m is not None and self.seen.get(m[0].name, 0) < m[1]:
                self.eng.wait_ge(m[0], m[1])
                self.seen[m[0].name] = m[1]

    def last(self):
        return (self.sem, self.n) if self.n else None

    def __call__(self, op, *args, after=(), mark=True, **kw):
        self.wait(*after)
        if self.chain:
            self.wait(self.last())
        ins = op(*args, **kw)
        if mark:
            self.n += 1
            ins.then_inc(self.sem, 1)
            return (self.sem, self.n)
        return None


class Buf:

    def __init__(self, t):
        self.t, self.free = t, []


class Ring:
    def __init__(self, bufs):
        self.bufs, self.i = bufs, 0

    def take(self):
        b = self.bufs[self.i % len(self.bufs)]
        self.i += 1
        return b


class Pack:

    def __init__(self, name):
        self.name, self.n, self.parts, self.t = name, 0, [], None

    def add(self, n, what):
        at = self.n
        self.n += n
        self.parts.append((at, n, what))
        return at

    def const(self, a):
        full = np.zeros((P, a.shape[1]), np.float32)
        full[:a.shape[0]] = a
        return self.add(a.shape[1], full)

    def param(self, name, idx, lead=0):
        idx = np.asarray(idx)
        full = np.zeros((P, idx.shape[1]), np.int64)
        full[:idx.shape[0]] = idx
        return self.add(idx.shape[1], (name, lead, full))

    def fill(self, inputs):
        out = np.zeros((P, self.n), np.float32)
        for at, n, what in self.parts:
            if isinstance(what, tuple):
                name, lead, idx = what
                a = inputs[name]
                a = a[lead] if lead is not None else a
                out[:, at:at + n] = np.where(idx < 0, np.float32(1), a.reshape(-1)[idx])
            else:
                out[:, at:at + n] = what
        return out


SLOT = 2048
NSLOT = 4


class Stream:

    def __init__(self, nc, pe, sb, sems):
        self.nc, self.pe, self.sems = nc, pe, sems
        self.slots = [sb(f"weight_slot{i}", [P, SLOT]) for i in range(NSLOT)]
        self.chunks = []
        self.pieces = []

    def piece(self, name, lead, rows, cols):
        rows, cols = np.asarray(rows), np.asarray(cols)
        nk, n = rows.shape[0], len(cols)
        size = nk * n
        assert size <= SLOT
        if not self.chunks or self.chunks[-1][0] + size > SLOT:
            self.chunks.append([0, None])
        c = len(self.chunks) - 1
        at = self.chunks[c][0]
        self.chunks[c][0] += size
        self.pieces.append((c, at, name, lead, rows, cols))
        t = self.slots[c % NSLOT][:, at:at + size].rearrange("p (k n) -> p k n", k=nk)
        loaded = (self.sems[c % NSLOT], 16 * (c // NSLOT + 1))
        self.pe.wait(loaded)
        return t, c

    def used(self, c, mark):
        self.chunks[c][1] = mark

    def issue(self, sp, dram):
        for c, (size, mark) in enumerate(self.chunks):
            if c >= NSLOT:
                sp.wait(self.chunks[c - NSLOT][1])
            sp.eng.dma_start(self.slots[c % NSLOT][:, 0:size], dram[c, :, 0:size]).then_inc(
                self.sems[c % NSLOT], 16)

    def fill(self, inputs):
        out = np.zeros((len(self.chunks), P, SLOT), np.float32)
        for c, at, name, lead, rows, cols in self.pieces:
            a = inputs[name]
            for i in lead:
                a = a[i]
            got = a[rows][:, :, cols] if a.ndim == 2 else None
            out[c, :, at:at + rows.shape[0] * len(cols)] = got.transpose(1, 0, 2).reshape(P, -1)
        return out


def rows_of(n, first=0):
    return first + np.arange(n * P).reshape(n, P)


class Core:

    def __init__(self, nc, ctx):
        self.nc, self.ctx = nc, ctx
        sem = lambda name: ctx.enter_context(nc.semaphore(name))
        self.sem = sem
        self.pe = Line(nc.tensor, sem("tensor_steps"), False)
        self.dve = Line(nc.vector, sem("vector_steps"), True)
        self.act = Line(nc.scalar, sem("scalar_steps"), True)
        self.pool = Line(nc.gpsimd, sem("gpsimd_steps"), True)
        self.sp = Line(nc.sync, sem("sync_steps"), False)
        self.psum = ctx.enter_context(nc.psum_tensor("psum", [P, 8 * BANK], F32))
        self.banks = [Buf(self.psum[:, i * BANK:(i + 1) * BANK]) for i in range(8)]
        self.area = [0, 8, 0]
        self.spare = [6, 2, 0]
        self.later = []
        self.flip = 0
        self.used = {}
        self.fence = ()

    def sb(self, name, shape, stack=None, dt=F32):
        self.used[name] = self.used.get(name, 0) + 1
        if self.used[name] > 1:
            name = f"{name}_{self.used[name]}"
        return (stack or self.ctx).enter_context(self.nc.sbuf_tensor(name, shape, dt))

    def all_marks(self):
        return [m for m in (x.last() for x in (self.pe, self.dve, self.act, self.pool)) if m]

    def barrier(self, pe=True):
        marks = self.all_marks()
        for line in (self.pe, self.dve, self.act, self.pool)[0 if pe else 1:]:
            line.wait(*marks)
        self.fence = tuple(marks)

    def next_banks(self, n=1):
        first, count, at = self.area
        if at + n > count:
            at = 0
        self.area[2] = at + n
        return self.claim(first + at, n)

    def fill(self, n=1):
        for _ in range(min(n, len(self.later))):
            self.area, self.spare = self.spare, self.area
            self.later.pop(0)()
            self.area, self.spare = self.spare, self.area

    def claim(self, i, n=1):
        for b in self.banks[i:i + n]:
            self.pe.wait(*b.free)
        return i

    def bank(self, i, n=1):
        return self.psum[:, i * BANK:(i + n) * BANK]

    def release(self, i, n, *marks):
        for b in self.banks[i:i + n]:
            b.free = list(marks)

    def mm(self, out, lhsT, rhs, start, stop, mark=False, after=()):
        return self.pe(self.nc.tensor.matmul, out, lhsT, rhs, start=start, stop=stop, mark=mark,
                       after=after)

    def copy(self, out, in_, after=(), engine=None):
        if engine is None:
            self.flip += 1
            engine = self.act if self.flip % 2 else self.dve
        if engine is self.act:
            return self.act(self.nc.scalar.copy, out, in_, after=after)
        return self.dve(self.nc.vector.tensor_copy, out, in_, after=after)

    def project(self, w, chunk, m, x, spans, after=()):
        i = self.next_banks(len(spans))
        self.pe.wait(*after)
        nk = w.shape[1]
        for s, (lo, hi) in enumerate(spans):
            for k in range(nk):
                done = self.mm(self.bank(i + s)[0:m, 0:hi - lo], w[:, k, :], x[:, k, lo:hi],
                               k == 0, k == nk - 1, mark=(k == nk - 1))
        if chunk is not None:
            self.stream.used(chunk, done)
        return i, done

    def rsqrt_small(self, out, t, tmp, after=()):
        V, S = self.nc.vector, self.nc.scalar
        m = self.act(S.activation, tmp, t, ACT.Ln, after=after)
        m = self.act(S.activation, out, tmp, ACT.Exp, scale=-0.5)
        self.dve(V.tensor_tensor, tmp, out, out, ALU.mult, after=[m])
        self.dve(V.scalar_tensor_tensor, tmp, tmp, -0.5, t, ALU.mult, ALU.mult)
        return self.dve(V.scalar_tensor_tensor, out, tmp, 1.5, out, ALU.add, ALU.mult)

    def rms_features(self, x, nk, lo, hi, gain, out, sq, dim, shift=None, after=(), func=ACT.Identity):
        n = Norm(self, x, nk, lo, hi, gain, out, sq, dim, shift, func)
        n.squares(after)
        n.sums()
        self.fill()
        n.inverse()
        return n.apply()


class Norm:

    def __init__(self, K, x, nk, lo, hi, gain, out, sq, dim, shift=None, func=ACT.Identity):
        self.K, self.x, self.nk, self.lo, self.hi, self.gain = K, x, nk, lo, hi, gain
        self.out, self.sq, self.dim, self.shift, self.func = out, sq, dim, shift, func
        self.n = hi - lo

    def squares(self, after=()):
        K, V, S = self.K, self.K.nc.vector, self.K.nc.scalar
        made = [K.act.last(), K.dve.last()] + list(after)
        self.squared = []
        for k in range(self.nk):
            s, x = self.sq[:, k, 0:self.n], self.x[:, k, self.lo:self.hi]
            if k % 2:
                m = K.dve(V.tensor_tensor, s, x, x, ALU.mult, after=made)
            else:
                m = K.act(S.activation, s, x, ACT.Square, after=made)
            self.squared.append(m)

    def sums(self):
        K = self.K
        nb = (self.n + BANK - 1) // BANK
        self.i, self.nb = K.next_banks(nb), nb
        for lo in range(0, self.n, BANK):
            hi = min(lo + BANK, self.n)
            for k in range(self.nk):
                self.summed = K.mm(K.bank(self.i, nb)[:, lo:hi], K.ones, self.sq[:, k, lo:hi], k == 0,
                                   k == self.nk - 1, mark=(k == self.nk - 1),
                                   after=[self.squared[k]])

    def inverse(self):
        K, V, S = self.K, self.K.nc.vector, self.K.nc.scalar
        t, self.row = self.sq[:, 0, 0:self.n], self.sq[:, 1, 0:self.n]
        r = self.row
        m = K.dve(V.tensor_scalar, t, K.bank(self.i, self.nb)[:, 0:self.n], 1.0 / self.dim, EPS,
                  ALU.mult, ALU.add, after=[self.summed])
        K.release(self.i, self.nb, m)
        m = K.act(S.activation, r, t, ACT.Ln, after=[m])
        m = K.act(S.activation, r, r, ACT.Exp, scale=-0.5)
        K.dve(V.tensor_tensor, t, t, r, ALU.mult, after=[m])
        K.dve(V.scalar_tensor_tensor, t, t, -0.5, r, ALU.mult, ALU.mult)
        K.dve(V.scalar_tensor_tensor, r, t, 1.5, r, ALU.add, ALU.mult)

    def apply(self):
        K, V, S = self.K, self.K.nc.vector, self.K.nc.scalar
        marks = []
        for k in range(self.nk):
            o = self.out[:, k, self.lo:self.hi]
            m = K.dve(V.scalar_tensor_tensor, o, self.x[:, k, self.lo:self.hi], self.gain(k), self.row,
                      ALU.mult, ALU.mult)
            if self.shift is not None:
                m = K.act(S.activation, o, o, self.func, bias=self.shift(k), after=[m])
            marks.append(m)
        return marks




def softmax_attention(K, units, scratch, o_bank=5):
    V, S, T = K.nc.vector, K.nc.scalar, K.nc.tensor

    def scores(u):
        u.p = scratch.probs.take()
        u.c = scratch.cols.take()
        top, bias, total = (u.c.t[:, 4 * j:4 * j + 4] for j in range(3))
        for h in range(u.heads):
            i = h % 3
            K.claim(i)
            done = u.logits(h, K.bank(i)[:, 0:u.keys])
            m = K.dve(V.tensor_tensor_reduce, u.p.t[:, h, 0:u.keys], K.bank(i)[:, 0:u.keys], u.mask,
                      1.0, LOWEST, ALU.add, ALU.max, top[:, h:h + 1], after=[done] + u.p.free + u.c.free)
            K.release(i, 1, m)
        m = K.dve(V.tensor_scalar, bias[:, 0:u.heads], top[:, 0:u.heads], -SCALE, None, ALU.mult)
        for h in range(u.heads):
            e = K.act(S.activation, u.p.t[:, h, 0:u.keys], u.p.t[:, h, 0:u.keys], ACT.Exp,
                      bias=bias[:, h:h + 1], scale=SCALE, after=[m],
                      accum_out=None if u.keep is not None else total[:, h:h + 1])
        if u.keep is not None:
            for h in range(u.heads):
                e = K.dve(V.tensor_tensor_reduce, u.p.t[:, h, 0:u.keys], u.p.t[:, h, 0:u.keys], u.keep,
                          1.0, 0.0, ALU.mult, ALU.add, total[:, h:h + 1], after=[e])
            K.dve(V.tensor_scalar, total[:, 0:u.heads], total[:, 0:u.heads], 1e-30, None, ALU.max)
        u.inv = u.c.t[:, 12:12 + u.heads]
        K.dve(V.reciprocal, u.inv, total[:, 0:u.heads], after=[e])
        u.ready = e

    def turned(u, h):
        nb = (u.keys + P - 1) // P
        w = min(P, u.keys)
        i = 3 + K.t_turn % 2
        K.t_turn += 1
        K.claim(i)
        pt = scratch.turned.take()
        for b in range(nb):
            done = K.pe(T.transpose, K.bank(i)[0:w, b * P:(b + 1) * P], u.p.t[:, h, b * P:b * P + w],
                        K.ident, after=[u.ready], mark=(b == nb - 1))
        if h == u.heads - 1:
            u.p.free = [done]
        m = K.copy(pt.t[0:w, 0:nb * P], K.bank(i)[0:w, 0:nb * P], after=[done] + pt.free)
        K.release(i, 1, m)
        return pt, m, nb, w

    def weigh(u, h, pt, copied, nb, w):
        if h == 0:
            K.claim(o_bank)
        for b in range(nb):
            done = K.mm(K.bank(o_bank)[:, h * HD:(h + 1) * HD], pt.t[0:w, b * P:(b + 1) * P],
                        u.value(h, b), b == 0, b == nb - 1, mark=(b == nb - 1), after=[copied])
        pt.free = [done]
        if h == u.heads - 1:
            m = u.finish(u, K.bank(o_bank)[:, 0:u.heads * HD], done)
            u.c.free = [m]
            K.release(o_bank, 1, m)

    for i in range(len(units) + 1):
        if i < len(units):
            scores(units[i])
        K.fill()
        if i >= 1:
            u = units[i - 1]
            waiting = None
            for h in range(u.heads):
                got = turned(u, h)
                if waiting:
                    weigh(u, *waiting)
                waiting = (h,) + got
            weigh(u, *waiting)


class Unit:

    def __init__(self, keys, logits, mask, keep, value, finish, qt):
        self.heads, self.keys, self.logits, self.mask, self.keep = HEADS, keys, logits, mask, keep
        self.value, self.finish, self.qt = value, finish, qt


class FirstBlock:
    def __init__(self, K, consts, small):
        self.K, self.c, self.small = K, consts, small

    def features(self, cols, l, x=None, name="w_in", k=KT, spans=((0, SEQ),), first=0, after=()):
        w, c = self.K.stream.piece(name, l, rows_of(k, first), cols)
        return self.K.project(w, c, len(cols), self.h if x is None else x, spans, after=after)

    def rope(self, i, done, out, tables, perm):
        K, V = self.K, self.K.nc.vector
        raw, tmp = self.raw.take(), self.rtmp.take()
        cos, sin = tables
        copied = K.copy(raw.t[:, :], K.bank(i), after=[done] + raw.free, engine=K.act)
        j = K.next_banks()
        swapped = K.mm(K.bank(j), perm, raw.t[:, :], True, True, mark=True, after=[copied])
        raw.free = [swapped]
        m = K.dve(V.tensor_tensor, out, K.bank(i), cos, ALU.mult, after=[copied])
        K.release(i, 1, m)
        m = K.dve(V.tensor_tensor, tmp.t[:, :], K.bank(j), sin, ALU.mult, after=[swapped])
        K.release(j, 1, m)
        return K.dve(V.tensor_tensor, out, out, tmp.t[:, :], ALU.add)

    def plain(self, i, done, out, scale=None):
        K, S = self.K, self.K.nc.scalar
        if scale is not None:
            m = K.act(S.activation, out, K.bank(i), ACT.Copy, scale=scale, after=[done])
        else:
            m = K.copy(out, K.bank(i), after=[done])
        K.release(i, 1, m)
        return m

    def values(self, cols, l, out, ntile=QT, x=None, name="w_in", k=KT, after=()):
        K = self.K
        x = self.h if x is None else x
        n = len(cols)
        w, c = K.stream.piece(name, l, rows_of(k), cols)
        per = BANK // n
        nb = (ntile + per - 1) // per
        i = K.next_banks(nb)
        K.pe.wait(*after)
        for t in range(ntile):
            at = t * n
            for kk in range(k):
                done = K.mm(K.bank(i, nb)[:, at:at + n], x[:, kk, t * P:(t + 1) * P], w[:, kk, :],
                            kk == 0, kk == k - 1, mark=(t == ntile - 1 and kk == k - 1))
        K.stream.used(c, done)
        m = K.copy(out, K.bank(i, nb)[:, 0:ntile * n], after=[done])
        K.release(i, nb, m)
        return m

    def gates(self, l):
        K, V, S = self.K, self.K.nc.vector, self.K.nc.scalar
        zs = ["dsa_z", "fox_z", "sb_z", "nsa_z", "mem_z"]
        groups = [np.concatenate([COL[zs[0]], COL[zs[1]]]), np.concatenate([COL[zs[2]], COL[zs[3]]]),
                  np.concatenate([COL[zs[4]], COL["nsa_g"], COL["idx_w"]])]
        half = KT // 2
        for g, cols in enumerate(groups):
            n = len(cols)
            first = K.next_banks(QT)
            for part in range(2):
                w, c = K.stream.piece("w_in", (l,), rows_of(half, part * half * P), cols)
                for t in range(QT):
                    for k in range(half):
                        kk = part * half + k
                        done = K.mm(K.bank(first + t)[:, 0:n], self.h[:, kk, t * P:(t + 1) * P],
                                    w[:, k, :], kk == 0, kk == KT - 1, mark=(k == half - 1),
                                    after=[self.h_ready[kk]])
                    if part:
                        nb = 2 if g < 2 else 1
                        z = self.gate[:, 2 * g:2 * g + nb, t * BR:(t + 1) * BR]
                        zp = K.bank(first + t)[:, 0:nb * BR].rearrange("p (b c) -> p b c", b=nb)
                        m = K.act(S.activation, z, zp, ACT.Tanh, scale=0.5, after=[done])
                        m = K.dve(V.scalar_tensor_tensor, z, z, 1.0, zp, ALU.add, ALU.mult, after=[m])
                        if g == 2:
                            m = K.act(S.copy, self.idx_w[:, t, :],
                                      K.bank(first + t)[:, BR + 3 * HEADS:BR + 3 * HEADS + IDX_HEADS],
                                      after=[m])
                            m = K.act(S.activation, self.mix[:, t, :],
                                      K.bank(first + t)[:, BR:BR + 3 * HEADS], ACT.Tanh, scale=0.5)
                            m = K.dve(V.tensor_scalar, self.mix[:, t, :], self.mix[:, t, :], 1.0, 0.5,
                                      ALU.add, ALU.mult, after=[m])
                        K.release(first + t, 1, m)
                K.stream.used(c, done)
        self.gates_ready = m

    def turn_branch(self, b):
        K, T = self.K, self.K.nc.tensor
        i = K.next_banks(2)
        ready = K.dve.last()
        for j in range(2):
            for t in range(QT):
                done = K.pe(T.transpose, K.bank(i, 2)[:, j * SEQ + t * P:j * SEQ + (t + 1) * P],
                            self.gate[:, b, t * BR + j * P:t * BR + (j + 1) * P], K.ident,
                            after=[ready], mark=True)
        m = K.copy(self.gate[:, b, :], K.bank(i, 2), after=[done])
        K.release(i, 2, m)
        return m

    def finish_plain(self, b):
        def finish(u, o, done):
            K, V = self.K, self.K.nc.vector
            for h in range(HEADS):
                y = self.gate[:, b, u.qt * BR + h * HD:u.qt * BR + (h + 1) * HD]
                m = K.dve(V.scalar_tensor_tensor, y, o[:, h * HD:(h + 1) * HD], u.inv[:, h:h + 1], y,
                          ALU.mult, ALU.mult, after=[done, self.gates_ready])
            return m
        return finish

    def pair_logits(self, q, k, ready, extra=None, keys=None):
        K = self.K

        def logits_of(qt):
            def logits(h, out):
                lo, j = HD * (h % 2), h // 2
                n = out.shape[1]
                kt = k[lo:lo + HD, j, 0:n] if len(k.shape) == 3 else k[lo:lo + HD, 0:n]
                done = K.mm(out, q[lo:lo + HD, j, qt * P:(qt + 1) * P], kt, True, extra is None,
                            mark=extra is None, after=ready)
                if extra is not None:
                    a, b = extra
                    done = K.mm(out, a[32 * h:32 * h + 32, qt * P:(qt + 1) * P],
                                b[32 * h:32 * h + 32, 0:n], False, True, mark=True)
                return done
            return logits
        return logits_of

    def causal(self, qt):
        return self.c.causal[:, (QT - 1 - qt) * P:QT * P]

    def dsa(self, l, a):
        K, V, S = self.K, self.K.nc.vector, self.K.nc.scalar
        D = a.sub
        q, k, v = D("q", [P, 2, SEQ]), D("k", [P, 2, SEQ]), D("v", [P, QT, BR])
        c_kv, c_n = D("c_kv", [P, 1, SEQ]), D("c_n", [P, 1, SEQ])
        qi, ki = D("q_idx", [P, SEQ]), D("k_idx", [P, SEQ])
        rel, score = D("rel", [P, SEQ]), D("score", [P, SEQ])
        drop = [None] + [D(f"drop{t}", [P, (t + 1) * P]) for t in range(1, QT)]
        i, done = self.features(COL["dsa_ckv"], (l,), after=a.after)
        m = self.plain(i, done, c_kv[:, 0, :])
        K.dve.wait(m)
        n = K.rms_features(c_kv, 1, 0, SEQ, lambda kk: self.small.kv_norm[l], c_n, self.sq1, KV_LATENT,
                           after=[m])
        for j in range(2):
            i, done = self.features(COL["dsa_q"][j * P:(j + 1) * P], (l,))
            self.rope(i, done, q[:, j, :], self.rope64, self.c.perm64)
        i, done = self.features(COL["idx_q"], (l,))
        self.rope(i, done, qi[:, :], self.rope32, self.c.perm32)
        i, done = self.features(np.tile(COL["idx_k"], IDX_HEADS), (l,))
        ready_idx = self.rope(i, done, ki[:, :], self.rope32, self.c.perm32)
        for j in range(2):
            i, done = self.features(np.arange(j * P, (j + 1) * P), (l,), x=c_n, name="w_uk", k=1,
                                    after=n)
            ready = self.rope(i, done, k[:, j, :], self.rope64, self.c.perm64)
        w, c = K.stream.piece("w_uv", (l,), rows_of(1), np.arange(BR))
        i = K.next_banks(2)
        for t in range(QT):
            done = K.mm(K.bank(i, 2)[:, t * BR:(t + 1) * BR], c_n[:, 0, t * P:(t + 1) * P], w[:, 0, :],
                        True, True, mark=True)
        K.stream.used(c, done)
        mv = K.copy(v[:, :, :].rearrange("p t c -> p (t c)"), K.bank(i, 2), after=[done])
        K.release(i, 2, mv)
        scale = IDX_DIM ** -0.5 * IDX_HEADS ** -0.5
        for t in range(1, QT):
            n = (t + 1) * P
            for h in range(IDX_HEADS):
                i = K.next_banks()
                done = K.mm(K.bank(i)[:, 0:n], qi[32 * h:32 * h + 32, t * P:(t + 1) * P],
                            ki[32 * h:32 * h + 32, 0:n], True, True, mark=True, after=[ready_idx])
                m = K.act(S.activation, rel[:, 0:n], K.bank(i)[:, 0:n], ACT.Relu,
                          after=[done, K.dve.last()])
                K.release(i, 1, m)
                wi = self.idx_w[:, t, h:h + 1]
                if h == 0:
                    K.dve(V.tensor_scalar, score[:, 0:n], rel[:, 0:n], wi, None, ALU.mult,
                          after=[m, self.gates_ready])
                else:
                    K.dve(V.scalar_tensor_tensor, score[:, 0:n], rel[:, 0:n], wi, score[:, 0:n],
                          ALU.mult, ALU.add, after=[m])
            K.dve(V.scalar_tensor_tensor, score[:, 0:n], score[:, 0:n], scale, self.causal(t),
                  ALU.mult, ALU.add)
            for r in range(TOPK // 8):
                if r % 5 == 4:
                    K.fill()
                K.dve(V.max, self.top8[:, :], score[:, 0:n])
                K.dve(V.match_replace, score[:, 0:n], self.top8[:, :], score[:, 0:n], LOWEST)
            K.dve(V.tensor_scalar, drop[t][:, :], score[:, 0:n], LOWEST, NEG, ALU.is_gt, ALU.mult)
        logits = self.pair_logits(q, k, [ready])
        units = [Unit((t + 1) * P, logits(t), self.causal(0) if t == 0 else drop[t][:, :], None,
                      lambda h, b: v[:, b, h * HD:(h + 1) * HD], self.finish_plain(0), t)
                 for t in range(QT)]
        K.pe.wait(mv)
        softmax_attention(K, units, self.scratch)

    def log_sigmoid(self, x, e, out, width=None, after=()):
        K, V, S = self.K, self.K.nc.vector, self.K.nc.scalar
        m = K.dve(V.scalar_tensor_tensor, e, x, -1.0, x, ALU.mult, ALU.min, after=after)
        m = K.act(S.activation, e, e, ACT.Exp, after=[m])
        m = K.act(S.activation, e, e, ACT.Ln, bias=1.0)
        return K.dve(V.scalar_tensor_tensor, out, x, 0.0, e, ALU.min, ALU.subtract, after=[m])

    def fox(self, l, a):
        K, V = self.K, self.K.nc.vector
        D = a.sub
        q, k, v = D("q", [P, 2, SEQ]), D("k", [P, 2, SEQ]), D("v", [P, QT, BR])
        f, g = D("f", [P, SEQ]), D("g", [P, SEQ])
        fa, fb = D("decay_q", [P, SEQ]), D("decay_k", [P, SEQ])
        i, done = self.features(np.repeat(COL["fox_f"], 32), (l,), after=a.after)
        m = K.dve(V.tensor_scalar, f[:, :], K.bank(i), self.small.fox_bias[l], None, ALU.add,
                  after=[done])
        K.release(i, 1, m)
        self.log_sigmoid(f[:, :], g[:, :], f[:, :])
        K.dve(V.tensor_tensor_scan, g[:, :], self.ones_row[:, :], f[:, :], 0.0, ALU.mult, ALU.add)
        K.dve(V.tensor_scalar, fa[:, :], g[:, :], self.c.fox[:, 0:1], self.c.fox[:, 1:2], ALU.mult,
              ALU.add)
        mf = K.dve(V.tensor_scalar, fb[:, :], g[:, :], self.c.fox[:, 2:3], self.c.fox[:, 3:4],
                   ALU.mult, ALU.add)
        marks = [mf]
        for j in range(2):
            for name, dst in (("fox_q", q), ("fox_k", k)):
                i, done = self.features(COL[name][j * P:(j + 1) * P], (l,))
                marks.append(self.plain(i, done, dst[:, j, :]))
        marks.append(self.values(COL["fox_v"], (l,), v[:, :, :].rearrange("p t c -> p (t c)")))
        logits = self.pair_logits(q, k, marks, extra=(fa, fb))
        units = [Unit((t + 1) * P, logits(t), self.causal(t), None,
                      lambda h, b: v[:, b, h * HD:(h + 1) * HD], self.finish_plain(1), t)
                 for t in range(QT)]
        softmax_attention(K, units, self.scratch)

    def sb_attention(self, l, a):
        K, V, S = self.K, self.K.nc.vector, self.K.nc.scalar
        D = a.sub
        q, k, v = D("q", [P, 2, SEQ]), D("k", [P, 2, SEQ]), D("v", [P, QT, BR])
        lk = [D(f"log_keep{b}", [P, SEQ - b * P]) for b in range(QT)]
        e, z = D("e", [P, SEQ]), D("z", [P, SEQ])
        wt = [D(f"weight{b}", [P, SEQ - b * P]) for b in range(QT)]
        marks = []
        for j in range(2):
            i, done = self.features(COL["sb_q"][j * P:(j + 1) * P], (l,), after=a.after)
            marks.append(self.plain(i, done, q[:, j, :], scale=SCALE))
            i, done = self.features(COL["sb_k"][j * P:(j + 1) * P], (l,))
            marks.append(self.plain(i, done, k[:, j, :]))
        marks.append(self.values(COL["sb_v"], (l,), v[:, :, :].rearrange("p t c -> p (t c)")))
        read = []
        for h in range(HEADS):
            lo, j = HD * (h % 2), h // 2
            for b in range(QT):
                n = SEQ - b * P
                i = K.next_banks()
                done = K.mm(K.bank(i)[:, 0:n], k[lo:lo + HD, j, b * P:(b + 1) * P],
                            q[lo:lo + HD, j, b * P:SEQ], True, True, mark=True, after=marks)
                m = K.dve(V.tensor_scalar, z[:, 0:n], K.bank(i)[:, 0:n], -1.0, None, ALU.mult,
                          after=[done])
                K.release(i, 1, m)
                m = self.log_sigmoid(z[:, 0:n], e[:, 0:n], lk[b][:, :], after=read)
                m = K.dve(V.tensor_tensor, lk[b][:, 0:P], lk[b][:, 0:P], self.c.before01, ALU.mult)
            K.fill()
            for b in range(QT):
                n = SEQ - b * P
                i = K.next_banks()
                bank = K.bank(i)
                K.mm(bank[:, 0:n], k[lo:lo + HD, j, b * P:(b + 1) * P], q[lo:lo + HD, j, b * P:SEQ],
                     True, False)
                K.mm(bank[:, 0:P], K.ident, self.c.before_add, False, False)
                K.mm(bank[:, 0:n], self.c.from_here, lk[b][:, :], False, b == QT - 1,
                     mark=True, after=[m])
                for b2 in range(b + 1, QT):
                    K.mm(bank[:, (b2 - b) * P:n], K.ones, lk[b2][:, :], False, b2 == QT - 1, mark=True)
                done = K.pe.last()
                w = K.act(S.activation, wt[b][:, :], bank[:, 0:n], ACT.Exp, after=[done] + read)
                K.release(i, 1, w)
            i = K.next_banks()
            for t in range(QT):
                for b in range(t + 1):
                    done = K.mm(K.bank(i)[:, t * HD:(t + 1) * HD], wt[b][:, (t - b) * P:(t - b + 1) * P],
                                v[:, b, h * HD:(h + 1) * HD], b == 0, b == t, mark=(b == t),
                                after=[w])
            read = [done]
            y = self.gate[:, 2, :].rearrange("p (t c) -> p t c", t=QT)[:, :, h * HD:(h + 1) * HD]
            m = K.dve(V.tensor_tensor, y,
                      K.bank(i)[:, 0:QT * HD].rearrange("p (t c) -> p t c", t=QT), y, ALU.mult,
                      after=[done, self.gates_ready])
            K.release(i, 1, m)

    def compress(self, l, a, x, which):
        K, V, S = self.K, self.K.nc.vector, self.K.nc.scalar
        blocks = a.sub("blocks_" + which, [P, CMP_LEN // 2, N_CMP])
        hid = a.sub("hidden_" + which, [P, N_CMP])
        pe_cols = self.small.pe[which][l]
        for g in range(2):
            src = bass.AP(tensor=x.tensor, offset=x[HD * g:HD * g + HD, g:g + 1].offset,
                          ap=[[x.ap[0][0], HD], [2, CMP_LEN // 2], [CMP_STRIDE, N_CMP]])
            p = pe_cols[HD * g:HD * g + HD, :]
            pe_b = bass.AP(tensor=p.tensor, offset=p.offset,
                           ap=[[p.ap[0][0], HD], [1, CMP_LEN // 2], [0, N_CMP]])
            m = K.dve(V.tensor_tensor, blocks[HD * g:HD * g + HD, :, :], src, pe_b, ALU.add,
                      after=[K.act.last()])
        rows = ((2 * np.arange(CMP_LEN // 2)[:, None] + np.arange(P)[None, :] // HD) * HD
                + np.arange(P)[None, :] % HD)
        w, c = K.stream.piece("nsa_wc1_" + which, (l,), rows, np.arange(CMP_HIDDEN))
        i = K.next_banks()
        for j in range(CMP_LEN // 2):
            done = K.mm(K.bank(i)[:, 0:N_CMP], w[:, j, :], blocks[:, j, :], j == 0,
                        j == CMP_LEN // 2 - 1, mark=(j == CMP_LEN // 2 - 1), after=[m])
        K.stream.used(c, done)
        m = K.act(S.activation, hid[:, :], K.bank(i)[:, 0:N_CMP], ACT.Silu, after=[done])
        K.release(i, 1, m)
        return hid, m

    def nsa(self, l, a):
        K, V, S = self.K, self.K.nc.vector, self.K.nc.scalar
        D = a.sub
        q = D("q", [P, 2, SEQ])
        twice = {n: D(n, [P, SEQ]) for n in ("nsa_kc", "nsa_vc", "nsa_ks", "nsa_kw")}
        v = D("v", [P, QT, 2 * HD])
        kct, vc = D("k_cmp", [P, N_CMP]), D("v_cmp", [N_CMP, HD])
        acc = D("mixed", [P, QT, BR])
        coef = D("coef", [P, HEADS])
        for n in twice:
            i, done = self.features(np.tile(COL[n], 2), (l,), after=a.after)
            if n == "nsa_vc":
                self.plain(i, done, twice[n][:, :])
            else:
                self.rope(i, done, twice[n][:, :], self.rope64, self.c.perm64)
        for j in range(2):
            i, done = self.features(COL["nsa_q"][j * P:(j + 1) * P], (l,))
            ready = self.rope(i, done, q[:, j, :], self.rope64, self.c.perm64)
        mv = self.values(np.concatenate([COL["nsa_vs"], COL["nsa_vw"]]), (l,),
                         v[:, :, :].rearrange("p t c -> p (t c)"))
        hid, m = self.compress(l, a, twice["nsa_kc"][:, :], "k")
        w, c = K.stream.piece("nsa_wc2_k", (l,), rows_of(1), np.tile(np.arange(HD), 2))
        i = K.next_banks()
        done = K.mm(K.bank(i)[:, 0:N_CMP], w[:, 0, :], hid[:, :], True, True, mark=True, after=[m])
        K.stream.used(c, done)
        m1 = K.copy(kct[:, :], K.bank(i)[:, 0:N_CMP], after=[done])
        K.release(i, 1, m1)
        hid, m = self.compress(l, a, twice["nsa_vc"][:, :], "v")
        w, c = K.stream.piece("nsa_wc2_v", (l,), rows_of(1), np.arange(HD))
        i = K.next_banks()
        done = K.mm(K.bank(i)[0:N_CMP, 0:HD], hid[:, :], w[:, 0, :], True, True, mark=True, after=[m])
        K.stream.used(c, done)
        m2 = K.copy(vc[:, :], K.bank(i)[0:N_CMP, 0:HD], after=[done])
        K.release(i, 1, m2)
        ks, kw = twice["nsa_ks"], twice["nsa_kw"]

        def finish(which):
            def end(u, o, done):
                m = K.dve(V.tensor_tensor, coef[:, :], u.inv,
                          self.mix[:, u.qt, which * HEADS:(which + 1) * HEADS], ALU.mult,
                          after=[self.gates_ready])
                for h in range(HEADS):
                    y = acc[:, u.qt, h * HD:(h + 1) * HD]
                    oh, ch = o[:, h * HD:(h + 1) * HD], coef[:, h:h + 1]
                    if which == 0:
                        m = K.dve(V.tensor_scalar, y, oh, ch, None, ALU.mult, after=[done])
                    else:
                        m = K.dve(V.scalar_tensor_tensor, y, oh, ch, y, ALU.mult, ALU.add,
                                  after=[done])
                if which == 2:
                    z = self.gate[:, 3, u.qt * BR:(u.qt + 1) * BR]
                    K.dve(V.tensor_tensor, z, acc[:, u.qt, :], z, ALU.mult)
                return m
            return end

        cmp_l = self.pair_logits(q, kct, [ready, m1, m2, mv])
        slc_l = self.pair_logits(q, ks, [ready])
        win_l = self.pair_logits(q, kw, [ready])
        units = []
        for t in range(QT):
            units.append(Unit(N_CMP, cmp_l(t), self.c.cmp_add[:, t * N_CMP:(t + 1) * N_CMP],
                              self.c.cmp_keep[:, t * N_CMP:(t + 1) * N_CMP],
                              lambda h, b: vc[:, :], finish(0), t))
            units.append(Unit((t + 1) * P, slc_l(t), self.causal(t), None,
                              lambda h, b: v[:, b, 0:HD], finish(1), t))
            units.append(Unit((t + 1) * P, win_l(t), self.causal(t), None,
                              lambda h, b: v[:, b, HD:2 * HD], finish(2), t))
        softmax_attention(K, units, self.scratch)

    def memory(self, l, a):
        K = self.K
        D = a.sub
        nt = N_MEM // P
        q, k, v = D("q", [P, 2, SEQ]), D("k", [P, 2, N_MEM]), D("v", [P, nt, BR])
        mem = D("mem_t", [P, KT, N_MEM])
        K.act.eng.dma_start(mem[:, :, :], self.dram_mem).then_inc(self.mem_sem, 16)
        loaded = (self.mem_sem, 16 * (l + 1))
        marks = []
        for j in range(2):
            i, done = self.features(COL["mem_q"][j * P:(j + 1) * P], (l,), after=a.after)
            marks.append(self.plain(i, done, q[:, j, :]))
        K.dve.wait(loaded)
        K.act.wait(loaded)
        n = K.rms_features(mem, KT, 0, N_MEM, lambda kk: self.small.mem_norm[l][kk], mem, self.sq8,
                           D_MODEL)
        for j in range(2):
            i, done = self.features(np.arange(j * P, (j + 1) * P), (l,), x=mem, name="w_mem_kv",
                                    spans=((0, N_MEM),), after=n)
            m = K.copy(k[:, j, :], K.bank(i)[:, 0:N_MEM], after=[done])
            K.release(i, 1, m)
            marks.append(m)
        marks.append(self.values(BR + np.arange(BR), (l,), v[:, :, :].rearrange("p t c -> p (t c)"),
                                 ntile=nt, x=mem, name="w_mem_kv"))
        logits = self.pair_logits(q, k, marks)
        units = [Unit(N_MEM, logits(t), self.c.causal[:, 0:N_MEM], None,
                      lambda h, b: v[:, b, h * HD:(h + 1) * HD], self.finish_plain(4), t)
                 for t in range(QT)]
        softmax_attention(K, units, self.scratch)

    def merge_later(self, l, b, first):
        K, V, S = self.K, self.K.nc.vector, self.K.nc.scalar

        def tile(d):
            i, done = self.features(COL["merge"][b * D_MODEL + d * P:b * D_MODEL + (d + 1) * P], (l,))
            s = self.sig.take()
            g = K.act(S.activation, s.t[:, :], K.bank(i), ACT.Tanh, scale=0.5, after=[done] + s.free)
            K.release(i, 1, g)
            y = self.gate[:, b, :].rearrange("p (j n) -> p j n", j=2)
            i, done = self.features(np.arange(d * P, (d + 1) * P), (l, b), x=y, name="w_branch", k=2,
                                    after=[self.turned_at[b]])
            dst = self.merged[:, d, :] if first else s.t[:, :]
            m = K.dve(V.scalar_tensor_tensor, dst, s.t[:, :], 1.0, K.bank(i), ALU.add, ALU.mult,
                      after=[done, g])
            K.release(i, 1, m)
            if not first:
                m = K.dve(V.tensor_tensor, self.merged[:, d, :], self.merged[:, d, :], s.t[:, :],
                          ALU.add)
            s.free = [m]
            self.merged_ready = m

        for d in range(KT):
            K.later.append(lambda d=d: tile(d))

    def merge_out(self, l):
        K, V = self.K, self.K.nc.vector
        for d in range(KT):
            i, done = self.features(np.arange(d * P, (d + 1) * P), (l,), x=self.merged, name="w_out",
                                    after=[self.merged_ready])
            r = K.dve(V.scalar_tensor_tensor, self.x[:, d, :], K.bank(i), 0.25, self.x[:, d, :],
                      ALU.mult, ALU.add, after=[done])
            K.release(i, 1, r)
        return r

    def tables(self, st):
        K, V, S = self.K, self.K.nc.vector, self.K.nc.scalar
        pos_i = K.sb("pos_i", [P, SEQ], st, I32)
        pos, ang, turn, red = (K.sb(n, [P, SEQ], st) for n in ("pos", "angle", "turns", "reduced"))
        K.sp.eng.dma_start(pos_i[:, :], self.dram_pos.partition_broadcast(P)).then_inc(self.pos_sem, 16)
        K.dve(V.tensor_copy, pos[:, :], pos_i[:, :], after=[(self.pos_sem, 16), self.consts_loaded])
        two_pi = 2.0 * np.pi
        c1 = 6.28125
        c2 = float(np.float32(np.round((two_pi - c1) * 2.0 ** 20) / 2.0 ** 20))
        c3 = float(np.float32(two_pi - c1 - c2))
        magic = 1.5 * 2.0 ** 23
        for (cos, sin), inv, sign in ((self.rope64, self.c.inv64, self.c.sign64),
                                      (self.rope32, self.c.inv32, self.c.sign32)):
            K.dve(V.tensor_scalar, ang[:, :], pos[:, :], inv, None, ALU.mult,
                  after=[K.act.last()])
            K.dve(V.tensor_scalar, turn[:, :], ang[:, :], float(1.0 / two_pi), magic, ALU.mult, ALU.add)
            K.dve(V.tensor_scalar, turn[:, :], turn[:, :], magic, None, ALU.subtract)
            for part, src in ((c1, ang), (c2, red), (c3, red)):
                K.dve(V.scalar_tensor_tensor, red[:, :], turn[:, :], -part, src[:, :], ALU.mult, ALU.add)
            pi = float(np.nextafter(np.float32(np.pi), np.float32(0)))
            m = K.dve(V.tensor_scalar, red[:, :], red[:, :], pi, -pi, ALU.min, ALU.max)
            m = K.act(S.activation, sin[:, :], red[:, :], ACT.Sin, after=[m])
            K.dve(V.tensor_scalar, sin[:, :], sin[:, :], sign, None, ALU.mult, after=[m])
            K.dve(V.scalar_tensor_tensor, red[:, :], red[:, :], -1.0, red[:, :], ALU.mult, ALU.min)
            m = K.dve(V.tensor_scalar, red[:, :], red[:, :], float(np.pi / 2), None, ALU.add)
            m = K.act(S.activation, cos[:, :], red[:, :], ACT.Sin, after=[m])
        K.dve.wait(m)

    def run(self):
        K, nc = self.K, self.K.nc
        V = nc.vector
        outer = ExitStack()
        cos64, sin64, cos32, sin32 = (K.sb(n, [P, SEQ], outer) for n in ("cos64", "sin64", "cos32", "sin32"))
        self.rope64, self.rope32 = (cos64[:, :], sin64[:, :]), (cos32[:, :], sin32[:, :])
        self.ones_row = K.sb("ones_row", [P, SEQ], outer)
        K.dve(V.memset, self.ones_row[:, :], 1.0)
        st = ExitStack()
        self.tables(st)
        K.barrier()
        st.close()
        for l in range(DEPTH):
            with ExitStack() as st:
                self.h = K.sb("h", [P, KT, SEQ], st)
                self.gate = K.sb("gate", [P, N_BRANCH, QT * BR], st)
                self.idx_w = K.sb("idx_w", [P, QT, IDX_HEADS], st)
                self.mix = K.sb("mix", [P, QT, 3 * HEADS], st)
                self.merged = K.sb("merged", [P, KT, SEQ], st)
                self.sig = Ring([Buf(K.sb(f"sig{i}", [P, SEQ], st)) for i in range(2)])
                self.turned_at = {}
                self.modulation.queue(l)
                with ExitStack() as s2:
                    self.sq8 = K.sb("squares", [P, KT, SEQ], s2)
                    self.h_ready = K.rms_features(self.x, KT, 0, SEQ, lambda k: self.small.norm_g[l][k],
                                                  self.h, self.sq8, D_MODEL)
                    self.gates(l)
                    K.barrier(pe=False)
                with ExitStack() as s2:
                    self.raw = Ring([Buf(K.sb(f"raw{i}", [P, SEQ], s2)) for i in range(2)])
                    self.rtmp = Ring([Buf(K.sb(f"rtmp{i}", [P, SEQ], s2)) for i in range(1)])
                    self.sq1 = K.sb("sq1", [P, 2, SEQ], s2)
                    self.top8 = K.sb("top8", [P, 8], s2)
                    self.scratch = Scratch(K, s2)
                    arenas = [Arena(K, s2, "big", 32 * 1024), Arena(K, s2, "small", 29 * 1024)]
                    K.area = [0, 6, 0]
                    for n, (b, branch) in enumerate(((1, self.fox), (0, self.dsa), (2, self.sb_attention),
                                                     (3, self.nsa))):
                        a = arenas[n % 2]
                        a.open()
                        branch(l, a)
                        self.turned_at[b] = self.turn_branch(b)
                        self.merge_later(l, b, n == 0)
                        a.close()
                    K.barrier()
                with ExitStack() as s2:
                    self.sq8 = K.sb("squares", [P, KT, N_MEM], s2)
                    self.scratch = Scratch(K, s2)
                    a = Arena(K, s2, "mem", 20 * 1024)
                    a.after = list(K.fence)
                    a.open()
                    self.memory(l, a)
                    self.turned_at[4] = self.turn_branch(4)
                    self.merge_later(l, 4, False)
                    K.fill(len(K.later))
                    K.area = [0, 8, 0]
                    self.merge_out(l)
                    K.barrier()
        with ExitStack() as st:
            sq = K.sb("squares", [P, KT, SEQ], st)
            K.rms_features(self.x, KT, 0, SEQ, lambda k: self.small.final_norm[k], self.x, sq, D_MODEL)
            K.barrier()
        outer.close()


class Scratch:

    def __init__(self, K, st, heads=HEADS, keys=SEQ, turned=4):
        self.probs = Ring([Buf(K.sb(f"probs{i}", [P, heads, keys], st)) for i in range(2)])
        self.turned = Ring([Buf(K.sb(f"turned{i}", [P, keys], st)) for i in range(turned)])
        self.cols = Ring([Buf(K.sb(f"softmax_cols{i}", [P, 16], st)) for i in range(3)])


class Arena:

    def __init__(self, K, st, name, size):
        self.K, self.t, self.size = K, K.sb("arena_" + name, [P, size // 4], st), size // 4
        self.after = []

    def open(self):
        self.at = 0
        for line in (self.K.dve, self.K.act, self.K.pool, self.K.pe):
            line.wait(*self.after)

    def sub(self, name, shape):
        n = int(np.prod(shape[1:]))
        if not self.at + n <= self.size:
            raise ValueError(name)
        t = self.t[0:shape[0], self.at:self.at + n]
        self.at += n
        if len(shape) == 3:
            return t.rearrange("p (a b) -> p a b", a=shape[1])
        return t

    def close(self):
        self.after = self.K.all_marks()


AB_COL, _o = {}, 0
for _name, _n in (("a", CONV_DIM), ("g", CONV_DIM), ("q", HEADS * ML_QK), ("k", HEADS * ML_QK),
                  ("v", HEADS * ML_V), ("o", HEADS * ML_V), ("gates", 4 * HEADS)):
    AB_COL[_name] = np.arange(_o, _o + _n)
    _o += _n
TT = TOK // P
CT = CTX // P
PAD = (CONV_WIDTH - 1) // 2
FT = FFN // P
BOTH = ((0, CTX), (CTX, TOK))
LATENT = ((CTX, TOK),)


class Modulation:

    def __init__(self, K, common, at):
        self.K = K
        self.silu_c = K.sb("silu_c", [P, KT, 2])
        self.c = [common[:, at[n]:at[n] + KT] for n in ("c", "c_ctx")]
        self.bias = [common[:, at["ada_b", l]:at["ada_b", l] + 6 * KT] for l in range(DEPTH)]
        self.mods = [K.sb(f"mods{l}", [P, 6 * KT, 2]) for l in range(DEPTH)]
        self.rows = Ring([Buf(K.sb(f"ada_row{i}", [2, BANK])) for i in range(2)])
        self.mods_ready = [None] * DEPTH

    def start(self):
        for side, c in enumerate(self.c):
            self.ready = self.K.act(self.K.nc.scalar.activation, self.silu_c[:, :, side], c, ACT.Silu)

    def queue(self, l):
        K, V, S, T = self.K, self.K.nc.vector, self.K.nc.scalar, self.K.nc.tensor
        half, per = KT // 2, BANK // P

        def products(c, got):
            i = K.next_banks()
            for part in range(2):
                w, ch = K.stream.piece("ada_w_2", (l,), rows_of(half, part * half * P),
                                       np.arange(c * BANK, (c + 1) * BANK))
                for k in range(half):
                    kk = part * half + k
                    done = K.mm(K.bank(i)[0:2, :], self.silu_c[:, kk, :], w[:, k, :], kk == 0,
                                kk == KT - 1, mark=(k == half - 1), after=[self.ready])
                K.stream.used(ch, done)
            row = self.rows.take()
            m = K.act(S.copy, row.t[:, :], K.bank(i)[0:2, :], after=[done] + row.free)
            K.release(i, 1, m)
            got.extend([row, m])

        def columns(c, got):
            row, copied = got
            i = K.next_banks()
            for j in range(per):
                done = K.pe(T.transpose, K.bank(i)[:, 2 * j:2 * j + 2], row.t[0:2, j * P:(j + 1) * P],
                            K.ident[0:2, 0:2], after=[copied], mark=True)
            row.free = [done]
            b = self.bias[l][:, c * per:(c + 1) * per]
            bias = bass.AP(tensor=b.tensor, offset=b.offset, ap=[[b.ap[0][0], P], [1, per], [0, 2]])
            out = self.mods[l][:, c * per:(c + 1) * per, :]
            one = 1.0 if c * per // KT in (1, 4) else 0.0
            m = K.dve(V.scalar_tensor_tensor, out,
                      K.bank(i)[:, 0:2 * per].rearrange("p (j s) -> p j s", s=2), one, bias, ALU.add,
                      ALU.add, after=[done])
            K.release(i, 1, m)
            self.mods_ready[l] = m

        before = None
        for c in range(6 * KT // per):
            got = []

            def step(c=c, got=got, before=before):
                products(c, got)
                if before:
                    columns(*before)
            K.later.append(step)
            before = (c, got)
        K.later.append(lambda: columns(*before))


class SecondBlock:

    def __init__(self, K, consts, small):
        self.K, self.c, self.small = K, consts, small

    def wide(self, w, chunk, x, spans, m=P, after=None, keep=None, k0=0, k1=None, last=True):
        K = self.K
        nk = w.shape[1]
        i = K.next_banks(2) if keep is None else keep
        for lo, hi in spans:
            for k in range(nk):
                first, end = k == 0 and k0 == 0, k == nk - 1 and last
                done = K.mm(K.bank(i, 2)[0:m, BANK - CTX + lo:BANK - CTX + hi], w[:, k, :],
                            x[:, k0 + k, lo:hi], first, end, mark=(k == nk - 1),
                            after=[after[lo][k]] if after else ())
        K.stream.used(chunk, done)
        return i, done

    def pair(self, i, lo=0, hi=TOK, m=P):
        return self.K.bank(i, 2)[0:m, BANK - CTX + lo:BANK - CTX + hi]

    def mod(self, l, which, k, side):
        return self.mods[l][:, which * KT + k, side:side + 1]

    def modulate(self, l, shift, scale, h, sq, with_ctx=True):
        K = self.K
        sides = ([(1, self.xc, 0, CTX, sq[1])] if with_ctx else []) + [(0, self.x, CTX, SEQ, sq[0])]
        norms = []
        for side, x, at, n, s in sides:
            norms.append(Norm(K, x, KT, 0, n, lambda k, side=side: self.mod(l, scale, k, side),
                              h[:, :, at:at + n], s, D_MODEL,
                              shift=lambda k, side=side: self.mod(l, shift, k, side)))
        for n in norms:
            n.squares([self.mods_ready[l]])
        for n in norms:
            n.sums()
        K.fill()
        for n in norms:
            n.inverse()
        return {side[2]: n.apply() for side, n in zip(sides, norms)}

    def residual(self, i, done, l, which, d, with_ctx=True):
        K, V = self.K, self.K.nc.vector
        m = K.dve(V.scalar_tensor_tensor, self.x[:, d, :], self.pair(i, CTX, TOK),
                  self.mod(l, which, d, 0), self.x[:, d, :], ALU.mult, ALU.add, after=[done])
        if with_ctx:
            m = K.dve(V.scalar_tensor_tensor, self.xc[:, d, :], self.pair(i, 0, CTX),
                      self.mod(l, which, d, 1), self.xc[:, d, :], ALU.mult, ALU.add)
        K.release(i, 2, m)
        return m

    def conformer(self, l, st):
        K, V, S, T = self.K, self.K.nc.vector, self.K.nc.scalar, self.K.nc.tensor
        y = K.sb("mixed_features", [P, 2 * HEADS, TOK], st)
        q, k = K.sb("ml_q", [P, HEADS, TOK], st), K.sb("ml_k", [P, 2, TOK], st)
        v = K.sb("ml_v", [P, TT, HEADS, ML_V + 1], st)
        rows_r = K.sb("ml_rows", [64, TOK], st)
        cols = K.sb("ml_cols", [P, TT, P], st)
        with ExitStack() as s1:
            h = K.sb("h2", [P, KT, TOK], s1)
            with ExitStack() as s2:
                sq = K.sb("squares2", [P, KT, SEQ], s2), K.sb("squares_ctx", [P, KT, CTX], s2)
                ready = self.modulate(l, 0, 1, h, sq)
                K.barrier(pe=False)
            lat0 = 3 * PAD + CTX
            up = K.sb("padded", [P, 4, CTX + SEQ + 4 * PAD], s1)
            sig = Ring([Buf(K.sb(f"sig2{i}", [P, TOK], s1)) for i in range(2)])
            pre, tmp = K.sb("gate_pre", [P, TOK], s1), K.sb("gate_tmp", [P, TOK], s1)
            stack = K.sb("gate_stack", [P, TOK], s1)
            b, cmx = K.sb("gate_sum", [64, TOK], s1), K.sb("gate_max", [64, TOK], s1)
            one = K.sb("one_row", [64, TOK], s1)
            m3 = K.pool(K.nc.gpsimd.memset, q[:, :, :], 0.0)
            mz = K.pool(K.nc.gpsimd.memset, up[:, :, :], 0.0)
            m1 = K.pool(K.nc.gpsimd.memset, v[:, :, :, ML_V:ML_V + 1], 1.0)
            m2 = K.pool(K.nc.gpsimd.memset, one[:, :], 1.0)
            K.area = [0, 6, 0]

            def projected(name, c):
                w, ch = K.stream.piece("ab_w_in_2", (0,), rows_of(KT),
                                       AB_COL[name][c * P:(c + 1) * P])
                return self.wide(w, ch, h, BOTH, after=ready)

            def gated(c):
                i, done = projected("g", c)
                s = sig.take()
                g = K.act(S.activation, s.t[:, :], self.pair(i), ACT.Sigmoid, after=[done] + s.free)
                K.release(i, 2, g)
                i, done = projected("a", c)
                K.dve(V.tensor_tensor, up[:, c, PAD:PAD + CTX], self.pair(i, 0, CTX), s.t[:, 0:CTX],
                      ALU.mult, after=[done, g, mz])
                m = K.dve(V.tensor_tensor, up[:, c, lat0:lat0 + SEQ], self.pair(i, CTX, TOK),
                          s.t[:, CTX:TOK], ALU.mult)
                K.release(i, 2, m)
                s.free = [m]

            def convolve(c):
                K.dve.wait(*K.banks[6].free, *K.banks[7].free)
                cw = self.small.conv_w[c]
                for lo, n, at in ((0, CTX, 0), (CTX, SEQ, lat0 - PAD)):
                    acc = self.pair(6, lo, lo + n)
                    K.dve(V.tensor_scalar, acc, up[:, c, at:at + n], cw[:, 0:1], self.small.conv_b[c],
                          ALU.mult, ALU.add)
                    for j in range(1, CONV_WIDTH):
                        m = K.dve(V.scalar_tensor_tensor, acc, up[:, c, at + j:at + j + n],
                                  cw[:, j:j + 1], acc, ALU.mult, ALU.add)
                return m

            def convolved(c, m):
                m = K.act(S.copy, y[:, c, :], self.pair(6), after=[m])
                K.release(6, 2, m)

            def queries(j):
                i, done = projected("q", j)
                for g in range(2):
                    half = slice(ML_QK * g, ML_QK * (g + 1))
                    m = K.act(S.copy, q[half, 2 * j + g, :], self.pair(i)[half, :], after=[done, m3])
                K.release(i, 2, m)

            def keys(j):
                i, done = projected("k", j)
                m = K.act(S.activation, k[:, j, :], self.pair(i), ACT.Copy, scale=ML_QK ** -0.5,
                          after=[done])
                K.release(i, 2, m)

            def out_gates(c):
                i, done = projected("o", c)
                m = K.act(S.activation, y[:, 4 + c, :], self.pair(i), ACT.Sigmoid, after=[done])
                K.release(i, 2, m)

            g4 = AB_COL["gates"].reshape(4, HEADS)[[0, 2, 1, 3]]
            w, ch = K.stream.piece("ab_w_in_2", (0,), rows_of(KT), np.tile(g4, (1, 32 // HEADS)).ravel())
            i, done = self.wide(w, ch, h, BOTH, after=ready)
            m = K.dve(V.tensor_scalar, pre[:, :], self.pair(i), self.small.gate_bias, None, ALU.add,
                      after=[done])
            K.release(i, 2, m)
            fg, e = pre[64:128, :], tmp[64:128, :]
            K.dve(V.scalar_tensor_tensor, e, fg, -1.0, fg, ALU.mult, ALU.min)
            K.act(S.activation, e, e, ACT.Exp, after=[K.dve.last()])
            m = K.act(S.activation, e, e, ACT.Ln, bias=1.0)
            lf = tmp[0:64, :]
            K.dve(V.scalar_tensor_tensor, lf, fg, 0.0, e, ALU.min, ALU.subtract, after=[m])

            def scans(out, data, op, init):
                K.dve(V.tensor_tensor_scan, out[0:32, :], one[0:32, :], data[0:32, :], init, ALU.mult,
                      op, after=[m2])
                K.dve(V.tensor_tensor_scan, out[32:64, 0:CTX][:, ::-1], one[32:64, 0:CTX],
                      data[32:64, 0:CTX][:, ::-1], init, ALU.mult, op)
                K.dve(V.tensor_tensor_scan, out[32:64, CTX:TOK][:, ::-1], one[32:64, 0:SEQ],
                      data[32:64, CTX:TOK][:, ::-1], out[32:64, 0:1], ALU.mult, op)

            scans(b, lf, ALU.add, 0.0)
            K.dve(V.tensor_tensor, stack[0:64, :], pre[0:64, :], b[:, :], ALU.subtract)
            scans(cmx, stack, ALU.max, LOWEST)
            K.dve(V.tensor_tensor, cmx[:, :], cmx[:, :], b[:, :], ALU.add)
            K.dve(V.tensor_scalar, cmx[:, :], cmx[:, :], 0.0, None, ALU.max)
            rows_ready = K.dve(V.tensor_tensor, rows_r[:, :], b[:, :], cmx[:, :], ALU.subtract)
            m = K.act(S.activation, stack[64:128, :], cmx[:, :], ACT.Exp, scale=-1.0,
                      after=[rows_ready])
            i = K.next_banks(2)
            for t in range(TT):
                done = K.pe(T.transpose, K.bank(i, 2)[:, t * P:(t + 1) * P],
                            stack[:, t * P:(t + 1) * P], K.ident, after=[m], mark=True)
            m = K.act(S.copy, cols[:, :, :].rearrange("p t c -> p (t c)"), K.bank(i, 2)[:, 0:TOK],
                      after=[done])
            K.release(i, 2, m)
            cols_ready = m
            for c, beside in enumerate(((queries, 0, queries, 1), (keys, 0, keys, 1),
                                        (out_gates, 0, out_gates, 1, out_gates, 2))):
                gated(c)
                cm = convolve(c)
                for step, j in zip(beside[::2], beside[1::2]):
                    step(j)
                convolved(c, cm)
            gated(3)
            cm = convolve(3)
            half = KT // 2
            for c in range(2):
                first = K.next_banks(3)
                for part in range(2):
                    w, ch = K.stream.piece("ab_w_in_2", (0,), rows_of(half, part * half * P),
                                           AB_COL["v"])
                    for t in range(3):
                        tt = 3 * c + t
                        for kk in range(half):
                            kg = part * half + kk
                            done = K.mm(K.bank(first + t), h[:, kg, tt * P:(tt + 1) * P], w[:, kk, :],
                                        kg == 0, kg == KT - 1, mark=(kk == half - 1))
                        if part:
                            m = K.act(S.copy, v[:, tt, :, 0:ML_V],
                                      K.bank(first + t).rearrange("p (h d) -> p h d", h=HEADS),
                                      after=[done])
                            K.release(first + t, 1, m)
                    K.stream.used(ch, done)
            out_gates(3)
            convolved(3, cm)
            K.area = [0, 8, 0]
            K.barrier()
        with ExitStack() as s1:
            sq = K.sb("squares3", [P, 4, TOK], s1)
            i = K.next_banks(2)
            for lo, hi in BOTH:
                for c in range(4):
                    done = K.mm(self.pair(i, lo, hi), K.ones, y[:, c, lo:hi], c == 0, c == 3,
                                mark=(c == 3))
            for c in range(4):
                m = K.dve(V.scalar_tensor_tensor, y[:, c, :], self.pair(i), -1.0 / CONV_DIM, y[:, c, :],
                          ALU.mult, ALU.add, after=[done])
            K.release(i, 2, m)
            K.rms_features(y[:, 0:4, :], 4, 0, TOK, lambda c: self.small.ln_g[c], y[:, 0:4, :], sq,
                           CONV_DIM, shift=lambda c: self.small.ln_b[c], after=[m], func=ACT.Silu)
            K.barrier()
        with ExitStack() as s1:
            self.mlstm(l, s1, y, q, k, v, rows_r, cols, cols_ready, rows_ready)
            K.barrier()
        for d in range(KT):
            w, ch = K.stream.piece("ab_w_out_2", (0,), rows_of(KT), np.arange(d * P, (d + 1) * P))
            i, done = self.wide(w, ch, y, BOTH)
            self.residual(i, done, l, 2, d)

    def mlstm(self, l, st, y, q, k, v, rows_r, cols, cols_ready, rows_ready):
        K, V, S, T = self.K, self.K.nc.vector, self.K.nc.scalar, self.K.nc.tensor
        hs = K.sb("ml_out", [P, TT, HEADS * ML_V], st)
        weights = Ring([Buf(K.sb(f"ml_weights{i}", [P, TT, TOK], st)) for i in range(3)])
        rowdiag = Ring([Buf(K.sb(f"ml_diag{i}", [P, TT, P], st)) for i in range(2)])
        den = K.sb("ml_den", [P, 16], st)
        todo = [(d, h) for h in range(HEADS) for d in range(2)]

        def seen_by(d, kb):
            if d == 0:
                return [(kb + 1, TT)] if kb + 1 < TT else []
            if kb < CT:
                return ([(0, kb)] if kb else []) + [(CT, TT)]
            return [(CT, kb)] if kb > CT else []

        def rows_of_head(d, h):
            r = 32 * d + h
            one = K.ident[0:64, r:r + 1]
            sel = bass.AP(tensor=one.tensor, offset=one.offset, ap=[[one.ap[0][0], 64], [0, P]])
            i = 0
            K.claim(i, 2)
            for lo, hi in BOTH:
                done = K.mm(self.pair(i, lo, hi), sel, rows_r[0:64, lo:hi], True, True, mark=True,
                            after=[rows_ready])
            rd = rowdiag.take()
            mask = self.c.ml_mask[d]
            mask6 = bass.AP(tensor=mask.tensor, offset=mask.offset,
                            ap=[[mask.ap[0][0], P], [0, TT], [1, P]])
            m = K.dve(V.tensor_tensor, rd.t[:, :, :], self.pair(i).rearrange("p (t c) -> p t c", t=TT),
                      mask6, ALU.add, after=[done] + rd.free)
            return i, rd, m

        def exponentials(d, h):
            i, rd, m = rows_of_head(d, h)
            w = weights.take()
            for kb in range(TT):
                u = cols[:, kb, 32 * d + h:32 * d + h + 1]
                K.act(S.activation, w.t[:, kb, kb * P:(kb + 1) * P], rd.t[:, kb, :], ACT.Exp, bias=u,
                      after=[m, cols_ready] + w.free)
                for a, b in seen_by(d, kb):
                    K.act(S.activation, w.t[:, kb, a * P:b * P], self.pair(i, a * P, b * P), ACT.Exp,
                          bias=u)
            e = K.act.last()
            rd.free = [e]
            K.release(i, 2, e)
            return d, h, w, e

        def scores(d, h, w, e):
            for kb in range(TT):
                s = 2 + 2 * (kb % 2)
                K.claim(s, 2)
                ranges = sorted(seen_by(d, kb) + [(kb, kb + 1)])
                joined = [list(ranges[0])]
                for a, b in ranges[1:]:
                    if a == joined[-1][1]:
                        joined[-1][1] = b
                    else:
                        joined.append([a, b])
                for a, b in joined:
                    for lo, hi in BOTH:
                        x0, x1 = max(a * P, lo), min(b * P, hi)
                        if x0 < x1:
                            done = K.mm(self.pair(s, x0, x1), k[:, h // 2, kb * P:(kb + 1) * P],
                                        q[:, h, x0:x1], True, True, mark=True)
                for a, b in joined:
                    m = K.dve(V.tensor_tensor, w.t[:, kb, a * P:b * P], self.pair(s, a * P, b * P),
                              w.t[:, kb, a * P:b * P], ALU.mult, after=[done, e])
                K.release(s, 2, m)
            return d, h, w, m

        def read(d, h, w, ready):
            n = ML_V + 1
            K.claim(6, 2)
            place = lambda t: 6 * BANK + (t // 3) * BANK + (t % 3) * n
            for t in range(TT):
                kbs = [kb for kb in range(TT) if kb == t or any(a <= t < b for a, b in seen_by(d, kb))]
                for kb in kbs:
                    done = K.mm(K.psum[:, place(t):place(t) + n], w.t[:, kb, t * P:(t + 1) * P],
                                v[:, kb, h, :], kb == kbs[0], kb == kbs[-1], mark=(kb == kbs[-1]),
                                after=[ready])
            w.free = [done]
            o2 = K.bank(6, 2).rearrange("p (b c) -> p b c", b=2)
            dcol = o2[:, :, 0:3 * n].rearrange("p b (t c) -> p b t c", t=3)[:, :, :, ML_V]
            d6 = den[:, 0:TT].rearrange("p (b t) -> p b t", b=2)
            K.dve(V.tensor_scalar, d6, dcol, -1.0, None, ALU.mult, after=[done])
            K.dve(V.tensor_tensor, d6, dcol, d6, ALU.max)
            K.dve(V.tensor_tensor, den[:, 0:TT], den[:, 0:TT], cols[:, :, 64 + 32 * d + h], ALU.max)
            K.dve(V.reciprocal, den[:, 0:TT], den[:, 0:TT])
            for t in range(TT):
                o = hs[:, t, h * ML_V:(h + 1) * ML_V]
                num = K.psum[:, place(t):place(t) + ML_V]
                if d == 0:
                    m = K.dve(V.tensor_scalar, o, num, den[:, t:t + 1], None, ALU.mult)
                else:
                    m = K.dve(V.scalar_tensor_tensor, o, num, den[:, t:t + 1], o, ALU.mult, ALU.add)
            K.release(6, 2, m)

        made, scored = {}, {}
        for n in range(len(todo) + 2):
            if n < len(todo):
                made[n] = exponentials(*todo[n])
            if 1 <= n <= len(todo):
                scored[n - 1] = scores(*made[n - 1])
            if n >= 2:
                read(*scored[n - 2])
        n = TT * HEADS
        ss, tmp2, rs = (K.sb(f"ml_small{i}", [P, n], st) for i in range(3))
        sqr = K.sb("ml_squares", [P, ML_V], st)
        last = K.dve.last()
        for t in range(TT):
            for h in range(HEADS):
                m = K.act(S.activation, sqr[:, :], hs[:, t, h * ML_V:(h + 1) * ML_V], ACT.Square,
                          accum_out=ss[:, t * HEADS + h:t * HEADS + h + 1], after=[last])
        m = K.dve(V.tensor_scalar, ss[:, :], ss[:, :], 1.0 / ML_V, EPS, ALU.mult, ALU.add, after=[m])
        K.rsqrt_small(rs[:, :], ss[:, :], tmp2[:, :], after=[m])
        rsb = bass.AP(tensor=rs[:, :].tensor, offset=rs[:, :].offset, ap=[[n, P], [1, n], [0, ML_V]])
        hv = hs[:, :, :].rearrange("p t c -> p (t c)").rearrange("p (n d) -> p n d", d=ML_V)
        m = K.dve(V.tensor_tensor, hv, hv, rsb, ALU.mult)
        for h in range(HEADS):
            i = 2 * (h % 3)
            K.claim(i, 2)
            for t in range(TT):
                done = K.pe(T.transpose, self.pair(i, t * P, (t + 1) * P),
                            hs[:, t, h * ML_V:(h + 1) * ML_V], K.ident, after=[m], mark=True)
            g = K.dve(V.scalar_tensor_tensor, y[:, HEADS + h, :], self.pair(i), self.small.head_gain[h],
                      y[:, HEADS + h, :], ALU.mult, ALU.mult, after=[done])
            K.release(i, 2, g)

    def latent_attention(self, l, st):
        K, V, S, T = self.K, self.K.nc.vector, self.K.nc.scalar, self.K.nc.tensor
        H = MLA_HEADS
        room = K.sb("mla_latents", [P, QT * H * MLA_V], st)
        cq = room[:, 0:4 * SEQ].rearrange("p (j n) -> p j n", j=4)
        ckv = room[:, 4 * SEQ:4 * SEQ + 2 * TOK].rearrange("p (j n) -> p j n", j=2)
        out = room[:, :].rearrange("p (t c) -> p t c", t=QT)
        kr = K.sb("k_rope", [P, TT, MLA_ROPE], st)
        sk, sq_ = K.sb("sum_k", [P, TT * H], st), K.sb("sum_q", [P, QT * H], st)
        rk, rq = K.sb("rstd_k", [P, TT * H], st), K.sb("rstd_q", [P, QT * H], st)
        small = K.sb("mla_small", [P, TT * H], st)
        with ExitStack() as s2:
            h = K.sb("h2", [P, KT, TOK], s2)
            with ExitStack() as s3:
                sq = K.sb("squares2", [P, KT, SEQ], s3), K.sb("squares_ctx", [P, KT, CTX], s3)
                ready = self.modulate(l, 0, 1, h, sq)
                K.barrier(pe=False)
            for j in range(4):
                w, ch = K.stream.piece("mla_w_in_2", (0,), rows_of(KT), np.arange(j * P, (j + 1) * P))
                i, done = self.wide(w, ch, h, LATENT, after=ready)
                m = K.copy(cq[:, j, :], self.pair(i, CTX, TOK), after=[done])
                K.release(i, 2, m)
            mq = [K.act.last(), K.dve.last()]
            for j in range(2):
                w, ch = K.stream.piece("mla_w_in_2", (0,), rows_of(KT),
                                       MLA_Q_LORA + np.arange(j * P, (j + 1) * P))
                i, done = self.wide(w, ch, h, BOTH, after=ready)
                m = K.copy(ckv[:, j, :], self.pair(i), after=[done])
                K.release(i, 2, m)
            w, ch = K.stream.piece("mla_w_in_2", (0,), rows_of(KT),
                                   MLA_Q_LORA + MLA_KV_LORA + np.arange(MLA_ROPE))
            i = K.next_banks()
            for t in range(TT):
                for kk in range(KT):
                    done = K.mm(K.bank(i)[:, t * MLA_ROPE:(t + 1) * MLA_ROPE],
                                h[:, kk, t * P:(t + 1) * P], w[:, kk, :], kk == 0, kk == KT - 1,
                                mark=(kk == KT - 1))
            K.stream.used(ch, done)
            m = K.act(S.copy, kr[:, :, :].rearrange("p t c -> p (t c)"),
                      K.bank(i)[:, 0:TT * MLA_ROPE], after=[done])
            K.release(i, 1, m)
            K.barrier()
        kt = K.sb("mla_k", [P, TT, H, MLA_QK], st)
        v = K.sb("mla_v", [P, TT, H, MLA_V], st)
        qt = K.sb("mla_q", [P, QT, H, MLA_QK], st)
        with ExitStack() as s1:
            sq = K.sb("squares4", [P, 4, TOK], s1)
            nq = K.rms_features(cq, 4, 0, SEQ, lambda j: self.small.q_norm[j], cq, sq, MLA_Q_LORA)
            nk = K.rms_features(ckv, 2, 0, TOK, lambda j: self.small.kv_norm2[j], ckv, sq, MLA_KV_LORA,
                                after=nq)
            flat = qt[:, :, :, :].rearrange("p t h d -> p t (h d)")
            squares = Ring([Buf(K.sb(f"mla_sq{i}", [P, BANK], s1)) for i in range(3)])
            sr = K.sb("mla_sr", [P, TT], s1)
            half = MLA_ROPE // 2
            t1 = K.sb("rot1", [P, H, half], s1)
            t2 = K.sb("rot2", [P, H, half], s1)
            per = 4

            def head_sums(x, sums, dim, after):
                s = squares.take()
                sv = s.t[:, 0:per * dim].rearrange("p (h d) -> p h d", h=per)
                q = K.act(S.activation, sv, x, ACT.Square, after=after + s.free)
                m = K.dve(V.tensor_reduce, sums, sv, AX_X, ALU.add, after=[q])
                s.free = [m]
                return q

            def inverse_rms(sums, out, n):
                m = K.dve(V.tensor_scalar, sums, sums, 1.0 / MLA_QK, EPS, ALU.mult, ALU.add)
                return K.rsqrt_small(out, sums, small[:, 0:n], after=[m])

            def rotate(x, heads, cos, sin):
                xp = x.rearrange("p h (i two) -> p h i two", two=2)
                even, odd = xp[:, :, :, 0], xp[:, :, :, 1]
                rep = lambda a: bass.AP(tensor=a.tensor, offset=a.offset,
                                        ap=[[a.ap[0][0], P], [0, heads], [1, half]])
                a, b = t1[:, 0:heads, :], t2[:, 0:heads, :]
                K.dve(V.tensor_tensor, a, even, rep(sin), ALU.mult)
                K.dve(V.tensor_tensor, b, odd, rep(sin), ALU.mult)
                K.dve(V.tensor_tensor, even, even, rep(cos), ALU.mult)
                K.dve(V.tensor_tensor, even, even, b, ALU.subtract)
                K.dve(V.tensor_tensor, odd, odd, rep(cos), ALU.mult)
                K.dve(V.tensor_tensor, odd, odd, a, ALU.add)

            def gain(x, heads, g, after=()):
                gb = bass.AP(tensor=g.tensor, offset=g.offset,
                             ap=[[g.ap[0][0], P], [0, heads], [1, MLA_ROPE]])
                K.dve(V.tensor_tensor, x, x, gb, ALU.mult, after=after)

            n = per * MLA_QK
            for c in range(H // per):
                w, ch = K.stream.piece("mla_w_uq_2", (0,), rows_of(4), np.arange(c * n, (c + 1) * n))
                for t in range(QT):
                    i = K.next_banks()
                    for j in range(4):
                        done = K.mm(K.bank(i)[:, 0:n], cq[:, j, t * P:(t + 1) * P], w[:, j, :], j == 0,
                                    j == 3, mark=(j == 3), after=nq)
                    m = K.copy(flat[:, t, c * n:(c + 1) * n], K.bank(i)[:, 0:n], after=[done],
                               engine=K.dve)
                    q = head_sums(K.bank(i)[:, 0:n].rearrange("p (h d) -> p h d", h=per),
                                  sq_[:, t * H + c * per:t * H + (c + 1) * per], MLA_QK, [m])
                    K.release(i, 1, q)
                K.stream.used(ch, done)
            kr_marks = []
            for t in range(TT):
                kr_marks.append(K.act(S.activation, small[:, 0:MLA_ROPE], kr[:, t, :], ACT.Square,
                                      accum_out=sr[:, t:t + 1], after=[K.dve.last()]))
            gain(kr[:, 0:CT, :], CT, self.small.k_gain_row, after=kr_marks)
            inverse_rms(sq_[:, :], rq[:, :], QT * H)
            K.dve(V.tensor_scalar, rq[:, :], rq[:, :], MLA_QK ** -0.5, None, ALU.mult)
            n = per * (MLA_NOPE + MLA_V)
            pieces = [K.stream.piece("mla_w_ukv_2", (0,), rows_of(2), np.arange(c * n, (c + 1) * n))
                      for c in range(H // per)]

            def finish_keys(t, last):
                r = rk[:, t * H:(t + 1) * H]
                s = sk[:, t * H:(t + 1) * H]
                K.dve(V.tensor_scalar, s, s, sr[:, t:t + 1], None, ALU.add)
                inverse_rms(s, r, H)
                rb = lambda n: bass.AP(tensor=r.tensor, offset=r.offset,
                                       ap=[[r.ap[0][0], P], [1, H], [0, n]])
                K.dve(V.tensor_tensor, kt[:, t, :, 0:MLA_NOPE], kt[:, t, :, 0:MLA_NOPE], rb(MLA_NOPE),
                      ALU.mult, after=[last])
                kb = kr[:, t, :]
                kbb = bass.AP(tensor=kb.tensor, offset=kb.offset,
                              ap=[[kb.ap[0][0], P], [0, H], [1, MLA_ROPE]])
                K.dve(V.tensor_tensor, kt[:, t, :, MLA_NOPE:], kbb, rb(MLA_ROPE), ALU.mult)

            for t in range(TT):
                for c, (w, ch) in enumerate(pieces):
                    i = K.next_banks()
                    for j in range(2):
                        done = K.mm(K.bank(i), ckv[:, j, t * P:(t + 1) * P], w[:, j, :], j == 0, j == 1,
                                    mark=(j == 1), after=nk)
                    kv = K.bank(i).rearrange("p (h d) -> p h d", h=per)
                    m2 = K.act(S.copy, kt[:, t, per * c:per * (c + 1), 0:MLA_NOPE],
                               kv[:, :, 0:MLA_NOPE], after=[done])
                    q = head_sums(kv[:, :, 0:MLA_NOPE], sk[:, t * H + c * per:t * H + (c + 1) * per],
                              MLA_NOPE, [m2])
                    m1 = K.dve(V.tensor_copy, v[:, t, per * c:per * (c + 1), :], kv[:, :, MLA_NOPE:],
                               after=[q])
                    K.release(i, 1, m1)
                    K.stream.used(ch, done)
                if t < QT:
                    cos = self.c.mla_cos[:, t * half:(t + 1) * half]
                    sin = self.c.mla_sin[:, t * half:(t + 1) * half]
                    x = qt[:, t, :, MLA_NOPE:]
                    gain(x, H, self.small.q_gain_row)
                    rotate(x, H, cos, sin)
                    x = kr[:, CT + t:CT + t + 1, :]
                    gain(x, 1, self.small.k_gain_row)
                    rotate(x, 1, cos, sin)
                if t:
                    finish_keys(t - 1, before)
                before = m2
            finish_keys(TT - 1, before)
            K.barrier()
        with ExitStack() as s1:
            self.heads_attention(s1, kt, v, qt, rq, out)
            K.barrier()
        with ExitStack() as s1:
            yt = K.sb("mla_out_t", [P, KT, SEQ], s1)
            for j in range(KT):
                i = K.next_banks()
                for t in range(QT):
                    done = K.pe(T.transpose, K.bank(i)[:, t * P:(t + 1) * P],
                                out[:, t, j * P:(j + 1) * P], K.ident, mark=True)
                m = K.copy(yt[:, j, :], K.bank(i), after=[done])
                K.release(i, 1, m)
            marks = [K.act.last(), K.dve.last()]
            ytw = yt[:, :, :]
            for d in range(KT):
                w, ch = K.stream.piece("mla_w_out_2", (0,), rows_of(KT), np.arange(d * P, (d + 1) * P))
                i = K.next_banks(2)
                K.pe.wait(*marks)
                for kk in range(KT):
                    done = K.mm(self.pair(i, CTX, TOK), w[:, kk, :], ytw[:, kk, :], kk == 0, kk == KT - 1,
                                mark=(kk == KT - 1))
                K.stream.used(ch, done)
                self.residual(i, done, l, 2, d, with_ctx=False)
            K.barrier()

    def heads_attention(self, st, kt, v, qt, rq, out):
        K, V, S, T = self.K, self.K.nc.vector, self.K.nc.scalar, self.K.nc.tensor
        H = MLA_HEADS
        kf = Ring([Buf(K.sb(f"k_feat{i}", [P, TOK], st)) for i in range(3)])
        qf = Ring([Buf(K.sb(f"q_feat{i}", [P, SEQ], st)) for i in range(3)])
        for b in kf.bufs + qf.bufs:
            b.free = [K.pool(K.nc.gpsimd.memset, b.t[MLA_QK:P, :], 0.0)]
        zeros = b.free
        probs = Ring([Buf(K.sb(f"mla_probs{i}", [P, TOK], st)) for i in range(3)])
        turned = Ring([Buf(K.sb(f"mla_turned{i}", [P, 3 * P], st)) for i in range(6)])
        colr = Ring([Buf(K.sb(f"mla_cols{i}", [P, 4], st)) for i in range(4)])
        K.area = [4, 3, 0]

        def to_features(src, tiles, dst, gain):
            i = K.next_banks()
            for n, t in enumerate(tiles):
                done = K.pe(T.transpose, K.bank(i)[0:MLA_QK, n * P:(n + 1) * P], src(t),
                            K.ident, mark=True)
            out = dst.t[0:MLA_QK, tiles[0] * P:(tiles[-1] + 1) * P]
            m = K.act(S.activation, out, K.bank(i)[0:MLA_QK, 0:len(tiles) * P], ACT.Copy, scale=gain,
                      after=[done] + dst.free)
            K.release(i, 1, m)
            return m

        def prepare(h):
            hd = Names()
            hd.h, hd.k, hd.q = h, kf.take(), qf.take()
            k_of, q_of = (lambda t: kt[:, t, h, :]), (lambda t: qt[:, t, h, :])

            def step(src, tiles, dst, gain):
                def go():
                    hd.ready = to_features(src, tiles, dst, gain)
                return go
            kg, qg = self.small.k_gain_col, self.small.q_gain_col
            return hd, [step(k_of, [0, 1, 2], hd.k, kg), step(k_of, [3, 4, 5], hd.k, kg),
                        step(q_of, [0, 1, 2, 3], hd.q, qg)]

        def scores(hd, t, n):
            u = Names()
            u.h, u.t, u.p, u.c = hd.h, t, probs.take(), colr.take()
            top, bias, total, u.inv = (u.c.t[:, j:j + 1] for j in range(4))
            i = 2 * (n % 2)
            K.claim(i, 2)
            for lo, hi in ((0, BANK), (BANK, TOK)):
                done = K.mm(K.bank(i, 2)[:, lo:hi], hd.q.t[:, t * P:(t + 1) * P], hd.k.t[:, lo:hi], True,
                            True, mark=True, after=[hd.ready] + zeros)
            hd.k.free, hd.q.free = [done], [done]
            logits = K.bank(i, 2)[:, 0:TOK]
            K.dve(V.tensor_reduce, top, logits, AX_X, ALU.max, after=[done] + u.c.free)
            s = rq[:, t * H + u.h:t * H + u.h + 1]
            m = K.dve(V.scalar_tensor_tensor, bias, top, -1.0, s, ALU.mult, ALU.mult)
            e = K.act(S.activation, u.p.t[:, :], logits, ACT.Exp, bias=bias, scale=s, accum_out=total,
                      after=[m] + u.p.free)
            K.release(i, 2, e)
            u.total, u.ready = total, e
            return u

        def turn(u):
            u.parts = []
            for part in range(2):
                i, pt = K.next_banks(), turned.take()
                for b in range(3):
                    kb = 3 * part + b
                    done = K.pe(T.transpose, K.bank(i)[:, b * P:(b + 1) * P],
                                u.p.t[:, kb * P:(kb + 1) * P], K.ident, after=[u.ready], mark=True)
                m = K.copy(pt.t[:, :], K.bank(i)[:, 0:3 * P], after=[done] + pt.free)
                K.release(i, 1, m)
                u.parts.append((pt, m))
            u.p.free = [done]

        def weigh(u):
            K.claim(7)
            for kb in range(TT):
                pt, m = u.parts[kb // 3]
                done = K.mm(K.bank(7)[:, 0:MLA_V], pt.t[:, (kb % 3) * P:(kb % 3 + 1) * P],
                            v[:, kb, u.h, :], kb == 0, kb == TT - 1, mark=(kb % 3 == 2), after=[m])
                if kb % 3 == 2:
                    pt.free = [done]
            K.dve(V.reciprocal, u.inv, u.total, after=[u.ready])
            m = K.dve(V.tensor_scalar, out[:, u.t, u.h * MLA_V:(u.h + 1) * MLA_V],
                      K.bank(7)[:, 0:MLA_V], u.inv, None, ALU.mult, after=[done])
            u.c.free = [m]
            K.release(7, 1, m)

        units = []
        hd, steps = prepare(0)
        for go in steps:
            go()
        for n in range(QT * H + 2):
            h, t = n // QT, n % QT
            if n < QT * H:
                if t == 0:
                    now = hd
                    if h + 1 < H:
                        hd, steps = prepare(h + 1)
                units.append(scores(now, t, n))
                if t and h + 1 < H:
                    steps[t - 1]()
            if n and n - 1 < QT * H:
                turn(units[n - 1])
            if n >= 2:
                weigh(units[n - 2])
        K.area = [0, 8, 0]

    def feed_forward(self, l, with_ctx):
        K, V, S = self.K, self.K.nc.vector, self.K.nc.scalar
        spans = BOTH if with_ctx else LATENT
        lo0 = 0 if with_ctx else CTX
        with ExitStack() as st:
            act = K.sb("ffn_act", [P, FT, TOK if with_ctx else SEQ], st)
            with ExitStack() as s1:
                h = K.sb("h2", [P, KT, TOK], s1)
                with ExitStack() as s2:
                    sq = K.sb("squares2", [P, KT, SEQ], s2), K.sb("squares_ctx", [P, KT, CTX], s2)
                    ready = self.modulate(l, 3, 4, h, sq, with_ctx)
                    K.barrier(pe=False)
                gap = 2
                row = [Buf(K.sb(f"ffn_row{i}", [P, TOK + 2 * gap], s1)) for i in range(2)]
                for r in row:
                    mz = K.pool(K.nc.gpsimd.memset, r.t[:, :], 0.0)
                rows = Ring(row)
                n = TOK + gap - lo0 if with_ctx else SEQ
                base = 0 if with_ctx else CTX + gap
                for f in range(FT):
                    cw = self.small.ffn_w[l][f]
                    w, ch = K.stream.piece("ffn_w_in_2", (l,), rows_of(KT), np.arange(f * P, (f + 1) * P))
                    i, done = self.wide(w, ch, h, spans, after=ready)
                    r = rows.take()
                    if with_ctx:
                        K.act(S.copy, r.t[:, 1:1 + CTX], self.pair(i, 0, CTX), after=[done, mz] + r.free)
                    m = K.act(S.copy, r.t[:, 1 + CTX + gap:1 + TOK + gap], self.pair(i, CTX, TOK),
                              after=[done, mz] + r.free)
                    t = K.bank(i, 2)[:, 0:n]
                    K.dve(V.tensor_scalar, t, r.t[:, base:base + n], cw[:, 0:1], self.small.ffn_b[l][f],
                          ALU.mult, ALU.add, after=[m])
                    for j in (1, 2):
                        m = K.dve(V.scalar_tensor_tensor, t, r.t[:, base + j:base + j + n],
                                  cw[:, j:j + 1], t, ALU.mult, ALU.add)
                    r.free = [m]
                    a = act[:, f, :]
                    if with_ctx:
                        K.act(S.activation, a[:, 0:CTX], t[:, 0:CTX], ACT.Gelu_apprx_tanh, after=[m])
                        g = K.act(S.activation, a[:, CTX:TOK], t[:, CTX + gap:TOK + gap],
                                  ACT.Gelu_apprx_tanh)
                    else:
                        g = K.act(S.activation, a, t, ACT.Gelu_apprx_tanh, after=[m])
                    K.release(i, 2, g)
                    w, ch = K.stream.piece("ffn_w_in_2", (l,), rows_of(KT),
                                           FFN + np.arange(f * P, (f + 1) * P))
                    i, done = self.wide(w, ch, h, spans, after=ready)
                    m = K.dve(V.tensor_tensor, a, self.pair(i, lo0, TOK), a, ALU.mult, after=[done, g])
                    K.release(i, 2, m)
                K.barrier()
            half = FT // 2
            for d in range(KT):
                i = K.next_banks(2)
                for part in range(2):
                    w, ch = K.stream.piece("ffn_w_out_2", (l,), rows_of(half, part * half * P),
                                           np.arange(d * P, (d + 1) * P))
                    for lo, hi in spans:
                        for kk in range(half):
                            kg = part * half + kk
                            done = K.mm(self.pair(i, lo, hi), w[:, kk, :], act[:, kg, lo - lo0:hi - lo0],
                                        kg == 0, kg == FT - 1, mark=(kk == half - 1))
                    K.stream.used(ch, done)
                self.residual(i, done, l, 5, d, with_ctx)
            K.barrier()

    def run(self):
        K, S = self.K, self.K.nc.scalar
        st = ExitStack()
        self.xc = K.sb("context", [P, KT, CTX], st)
        K.act.eng.dma_start(self.xc[:, :, :], self.dram_ctx).then_inc(self.ctx_sem, 16)
        for line in (K.pe, K.dve, K.act):
            line.wait((self.ctx_sem, 32))
        for l in range(DEPTH):
            with ExitStack() as s1:
                if l == 0:
                    self.conformer(l, s1)
                else:
                    self.latent_attention(l, s1)
                K.barrier()
            self.feed_forward(l, l < DEPTH - 1)
        st.close()


class Names:
    pass


def pack_constants():
    common, first = Pack("common"), Pack("first")
    at = {}
    i, j = np.arange(P)[:, None], np.arange(P)[None, :]
    at["ident"] = common.const(np.eye(P))
    at["ones"] = common.const(np.ones((P, P)))
    causal = np.zeros((P, SEQ))
    causal[:, SEQ - P:] = np.where(j <= i, 0.0, NEG)
    at["causal"] = first.const(causal)
    at["before01"] = first.const((i < j) * 1.0)
    at["before_add"] = first.const(np.where(i < j, 0.0, NEG))
    at["from_here"] = first.const((i >= j) * 1.0)

    def partner(dim):
        half = dim // 2
        f = np.arange(P) % dim
        return np.arange(P) + np.where(f < half, half, -half)

    for dim in (64, 32):
        half = dim // 2
        perm = np.zeros((P, P))
        perm[partner(dim), np.arange(P)] = 1.0
        at[f"perm{dim}"] = first.const(perm)
        f = np.arange(P) % dim
        inv = (10000.0 ** (-2.0 * (f % half) / dim)).astype(np.float32)
        at[f"inv{dim}"] = first.const(inv[:, None])
        at[f"sign{dim}"] = first.const(np.where(f < half, -1.0, 1.0)[:, None])
    n = np.arange(N_CMP)[None, None, :]
    t = np.arange(QT)[None, :, None] * P + np.arange(P)[:, None, None]
    seen = n * CMP_STRIDE + CMP_LEN - 1 <= t
    at["cmp_add"] = first.const(np.where(seen, 0.0, NEG).reshape(P, -1))
    at["cmp_keep"] = first.const((seen * 1.0).reshape(P, -1))
    r = np.arange(P) % 32
    at["fox"] = first.const(np.stack([(r == 0) / SCALE, (r == 1) * 1.0, (r == 1) / -SCALE,
                                      (r == 0) * 1.0], 1))
    p = np.arange(P)[:, None]
    feature = np.arange(KT)[None, :] * P + p
    at["c"], at["c_ctx"] = (common.param(n, feature, None) for n in ("c_2", "c_ctx_2"))
    for l in range(DEPTH):
        at["ada_b", l] = common.param("ada_b_2", np.arange(6 * KT)[None, :] * P + p, l)
        at["norm_g", l] = first.param("norm_g", feature, l)
        at["mem_norm", l] = first.param("mem_norm", feature, l)
        at["kv_norm", l] = first.param("kv_norm", p, l)
        at["fox_bias", l] = first.param("fox_bias", p // 32, l)
        pe = (2 * np.arange(CMP_LEN // 2)[None, :] + p // HD) * HD + p % HD
        at["pe_k", l] = first.param("nsa_pe_k", pe, l)
        at["pe_v", l] = first.param("nsa_pe_v", pe, l)
    at["final_norm"] = first.param("final_norm", np.arange(KT)[None, :] * P + p, None)
    second = Pack("second")
    at["le"] = second.const(np.where(i <= j, 0.0, NEG))
    at["ge"] = second.const(np.where(i >= j, 0.0, NEG))
    tok = np.arange(SEQ)
    half = MLA_ROPE // 2
    inv = (10000.0 ** (-np.arange(0, half, 2) / half)).astype(np.float32)
    ang = np.concatenate([(tok // GRID_W).astype(np.float32)[:, None] * inv,
                          (tok % GRID_W).astype(np.float32)[:, None] * inv], 1)
    by_tile = lambda a: a.reshape(QT, P, half).transpose(1, 0, 2).reshape(P, -1)
    at["mla_cos"] = second.const(by_tile(np.cos(ang)))
    at["mla_sin"] = second.const(by_tile(np.sin(ang)))
    at["gate_bias"] = second.param("ab_gate_bias_2",
                                   HEADS * np.array([0, 2, 1, 3])[p // 32] + p % HEADS, 0)
    for c in range(4):
        at["conv_w", c] = second.param("ab_conv_w_2",
                                       np.arange(CONV_WIDTH)[None, :] * CONV_DIM + c * P + p, 0)
    four = np.arange(4)[None, :] * P + p
    for n in ("ab_conv_b_2", "ab_ln_g_2", "ab_ln_b_2", "ab_head_gain_2", "mla_q_norm_2"):
        at[n] = second.param(n, four, 0)
    at["mla_kv_norm_2"] = second.param("mla_kv_norm_2", four[:, 0:2], 0)
    for n in ("mla_q_gain_2", "mla_k_gain_2"):
        at[n] = second.param(n, np.where(p < MLA_NOPE, p, -1), 0)
        at[n, "row"] = second.param(n, MLA_NOPE + np.arange(MLA_ROPE)[None, :] + 0 * p, 0)
    for l in range(DEPTH):
        taps = (np.arange(FT)[None, :, None] * P + p[:, :, None]
                + np.arange(3)[None, None, :] * FFN).reshape(P, -1)
        at["ffn_w", l] = second.param("ffn_conv_w_2", taps, l)
        at["ffn_b", l] = second.param("ffn_conv_b_2", np.arange(FT)[None, :] * P + p, l)
    return common, first, second, at


def name_second(at, second):
    c, s = Names(), Names()
    col = lambda n, w=1, lo=0: second[:, at[n] + lo:at[n] + lo + w]
    c.ml_mask = [col("le", P), col("ge", P)]
    half = MLA_ROPE // 2
    c.mla_cos, c.mla_sin = col("mla_cos", QT * half), col("mla_sin", QT * half)
    s.gate_bias = col("gate_bias")
    s.conv_w = [col(("conv_w", k), CONV_WIDTH) for k in range(4)]
    s.conv_b, s.ln_g, s.ln_b, s.head_gain, s.q_norm = (
        [col(n, 1, k) for k in range(4)]
        for n in ("ab_conv_b_2", "ab_ln_g_2", "ab_ln_b_2", "ab_head_gain_2", "mla_q_norm_2"))
    s.kv_norm2 = [col("mla_kv_norm_2", 1, k) for k in range(2)]
    s.q_gain_col, s.k_gain_col = (col(n)[0:MLA_QK, :] for n in ("mla_q_gain_2", "mla_k_gain_2"))
    s.q_gain_row, s.k_gain_row = (col((n, "row"), MLA_ROPE) for n in ("mla_q_gain_2", "mla_k_gain_2"))
    s.ffn_w = [[col(("ffn_w", l), 3, 3 * f) for f in range(FT)] for l in range(DEPTH)]
    s.ffn_b = [[col(("ffn_b", l), 1, f) for f in range(FT)] for l in range(DEPTH)]
    return c, s


def name_constants(at, common, first):
    c, s = Names(), Names()
    c.causal = first[:, at["causal"]:at["causal"] + SEQ]
    sq = lambda t, n: t[:, at[n]:at[n] + P]
    c.before01, c.before_add, c.from_here = (sq(first, n) for n in ("before01", "before_add", "from_here"))
    c.perm64, c.perm32 = sq(first, "perm64"), sq(first, "perm32")
    col = lambda t, n, w=1: t[:, at[n]:at[n] + w]
    c.inv64, c.inv32, c.sign64, c.sign32 = (col(first, n) for n in ("inv64", "inv32", "sign64", "sign32"))
    c.cmp_add, c.cmp_keep = (col(first, n, QT * N_CMP) for n in ("cmp_add", "cmp_keep"))
    c.fox = col(first, "fox", 4)
    tiles = lambda n: [first[:, at[n] + k:at[n] + k + 1] for k in range(KT)]
    s.norm_g = [tiles(("norm_g", l)) for l in range(DEPTH)]
    s.mem_norm = [tiles(("mem_norm", l)) for l in range(DEPTH)]
    s.kv_norm = [col(first, ("kv_norm", l)) for l in range(DEPTH)]
    s.fox_bias = [col(first, ("fox_bias", l)) for l in range(DEPTH)]
    s.pe = {w: [col(first, ("pe_" + w, l), CMP_LEN // 2) for l in range(DEPTH)] for w in "kv"}
    s.final_norm = tiles("final_norm")
    return c, s


def build(nc):
    common, first, second, at = pack_constants()
    dram = lambda name, shape, dt=F32, kind="ExternalInput": nc.dram_tensor(name, shape, dt, kind=kind).ap()
    with ExitStack() as ctx:
        K = Core(nc, ctx)
        d_common, d_first = dram("common_dram", (P, common.n)), dram("first_dram", (P, first.n))
        d_x, d_mem = dram("x_dram", (P, KT, SEQ)), dram("mem_dram", (P, KT, N_MEM))
        d_pos = dram("positions_dram", (SEQ,), I32)
        d_out = dram("out_dram", (P, KT, SEQ), kind="ExternalOutput")
        K.stream = Stream(nc, K.pe, K.sb, [K.sem(f"weights_in_slot{i}") for i in range(NSLOT)])
        t_common = K.sb("common", [P, common.n])
        K.ident, K.ones = t_common[:, 0:P], t_common[:, P:2 * P]
        K.t_turn = 0
        d_second, d_ctx = dram("second_dram", (P, second.n)), dram("context_dram", (P, KT, CTX))
        x = K.sb("x", [P, KT, SEQ])
        loaded, stored = K.sem("constants_in"), K.sem("output_stored")
        M = Modulation(K, t_common, at)
        with ExitStack() as st:
            t_first = K.sb("first", [P, first.n], st)
            c, small = name_constants(at, t_common, t_first)
            for t, d in ((t_common, d_common), (t_first, d_first), (x, d_x)):
                nc.sync.dma_start(t[:], d).then_inc(loaded, 16)
            for line in (K.pe, K.dve, K.act):
                line.wait((loaded, 48))
            M.start()
            B = FirstBlock(K, c, small)
            B.modulation = M
            B.x, B.dram_mem, B.dram_pos = x, d_mem, d_pos
            B.mem_sem, B.pos_sem, B.consts_loaded = K.sem("mem_in"), K.sem("positions_in"), (loaded, 48)
            B.run()
        with ExitStack() as st:
            t_second = K.sb("second", [P, second.n], st)
            ctx_sem = K.sem("context_in")
            nc.scalar.dma_start(t_second[:], d_second).then_inc(ctx_sem, 16)
            c, small = name_second(at, t_second)
            B = SecondBlock(K, c, small)
            B.mods, B.mods_ready = M.mods, M.mods_ready
            B.x, B.dram_ctx, B.ctx_sem = x, d_ctx, ctx_sem
            B.run()
        d_stream = dram("stream_dram", (len(K.stream.chunks), P, SLOT))
        K.stream.issue(K.sp, d_stream)
        K.sp.wait(*K.all_marks())
        nc.sync.dma_start(d_out, x[:, :, :]).then_inc(stored, 16)
        nc.sync.wait_ge(stored, 16)
    return K.stream, [common, first, second]


def feature_major(a):
    return np.ascontiguousarray(a.reshape(a.shape[0], -1, P).transpose(2, 1, 0))


def kernel(**inputs):
    import concourse.bacc as bacc
    from concourse.bass_utils import run_bass_kernel_spmd

    inputs = {k: np.asarray(v) for k, v in inputs.items()}
    nc = bacc.Bacc("TRN2", target_bir_lowering=False, num_devices=1,
                   dynamic_dma_scratch_size=1024)
    stream, packs = build(nc)
    arrays = {"common_dram": packs[0].fill(inputs), "first_dram": packs[1].fill(inputs),
              "second_dram": packs[2].fill(inputs), "context_dram": feature_major(inputs["ctx_2"][0]),
              "x_dram": feature_major(inputs["x"][0]), "mem_dram": feature_major(inputs["mem"][0]),
              "positions_dram": inputs["positions"][0], "stream_dram": stream.fill(inputs)}
    got = run_bass_kernel_spmd(nc, [arrays], core_ids=[0]).results[0]["out_dram"]
    return np.ascontiguousarray(got.transpose(2, 1, 0)).reshape(1, SEQ, D_MODEL)
```

```python
from contextlib import ExitStack

import numpy as np

import concourse.bass as bass
from concourse import mybir

F32 = mybir.dt.float32
F32R = mybir.dt.float32r
I32 = mybir.dt.int32
ALU = mybir.AluOpType
ACT = mybir.ActivationFunctionType
AX_X = mybir.AxisListType.X
P = 128
BANK = 512
NEG = -1.0e30
LOWEST = -3.0e38
EPS = 1e-6

D_MODEL, SEQ, DEPTH, N_MEM, CTX = 1024, 512, 2, 256, 256
HEADS, HD = 4, 64
BR = HEADS * HD
N_BRANCH = 5
IDX_HEADS, IDX_DIM = 4, 32
KV_LATENT = 128
CMP_LEN, CMP_STRIDE, CMP_HIDDEN = 32, 16, 128
N_CMP = (SEQ - CMP_LEN) // CMP_STRIDE + 1
TOPK = min(256, SEQ // 4)
CONV_DIM, CONV_WIDTH = 512, 31
ML_QK, ML_V = 64, 128
MLA_HEADS, MLA_Q_LORA, MLA_KV_LORA, MLA_NOPE, MLA_ROPE, MLA_V = 16, 512, 256, 64, 32, 64
MLA_QK = MLA_NOPE + MLA_ROPE
GRID_W = 64
FFN = 2816
KT = D_MODEL // P
QT = SEQ // P
TOK = CTX + SEQ
SCALE = HD ** -0.5

IN_LAYOUT = (
    ('dsa_q', BR), ('dsa_ckv', KV_LATENT), ('idx_q', IDX_HEADS * IDX_DIM), ('idx_k', IDX_DIM),
    ('idx_w', IDX_HEADS), ('dsa_z', BR),
    ('fox_q', BR), ('fox_k', BR), ('fox_v', BR), ('fox_f', HEADS), ('fox_z', BR),
    ('sb_q', BR), ('sb_k', BR), ('sb_v', BR), ('sb_z', BR),
    ('nsa_q', BR), ('nsa_kc', HD), ('nsa_vc', HD), ('nsa_ks', HD), ('nsa_vs', HD),
    ('nsa_kw', HD), ('nsa_vw', HD), ('nsa_g', 3 * HEADS), ('nsa_z', BR),
    ('mem_q', BR), ('mem_z', BR), ('merge', N_BRANCH * D_MODEL),
)
COL = {}
_off = 0
for _name, _n in IN_LAYOUT:
    COL[_name] = np.arange(_off, _off + _n)
    _off += _n


class Line:

    def __init__(self, eng, sem, chain):
        self.eng, self.sem, self.n, self.chain, self.seen = eng, sem, 0, chain, {}

    def wait(self, *marks):
        for m in marks:
            if m is not None and self.seen.get(m[0].name, 0) < m[1]:
                self.eng.wait_ge(m[0], m[1])
                self.seen[m[0].name] = m[1]

    def last(self):
        return (self.sem, self.n) if self.n else None

    def __call__(self, op, *args, after=(), mark=True, **kw):
        self.wait(*after)
        if self.chain:
            self.wait(self.last())
        ins = op(*args, **kw)
        if mark:
            self.n += 1
            ins.then_inc(self.sem, 1)
            return (self.sem, self.n)
        return None


class Buf:

    def __init__(self, t):
        self.t, self.free = t, []


class Ring:
    def __init__(self, bufs):
        self.bufs, self.i = bufs, 0

    def take(self):
        b = self.bufs[self.i % len(self.bufs)]
        self.i += 1
        return b


class Pack:

    def __init__(self, name):
        self.name, self.n, self.parts, self.t = name, 0, [], None

    def add(self, n, what):
        at = self.n
        self.n += n
        self.parts.append((at, n, what))
        return at

    def const(self, a):
        full = np.zeros((P, a.shape[1]), np.float32)
        full[:a.shape[0]] = a
        return self.add(a.shape[1], full)

    def param(self, name, idx, lead=0):
        idx = np.asarray(idx)
        full = np.zeros((P, idx.shape[1]), np.int64)
        full[:idx.shape[0]] = idx
        return self.add(idx.shape[1], (name, lead, full))

    def fill(self, inputs):
        out = np.zeros((P, self.n), np.float32)
        for at, n, what in self.parts:
            if isinstance(what, tuple):
                name, lead, idx = what
                a = inputs[name]
                a = a[lead] if lead is not None else a
                out[:, at:at + n] = np.where(idx < 0, np.float32(1), a.reshape(-1)[idx])
            else:
                out[:, at:at + n] = what
        return out


SLOT = 1024
NRAW = 4
NSPLIT = 3


class Split:

    def __init__(self, high, low):
        self.high, self.low, self.shape = high, low, high.shape

    def __getitem__(self, at):
        return Split(self.high[at], self.low[at])

    def rearrange(self, *args, **kw):
        return Split(self.high.rearrange(*args, **kw), self.low.rearrange(*args, **kw))


class Stream:

    def __init__(self, K, sems, plan):
        self.K, self.sems, self.plan = K, sems, plan
        self.raw = [K.sb(f"weights_loaded{i}", [P, SLOT]) for i in range(NRAW)]
        self.high = [K.sb(f"weights_high{i}", [P, SLOT], None, F32R) for i in range(NSPLIT)]
        self.low = [K.sb(f"weights_low{i}", [P, SLOT], None, F32R) for i in range(NSPLIT)]
        self.chunks = []
        self.last_use = []
        self.raw_free = {}
        self.pieces = []
        self.split_index = {}
        self.split_chunk = []
        self.split_ready = {}
        self.next_split = 0

    def loaded(self, c):
        return (self.sems[c % NRAW], 16 * (c // NRAW + 1))

    def prepare(self, upto):
        K = self.K
        S = K.nc.scalar
        while self.plan and self.next_split <= min(upto, len(self.plan) - 1):
            c = self.next_split
            self.next_split += 1
            size, split = self.plan[c]
            if not split:
                continue
            s = len(self.split_chunk)
            self.split_chunk.append(c)
            self.split_index[c] = s
            free = [self.last_use[self.split_chunk[s - NSPLIT]]] if s >= NSPLIT else []
            assert None not in free
            raw = self.raw[c % NRAW][:, 0:size]
            high, low = self.high[s % NSPLIT][:, 0:size], self.low[s % NSPLIT][:, 0:size]
            m = K.act(S.copy, high, raw, after=free + [self.loaded(c)])
            m = K.pool(K.nc.gpsimd.tensor_tensor, low, raw, high, ALU.subtract, after=free + [m])
            self.split_ready[c] = self.raw_free[c] = m

    def piece(self, name, lead, rows, cols, split=False, ahead=2):
        rows, cols = np.asarray(rows), np.asarray(cols)
        nk, n = rows.shape[0], len(cols)
        size = nk * n
        assert size <= SLOT
        if not self.chunks or self.chunks[-1][0] + size > SLOT or self.chunks[-1][1] != split:
            self.chunks.append([0, split])
            self.last_use.append(None)
        c = len(self.chunks) - 1
        at = self.chunks[c][0]
        self.chunks[c][0] += size
        self.pieces.append((c, at, name, lead, rows, cols))
        self.prepare(c + ahead)
        part = lambda t: t[:, at:at + size].rearrange("p (k n) -> p k n", k=nk)
        if split:
            s = self.split_index.get(c, 0) % NSPLIT
            self.K.pe.wait(self.split_ready.get(c))
            return Split(part(self.high[s]), part(self.low[s])), c
        self.K.pe.wait(self.loaded(c))
        return part(self.raw[c % NRAW]), c

    def used(self, c, mark):
        self.last_use[c] = mark
        if not self.chunks[c][1]:
            self.raw_free[c] = mark

    def issue(self, sp, dram):
        for c, (size, _) in enumerate(self.chunks):
            if c >= NRAW and c - NRAW in self.raw_free:
                sp.wait(self.raw_free[c - NRAW])
            sp.eng.dma_start(self.raw[c % NRAW][:, 0:size], dram[c, :, 0:size]).then_inc(
                self.sems[c % NRAW], 16)

    def fill(self, inputs):
        out = np.zeros((len(self.chunks), P, SLOT), np.float32)
        for c, at, name, lead, rows, cols in self.pieces:
            a = inputs[name]
            for i in lead:
                a = a[i]
            out[c, :, at:at + rows.shape[0] * len(cols)] = (
                a[rows][:, :, cols].transpose(1, 0, 2).reshape(P, -1))
        return out


class Tall:

    def __init__(self, stream, name, lead, nk, cols, split):
        self.stream, self.half = stream, (nk + 1) // 2
        whole = nk * len(cols) <= SLOT
        cuts = ((0, nk),) if whole else ((0, self.half), (self.half, nk))
        self.half = nk if whole else self.half
        self.parts = [stream.piece(name, lead, rows_of(hi - lo, lo * P), cols, split,
                                   ahead=1 if lo else 2) for lo, hi in cuts]

    def __call__(self, k):
        return self.parts[k // self.half][0][:, k % self.half, :]

    def used(self, mark):
        for _, c in self.parts:
            self.stream.used(c, mark)


def rows_of(n, first=0):
    return first + np.arange(n * P).reshape(n, P)


class Core:

    def __init__(self, nc, ctx):
        self.nc, self.ctx = nc, ctx
        sem = lambda name: ctx.enter_context(nc.semaphore(name))
        self.sem = sem
        self.pe = Line(nc.tensor, sem("tensor_steps"), False)
        self.dve = Line(nc.vector, sem("vector_steps"), True)
        self.act = Line(nc.scalar, sem("scalar_steps"), True)
        self.pool = Line(nc.gpsimd, sem("gpsimd_steps"), True)
        self.sp = Line(nc.sync, sem("sync_steps"), False)
        self.psum = ctx.enter_context(nc.psum_tensor("psum", [P, 8 * BANK], F32))
        self.banks = [Buf(self.psum[:, i * BANK:(i + 1) * BANK]) for i in range(8)]
        self.area = [0, 8, 0]
        self.spare = [6, 2, 0]
        self.later = []
        self.flip = 0
        self.used = {}
        self.fence = ()

    def sb(self, name, shape, stack=None, dt=F32):
        self.used[name] = self.used.get(name, 0) + 1
        if self.used[name] > 1:
            name = f"{name}_{self.used[name]}"
        return (stack or self.ctx).enter_context(self.nc.sbuf_tensor(name, shape, dt))

    def all_marks(self):
        return [m for m in (x.last() for x in (self.pe, self.dve, self.act, self.pool)) if m]

    def barrier(self, pe=True):
        marks = self.all_marks()
        for line in (self.pe, self.dve, self.act, self.pool)[0 if pe else 1:]:
            line.wait(*marks)
        self.fence = tuple(marks)

    def next_banks(self, n=1):
        first, count, at = self.area
        if at + n > count:
            at = 0
        self.area[2] = at + n
        return self.claim(first + at, n)

    def fill(self, n=1):
        for _ in range(min(n, len(self.later))):
            self.area, self.spare = self.spare, self.area
            self.later.pop(0)()
            self.area, self.spare = self.spare, self.area

    def claim(self, i, n=1):
        for b in self.banks[i:i + n]:
            self.pe.wait(*b.free)
        return i

    def bank(self, i, n=1):
        return self.psum[:, i * BANK:(i + n) * BANK]

    def release(self, i, n, *marks):
        for b in self.banks[i:i + n]:
            b.free = list(marks)

    def mm(self, out, lhsT, rhs, start, stop, mark=False, after=()):
        if not isinstance(lhsT, Split):
            return self.pe(self.nc.tensor.matmul, out, lhsT, rhs, start=start, stop=stop, mark=mark,
                           after=after)
        products = ((lhsT.high, rhs.high), (lhsT.high, rhs.low), (lhsT.low, rhs.high))
        for n, (a, b) in enumerate(products):
            done = self.pe(self.nc.tensor.matmul, out, a, b, start=start and n == 0,
                           stop=stop and n == 2, mark=mark and n == 2, after=after)
        return done

    def copy(self, out, in_, after=(), engine=None):
        if engine is None:
            self.flip += 1
            engine = self.act if self.flip % 2 else self.dve
        if engine is self.act:
            return self.act(self.nc.scalar.copy, out, in_, after=after)
        return self.dve(self.nc.vector.tensor_copy, out, in_, after=after)

    def split(self, out, x, after=()):
        m = self.act(self.nc.scalar.copy, out.high, x, after=after)
        return self.dve(self.nc.vector.tensor_tensor, out.low, x, out.high, ALU.subtract,
                        after=[m] + list(after))

    def project(self, w, chunk, m, x, spans, after=(), each=None):
        i = self.next_banks(len(spans))
        self.pe.wait(*after)
        nk = w.shape[1]
        for s, (lo, hi) in enumerate(spans):
            for k in range(nk):
                done = self.mm(self.bank(i + s)[0:m, 0:hi - lo], w[:, k, :], x[:, k, lo:hi],
                               k == 0, k == nk - 1, mark=(k == nk - 1),
                               after=[each[k]] if each else ())
        if chunk is not None:
            self.stream.used(chunk, done)
        return i, done

    def rsqrt_small(self, out, t, tmp, after=()):
        V, S = self.nc.vector, self.nc.scalar
        m = self.act(S.activation, tmp, t, ACT.Ln, after=after)
        m = self.act(S.activation, out, tmp, ACT.Exp, scale=-0.5)
        self.dve(V.tensor_tensor, tmp, out, out, ALU.mult, after=[m])
        self.dve(V.scalar_tensor_tensor, tmp, tmp, -0.5, t, ALU.mult, ALU.mult)
        return self.dve(V.scalar_tensor_tensor, out, tmp, 1.5, out, ALU.add, ALU.mult)

    def rms_features(self, x, nk, lo, hi, gain, out, sq, dim, shift=None, after=(), func=ACT.Identity,
                     rounded=None):
        n = Norm(self, x, nk, lo, hi, gain, out, sq, dim, shift, func, rounded)
        n.squares(after)
        n.sums()
        self.fill()
        n.inverse()
        return n.apply()


class Norm:

    def __init__(self, K, x, nk, lo, hi, gain, out, sq, dim, shift=None, func=ACT.Identity,
                 rounded=None):
        self.rounded = rounded
        self.K, self.x, self.nk, self.lo, self.hi, self.gain = K, x, nk, lo, hi, gain
        self.out, self.sq, self.dim, self.shift, self.func = out, sq, dim, shift, func
        self.n = hi - lo

    def squares(self, after=()):
        K, V, S = self.K, self.K.nc.vector, self.K.nc.scalar
        made = [K.act.last(), K.dve.last()] + list(after)
        self.squared = []
        for k in range(self.nk):
            s, x = self.sq[:, k, 0:self.n], self.x[:, k, self.lo:self.hi]
            if k % 2:
                m = K.dve(V.tensor_tensor, s, x, x, ALU.mult, after=made)
            else:
                m = K.act(S.activation, s, x, ACT.Square, after=made)
            self.squared.append(m)

    def sums(self):
        K = self.K
        nb = (self.n + BANK - 1) // BANK
        self.i, self.nb = K.next_banks(nb), nb
        for lo in range(0, self.n, BANK):
            hi = min(lo + BANK, self.n)
            for k in range(self.nk):
                self.summed = K.mm(K.bank(self.i, nb)[:, lo:hi], K.ones, self.sq[:, k, lo:hi], k == 0,
                                   k == self.nk - 1, mark=(k == self.nk - 1),
                                   after=[self.squared[k]])

    def inverse(self):
        self.logarithms()
        self.exponentials()
        self.newton()

    def logarithms(self):
        K, V, S = self.K, self.K.nc.vector, self.K.nc.scalar
        t, self.row = self.sq[:, 0, 0:self.n], self.sq[:, 1, 0:self.n]
        r = self.row
        m = K.dve(V.tensor_scalar, t, K.bank(self.i, self.nb)[:, 0:self.n], 1.0 / self.dim, EPS,
                  ALU.mult, ALU.add, after=[self.summed])
        K.release(self.i, self.nb, m)
        K.act(S.activation, r, t, ACT.Ln, after=[m])

    def exponentials(self):
        self.guess = self.K.act(self.K.nc.scalar.activation, self.row, self.row, ACT.Exp, scale=-0.5)

    def newton(self):
        K, V = self.K, self.K.nc.vector
        t, r = self.sq[:, 0, 0:self.n], self.row
        K.dve(V.tensor_tensor, t, t, r, ALU.mult, after=[self.guess])
        K.dve(V.scalar_tensor_tensor, t, t, -0.5, r, ALU.mult, ALU.mult)
        K.dve(V.scalar_tensor_tensor, r, t, 1.5, r, ALU.add, ALU.mult)

    def apply(self):
        K, V, S = self.K, self.K.nc.vector, self.K.nc.scalar
        marks = []
        for k in range(self.nk):
            split = isinstance(self.out, Split)
            if split:
                part = self.out[:, k, self.lo:self.hi]
                r = self.rounded.take()
                o = r.t[:, 0:self.n]
                K.dve.wait(*r.free)
            else:
                o = self.out[:, k, self.lo:self.hi]
            m = K.dve(V.scalar_tensor_tensor, o, self.x[:, k, self.lo:self.hi], self.gain(k), self.row,
                      ALU.mult, ALU.mult)
            if self.shift is not None:
                m = K.act(S.activation, o, o, self.func, bias=self.shift(k), after=[m])
            if split:
                m = K.act(S.copy, part.high, o, after=[m])
                m = K.dve(V.tensor_tensor, part.low, o, part.high, ALU.subtract, after=[m])
                r.free = [m]
            marks.append(m)
        return marks




def softmax_attention(K, units, scratch, o_bank=5):
    V, S, T = K.nc.vector, K.nc.scalar, K.nc.tensor

    def start(u):
        u.p = scratch.probs.take()
        u.c = scratch.cols.take()

    def logits(u, h):
        i = h % 2
        K.claim(i)
        done = u.logits(h, K.bank(i)[:, 0:u.keys])
        m = K.dve(V.tensor_tensor_reduce, u.p.t[:, h, 0:u.keys], K.bank(i)[:, 0:u.keys], u.mask,
                  1.0, LOWEST, ALU.add, ALU.max, u.c.t[:, h:h + 1], after=[done] + u.p.free + u.c.free)
        K.release(i, 1, m)

    def exponentials(u):
        top, bias, total = (u.c.t[:, 4 * j:4 * j + 4] for j in range(3))
        m = K.dve(V.tensor_scalar, bias[:, 0:u.heads], top[:, 0:u.heads], -SCALE, None, ALU.mult)
        for h in range(u.heads):
            e = K.act(S.activation, u.p.t[:, h, 0:u.keys], u.p.t[:, h, 0:u.keys], ACT.Exp,
                      bias=bias[:, h:h + 1], scale=SCALE, after=[m],
                      accum_out=None if u.keep is not None else total[:, h:h + 1])
        if u.keep is not None:
            for h in range(u.heads):
                e = K.dve(V.tensor_tensor_reduce, u.p.t[:, h, 0:u.keys], u.p.t[:, h, 0:u.keys], u.keep,
                          1.0, 0.0, ALU.mult, ALU.add, total[:, h:h + 1], after=[e])
            K.dve(V.tensor_scalar, total[:, 0:u.heads], total[:, 0:u.heads], 1e-30, None, ALU.max)
        u.inv = u.c.t[:, 12:12 + u.heads]
        K.dve(V.reciprocal, u.inv, total[:, 0:u.heads], after=[e])
        u.ready = e

    def turned(u, h):
        nb = (u.keys + P - 1) // P
        w = min(P, u.keys)
        i = 2 + K.t_turn % 3
        K.t_turn += 1
        K.claim(i)
        pt = scratch.turned.take()
        for b in range(nb):
            done = K.pe(T.transpose, K.bank(i)[0:w, b * P:(b + 1) * P], u.p.t[:, h, b * P:b * P + w],
                        K.ident, after=[u.ready], mark=(b == nb - 1))
        if h == u.heads - 1:
            u.p.free = [done]
        m = K.copy(pt.t[0:w, 0:nb * P], K.bank(i)[0:w, 0:nb * P], after=[done] + pt.free)
        K.release(i, 1, m)
        return pt, m, nb, w

    def weigh(u, h, pt, copied, nb, w):
        if h == 0:
            K.claim(o_bank)
        for b in range(nb):
            done = K.mm(K.bank(o_bank)[:, h * HD:(h + 1) * HD], pt.t[0:w, b * P:(b + 1) * P],
                        u.value(h, b), b == 0, b == nb - 1, mark=(b == nb - 1), after=[copied])
        pt.free = [done]
        if h == u.heads - 1:
            m = u.finish(u, K.bank(o_bank)[:, 0:u.heads * HD], done)
            u.c.free = [m]
            K.release(o_bank, 1, m)

    def turn(u, h):
        if u:
            u.waiting.append((h,) + turned(u, h))

    def value(u):
        if u:
            weigh(u, *u.waiting.pop(0))

    for i in range(len(units) + 1):
        u = units[i] if i < len(units) else None
        before = units[i - 1] if i else None
        if u:
            u.waiting = []
            start(u)
            logits(u, 0)
            logits(u, 1)
        K.fill()
        turn(before, 0)
        if u:
            logits(u, 2)
        turn(before, 1)
        value(before)
        if u:
            logits(u, 3)
        turn(before, 2)
        value(before)
        if u:
            exponentials(u)
        K.fill()
        turn(before, 3)
        value(before)
        value(before)


class Unit:

    def __init__(self, keys, logits, mask, keep, value, finish, qt):
        self.heads, self.keys, self.logits, self.mask, self.keep = HEADS, keys, logits, mask, keep
        self.value, self.finish, self.qt = value, finish, qt


class FirstBlock:
    def __init__(self, K, consts, small):
        self.K, self.c, self.small = K, consts, small

    def features(self, cols, l, x=None, name="w_in", k=KT, spans=((0, SEQ),), first=0, after=(),
                 each=None):
        w, c = self.K.stream.piece(name, l, rows_of(k, first), cols,
                                     split=x is None or isinstance(x, Split))
        return self.K.project(w, c, len(cols), self.h if x is None else x, spans, after=after, each=each)

    def rope(self, i, done, out, tables, perm):
        K, V = self.K, self.K.nc.vector
        raw, tmp = self.scratch.turned.take(), self.scratch.turned.take()
        cos, sin = tables
        copied = K.copy(raw.t[:, :], K.bank(i), after=[done] + raw.free, engine=K.act)
        j = K.next_banks()
        swapped = K.mm(K.bank(j), perm, raw.t[:, :], True, True, mark=True, after=[copied])
        m = K.dve(V.tensor_tensor, tmp.t[:, :], K.bank(i), cos, ALU.mult, after=[copied] + tmp.free)
        K.release(i, 1, m)
        m = K.dve(V.tensor_tensor, raw.t[:, :], K.bank(j), sin, ALU.mult, after=[swapped])
        K.release(j, 1, m)
        for part, o in self.halves(out):
            m = K.dve(V.tensor_tensor, o, tmp.t[part, :], raw.t[part, :], ALU.add)
        raw.free = tmp.free = [m]
        return m

    def halves(self, out):
        if isinstance(out, tuple):
            return [(slice(HD * g, HD * (g + 1)), o) for g, o in enumerate(out)]
        return [(slice(0, P), out)]

    def padded_queries(self, a):
        K = self.K
        q = a.sub("q", [P, HEADS, SEQ])
        pairs = q.rearrange("p (j g) n -> p j g n", g=2)
        K.pool.wait(*a.after)
        for g in range(2):
            self.zeros = K.pool(K.nc.gpsimd.memset, pairs[HD * (1 - g):HD * (2 - g), :, g, :], 0.0)
        return q

    def pair_of(self, q, j):
        return tuple(q[HD * g:HD * (g + 1), 2 * j + g, :] for g in range(2))

    def plain(self, i, done, out, scale=1.0):
        K, V, S = self.K, self.K.nc.vector, self.K.nc.scalar
        K.flip += 1
        for part, o in self.halves(out):
            x = K.bank(i)[part, :]
            if K.flip % 2:
                m = K.act(S.activation, o, x, ACT.Copy, scale=scale, after=[done])
            else:
                m = K.dve(V.tensor_scalar, o, x, scale, None, ALU.mult, after=[done])
        K.release(i, 1, m)
        return m

    def values(self, cols, l, out, ntile=QT, x=None, name="w_in", k=KT, after=()):
        K = self.K
        n = len(cols)
        w = Tall(K.stream, name, l, k, cols, x is None)
        x = self.h if x is None else x
        per = BANK // n
        nb = (ntile + per - 1) // per
        i = K.next_banks(nb)
        K.pe.wait(*after)
        for t in range(ntile):
            at = t * n
            for kk in range(k):
                done = K.mm(K.bank(i, nb)[:, at:at + n], x[:, kk, t * P:(t + 1) * P], w(kk),
                            kk == 0, kk == k - 1, mark=(t == ntile - 1 and kk == k - 1))
        w.used(done)
        m = K.copy(out, K.bank(i, nb)[:, 0:ntile * n], after=[done])
        K.release(i, nb, m)
        return m

    def gates(self, l):
        K, V, S = self.K, self.K.nc.vector, self.K.nc.scalar
        zs = ["dsa_z", "fox_z", "sb_z", "nsa_z", "mem_z"]
        groups = [np.concatenate([COL[zs[0]], COL[zs[1]]]), np.concatenate([COL[zs[2]], COL[zs[3]]]),
                  np.concatenate([COL[zs[4]], COL["nsa_g"], COL["idx_w"]])]
        per = 2
        for g, cols in enumerate(groups):
            n = len(cols)
            first = K.next_banks(QT)
            for part in range(KT // per):
                w, c = K.stream.piece("w_in", (l,), rows_of(per, part * per * P), cols, split=True)
                for t in range(QT):
                    for k in range(per):
                        kk = part * per + k
                        done = K.mm(K.bank(first + t)[:, 0:n], self.h[:, kk, t * P:(t + 1) * P],
                                    w[:, k, :], kk == 0, kk == KT - 1, mark=(k == per - 1),
                                    after=[self.h_ready[kk]])
                    if part == KT // per - 1:
                        nb = 2 if g < 2 else 1
                        z = self.gate[:, 2 * g:2 * g + nb, t * BR:(t + 1) * BR]
                        zp = K.bank(first + t)[:, 0:nb * BR].rearrange("p (b c) -> p b c", b=nb)
                        m = K.act(S.activation, z, zp, ACT.Tanh, scale=0.5, after=[done])
                        m = K.dve(V.scalar_tensor_tensor, z, z, 1.0, zp, ALU.add, ALU.mult, after=[m])
                        if g == 2:
                            m = K.act(S.copy, self.idx_w[:, t, :],
                                      K.bank(first + t)[:, BR + 3 * HEADS:BR + 3 * HEADS + IDX_HEADS],
                                      after=[m])
                            m = K.act(S.activation, self.mix[:, t, :],
                                      K.bank(first + t)[:, BR:BR + 3 * HEADS], ACT.Tanh, scale=0.5)
                            m = K.dve(V.tensor_scalar, self.mix[:, t, :], self.mix[:, t, :], 1.0, 0.5,
                                      ALU.add, ALU.mult, after=[m])
                        K.release(first + t, 1, m)
                K.stream.used(c, done)
        self.gates_ready = m

    def turn_branch(self, b):
        K, T = self.K, self.K.nc.tensor
        i = K.next_banks(2)
        ready = K.dve.last()
        for j in range(2):
            for t in range(QT):
                done = K.pe(T.transpose, K.bank(i, 2)[:, j * SEQ + t * P:j * SEQ + (t + 1) * P],
                            self.gate[:, b, t * BR + j * P:t * BR + (j + 1) * P], K.ident,
                            after=[ready], mark=True)
        m = K.copy(self.gate[:, b, :], K.bank(i, 2), after=[done])
        K.release(i, 2, m)
        return m

    def finish_plain(self, b):
        def finish(u, o, done):
            K, V = self.K, self.K.nc.vector
            for h in range(HEADS):
                y = self.gate[:, b, u.qt * BR + h * HD:u.qt * BR + (h + 1) * HD]
                m = K.dve(V.scalar_tensor_tensor, y, o[:, h * HD:(h + 1) * HD], u.inv[:, h:h + 1], y,
                          ALU.mult, ALU.mult, after=[done, self.gates_ready])
            return m
        return finish

    def pair_logits(self, q, k, ready, extra=None):
        K = self.K
        ready = list(ready) + [self.zeros]

        def logits_of(qt):
            def logits(h, out):
                n = out.shape[1]
                kt = k[:, h // 2, 0:n] if len(k.shape) == 3 else k[:, 0:n]
                done = K.mm(out, q[:, h, qt * P:(qt + 1) * P], kt, True, extra is None,
                            mark=extra is None, after=ready)
                if extra is not None:
                    a, b = extra
                    done = K.mm(out, a[:, h, qt * P:(qt + 1) * P], b[:, 0:n], False, True, mark=True)
                return done
            return logits
        return logits_of

    def causal(self, qt):
        return self.c.causal[:, (QT - 1 - qt) * P:QT * P]

    def dsa(self, l, a):
        K, V, S = self.K, self.K.nc.vector, self.K.nc.scalar
        D = a.sub
        q, k, v = self.padded_queries(a), D("k", [P, 2, SEQ]), D("v", [P, QT, BR])
        c_kv, c_n = D("c_kv", [P, 1, SEQ]), D("c_n", [P, 1, SEQ])
        qi, ki = D("q_idx", [P, SEQ]), D("k_idx", [P, SEQ])
        work = D("work", [P, 2, SEQ])
        rel, score = work[:, 0, :], work[:, 1, :]
        drop = [None] + [D(f"drop{t}", [P, (t + 1) * P]) for t in range(1, QT)]
        i, done = self.features(COL["dsa_ckv"], (l,), after=a.after)
        m = self.plain(i, done, c_kv[:, 0, :])
        K.dve.wait(m)
        n = K.rms_features(c_kv, 1, 0, SEQ, lambda kk: self.small.kv_norm[l], c_n, work, KV_LATENT,
                           after=[m])
        for j in range(2):
            i, done = self.features(COL["dsa_q"][j * P:(j + 1) * P], (l,))
            self.rope(i, done, self.pair_of(q, j), self.rope64, self.c.perm64)
        i, done = self.features(COL["idx_q"], (l,))
        self.rope(i, done, qi[:, :], self.rope32, self.c.perm32)
        i, done = self.features(np.tile(COL["idx_k"], IDX_HEADS), (l,))
        ready_idx = self.rope(i, done, ki[:, :], self.rope32, self.c.perm32)
        for j in range(2):
            i, done = self.features(np.arange(j * P, (j + 1) * P), (l,), x=c_n, name="w_uk", k=1,
                                    after=n)
            ready = self.rope(i, done, k[:, j, :], self.rope64, self.c.perm64)
        w, c = K.stream.piece("w_uv", (l,), rows_of(1), np.arange(BR))
        i = K.next_banks(2)
        for t in range(QT):
            done = K.mm(K.bank(i, 2)[:, t * BR:(t + 1) * BR], c_n[:, 0, t * P:(t + 1) * P], w[:, 0, :],
                        True, True, mark=True)
        K.stream.used(c, done)
        mv = K.copy(v[:, :, :].rearrange("p t c -> p (t c)"), K.bank(i, 2), after=[done])
        K.release(i, 2, mv)
        scale = IDX_DIM ** -0.5 * IDX_HEADS ** -0.5
        for t in range(1, QT):
            n = (t + 1) * P
            for h in range(IDX_HEADS):
                i = K.next_banks()
                done = K.mm(K.bank(i)[:, 0:n], qi[32 * h:32 * h + 32, t * P:(t + 1) * P],
                            ki[32 * h:32 * h + 32, 0:n], True, True, mark=True, after=[ready_idx])
                m = K.act(S.activation, rel[:, 0:n], K.bank(i)[:, 0:n], ACT.Relu,
                          after=[done, K.dve.last()])
                K.release(i, 1, m)
                wi = self.idx_w[:, t, h:h + 1]
                if h == 0:
                    K.dve(V.tensor_scalar, score[:, 0:n], rel[:, 0:n], wi, None, ALU.mult,
                          after=[m, self.gates_ready])
                else:
                    K.dve(V.scalar_tensor_tensor, score[:, 0:n], rel[:, 0:n], wi, score[:, 0:n],
                          ALU.mult, ALU.add, after=[m])
            K.dve(V.scalar_tensor_tensor, score[:, 0:n], score[:, 0:n], scale, self.causal(t),
                  ALU.mult, ALU.add)
            for r in range(TOPK // 8):
                if r % 3 == 2:
                    K.fill()
                K.dve(V.max, self.top8[:, :], score[:, 0:n])
                K.dve(V.match_replace, score[:, 0:n], self.top8[:, :], score[:, 0:n], LOWEST)
            K.dve(V.tensor_scalar, drop[t][:, :], score[:, 0:n], LOWEST, NEG, ALU.is_gt, ALU.mult)
        logits = self.pair_logits(q, k, [ready])
        units = [Unit((t + 1) * P, logits(t), self.causal(0) if t == 0 else drop[t][:, :], None,
                      lambda h, b: v[:, b, h * HD:(h + 1) * HD], self.finish_plain(0), t)
                 for t in range(QT)]
        K.pe.wait(mv)
        softmax_attention(K, units, self.scratch)

    def log_sigmoid(self, x, e, out, width=None, after=()):
        K, V, S = self.K, self.K.nc.vector, self.K.nc.scalar
        m = K.dve(V.scalar_tensor_tensor, e, x, -1.0, x, ALU.mult, ALU.min, after=after)
        m = K.act(S.activation, e, e, ACT.Exp, after=[m])
        m = K.act(S.activation, e, e, ACT.Ln, bias=1.0)
        return K.dve(V.scalar_tensor_tensor, out, x, 0.0, e, ALU.min, ALU.subtract, after=[m])

    def fox(self, l, a):
        K, V = self.K, self.K.nc.vector
        D = a.sub
        q, k, v = self.padded_queries(a), D("k", [P, 2, SEQ]), D("v", [P, QT, BR])
        f, g = D("f", [P, SEQ]), D("g", [P, SEQ])
        fa, fb = D("decay_q", [P, HEADS, SEQ]), D("decay_k", [P, SEQ])
        i, done = self.features(np.repeat(COL["fox_f"], 32), (l,), after=a.after)
        m = K.dve(V.tensor_scalar, f[:, :], K.bank(i), self.small.fox_bias[l], None, ALU.add,
                  after=[done])
        K.release(i, 1, m)
        self.log_sigmoid(f[:, :], g[:, :], f[:, :])
        one = K.ones[:, 0:1]
        ones_row = bass.AP(tensor=one.tensor, offset=one.offset, ap=[[one.ap[0][0], P], [0, SEQ]])
        K.dve(V.tensor_tensor_scan, g[:, :], ones_row, f[:, :], 0.0, ALU.mult, ALU.add)
        for h in range(HEADS):
            K.dve(V.tensor_scalar, fa[:, h, :], g[:, :], self.c.fox[:, 2 * h:2 * h + 1],
                  self.c.fox[:, 2 * h + 1:2 * h + 2], ALU.mult, ALU.add)
        at = 2 * HEADS
        mf = K.dve(V.tensor_scalar, fb[:, :], g[:, :], self.c.fox[:, at:at + 1],
                   self.c.fox[:, at + 1:at + 2], ALU.mult, ALU.add)
        marks = [mf]
        for j in range(2):
            for name, dst in (("fox_q", self.pair_of(q, j)), ("fox_k", k[:, j, :])):
                i, done = self.features(COL[name][j * P:(j + 1) * P], (l,))
                marks.append(self.plain(i, done, dst))
        marks.append(self.values(COL["fox_v"], (l,), v[:, :, :].rearrange("p t c -> p (t c)")))
        logits = self.pair_logits(q, k, marks, extra=(fa, fb))
        units = [Unit((t + 1) * P, logits(t), self.causal(t), None,
                      lambda h, b: v[:, b, h * HD:(h + 1) * HD], self.finish_plain(1), t)
                 for t in range(QT)]
        softmax_attention(K, units, self.scratch)

    def sb_attention(self, l, a):
        K, V, S = self.K, self.K.nc.vector, self.K.nc.scalar
        D = a.sub
        q, k, v = self.padded_queries(a), D("k", [P, 2, SEQ]), D("v", [P, QT, BR])
        lk = [D(f"log_keep{b}", [P, SEQ - b * P]) for b in range(QT)]
        wt = [D(f"weight{b}", [P, SEQ - b * P]) for b in range(QT)]
        marks = [self.zeros]
        for j in range(2):
            i, done = self.features(COL["sb_q"][j * P:(j + 1) * P], (l,), after=a.after)
            marks.append(self.plain(i, done, self.pair_of(q, j), scale=SCALE))
            i, done = self.features(COL["sb_k"][j * P:(j + 1) * P], (l,))
            marks.append(self.plain(i, done, k[:, j, :]))
        marks.append(self.values(COL["sb_v"], (l,), v[:, :, :].rearrange("p t c -> p (t c)")))
        read = []
        for h in range(HEADS):
            j = h // 2
            blocks = []
            for b in range(QT):
                n = SEQ - b * P
                i = K.next_banks()
                done = K.mm(K.bank(i)[:, 0:n], k[:, j, b * P:(b + 1) * P],
                            q[:, h, b * P:SEQ], True, True, mark=True, after=marks)
                m = K.dve(V.tensor_scalar, lk[b][:, :], K.bank(i)[:, 0:n], -1.0, None, ALU.mult,
                          after=[done] + read)
                K.release(i, 1, m)
                blocks.append(K.dve(V.scalar_tensor_tensor, wt[b][:, :], lk[b][:, :], -1.0, lk[b][:, :],
                                    ALU.mult, ALU.min))
            for b in range(QT):
                K.act(S.activation, wt[b][:, :], wt[b][:, :], ACT.Exp, after=[blocks[b]])
            for b in range(QT):
                m = K.act(S.activation, wt[b][:, :], wt[b][:, :], ACT.Ln, bias=1.0)
                m = K.dve(V.scalar_tensor_tensor, lk[b][:, :], lk[b][:, :], 0.0, wt[b][:, :], ALU.min,
                          ALU.subtract, after=[m])
                m = K.dve(V.tensor_tensor, lk[b][:, 0:P], lk[b][:, 0:P], self.c.before01, ALU.mult)
            K.fill()
            for b in range(QT):
                n = SEQ - b * P
                i = K.next_banks()
                bank = K.bank(i)
                K.mm(bank[:, 0:n], k[:, j, b * P:(b + 1) * P], q[:, h, b * P:SEQ],
                     True, False)
                K.mm(bank[:, 0:P], K.ident, self.c.before_add, False, False)
                K.mm(bank[:, 0:n], self.c.from_here, lk[b][:, :], False, b == QT - 1,
                     mark=True, after=[m])
                for b2 in range(b + 1, QT):
                    K.mm(bank[:, (b2 - b) * P:n], K.ones, lk[b2][:, :], False, b2 == QT - 1, mark=True)
                done = K.pe.last()
                w = K.act(S.activation, wt[b][:, :], bank[:, 0:n], ACT.Exp, after=[done, m])
                K.release(i, 1, w)
            K.fill()
            i = K.next_banks()
            for t in range(QT):
                for b in range(t + 1):
                    done = K.mm(K.bank(i)[:, t * HD:(t + 1) * HD], wt[b][:, (t - b) * P:(t - b + 1) * P],
                                v[:, b, h * HD:(h + 1) * HD], b == 0, b == t, mark=(b == t),
                                after=[w])
            read = [done]
            y = self.gate[:, 2, :].rearrange("p (t c) -> p t c", t=QT)[:, :, h * HD:(h + 1) * HD]
            m = K.dve(V.tensor_tensor, y,
                      K.bank(i)[:, 0:QT * HD].rearrange("p (t c) -> p t c", t=QT), y, ALU.mult,
                      after=[done, self.gates_ready])
            K.release(i, 1, m)

    def compress(self, l, a, x, which):
        K, V, S = self.K, self.K.nc.vector, self.K.nc.scalar
        blocks = a.sub("blocks_" + which, [P, CMP_LEN // 2, N_CMP])
        hid = a.sub("hidden_" + which, [P, N_CMP])
        pe_cols = self.small.pe[which][l]
        for g in range(2):
            src = bass.AP(tensor=x.tensor, offset=x[HD * g:HD * g + HD, g:g + 1].offset,
                          ap=[[x.ap[0][0], HD], [2, CMP_LEN // 2], [CMP_STRIDE, N_CMP]])
            p = pe_cols[HD * g:HD * g + HD, :]
            pe_b = bass.AP(tensor=p.tensor, offset=p.offset,
                           ap=[[p.ap[0][0], HD], [1, CMP_LEN // 2], [0, N_CMP]])
            m = K.dve(V.tensor_tensor, blocks[HD * g:HD * g + HD, :, :], src, pe_b, ALU.add,
                      after=[K.act.last()])
        rows = ((2 * np.arange(CMP_LEN // 2)[:, None] + np.arange(P)[None, :] // HD) * HD
                + np.arange(P)[None, :] % HD)
        half = CMP_LEN // 4
        pieces = [K.stream.piece("nsa_wc1_" + which, (l,), rows[lo:lo + half], np.arange(CMP_HIDDEN))
                  for lo in (0, half)]
        i = K.next_banks()
        for j in range(CMP_LEN // 2):
            done = K.mm(K.bank(i)[:, 0:N_CMP], pieces[j // half][0][:, j % half, :], blocks[:, j, :], j == 0,
                        j == CMP_LEN // 2 - 1, mark=(j == CMP_LEN // 2 - 1), after=[m])
        for _, c in pieces:
            K.stream.used(c, done)
        m = K.act(S.activation, hid[:, :], K.bank(i)[:, 0:N_CMP], ACT.Silu, after=[done])
        K.release(i, 1, m)
        return hid, m

    def nsa(self, l, a):
        K, V, S = self.K, self.K.nc.vector, self.K.nc.scalar
        D = a.sub
        q = self.padded_queries(a)
        twice = {n: D(n, [P, SEQ]) for n in ("nsa_kc", "nsa_vc", "nsa_ks", "nsa_kw")}
        v = D("v", [P, QT, 2 * HD])
        kct, vc = D("k_cmp", [P, N_CMP]), D("v_cmp", [N_CMP, HD])
        acc = D("mixed", [P, QT, BR])
        coef = D("coef", [P, HEADS])
        for n in twice:
            i, done = self.features(np.tile(COL[n], 2), (l,), after=a.after)
            if n == "nsa_vc":
                self.plain(i, done, twice[n][:, :])
            else:
                self.rope(i, done, twice[n][:, :], self.rope64, self.c.perm64)
        for j in range(2):
            i, done = self.features(COL["nsa_q"][j * P:(j + 1) * P], (l,))
            ready = self.rope(i, done, self.pair_of(q, j), self.rope64, self.c.perm64)
        mv = self.values(np.concatenate([COL["nsa_vs"], COL["nsa_vw"]]), (l,),
                         v[:, :, :].rearrange("p t c -> p (t c)"))
        hid, m = self.compress(l, a, twice["nsa_kc"][:, :], "k")
        w, c = K.stream.piece("nsa_wc2_k", (l,), rows_of(1), np.tile(np.arange(HD), 2))
        i = K.next_banks()
        done = K.mm(K.bank(i)[:, 0:N_CMP], w[:, 0, :], hid[:, :], True, True, mark=True, after=[m])
        K.stream.used(c, done)
        m1 = K.copy(kct[:, :], K.bank(i)[:, 0:N_CMP], after=[done])
        K.release(i, 1, m1)
        hid, m = self.compress(l, a, twice["nsa_vc"][:, :], "v")
        w, c = K.stream.piece("nsa_wc2_v", (l,), rows_of(1), np.arange(HD))
        i = K.next_banks()
        done = K.mm(K.bank(i)[0:N_CMP, 0:HD], hid[:, :], w[:, 0, :], True, True, mark=True, after=[m])
        K.stream.used(c, done)
        m2 = K.copy(vc[:, :], K.bank(i)[0:N_CMP, 0:HD], after=[done])
        K.release(i, 1, m2)
        ks, kw = twice["nsa_ks"], twice["nsa_kw"]

        def finish(which):
            def end(u, o, done):
                m = K.dve(V.tensor_tensor, coef[:, :], u.inv,
                          self.mix[:, u.qt, which * HEADS:(which + 1) * HEADS], ALU.mult,
                          after=[self.gates_ready])
                for h in range(HEADS):
                    y = acc[:, u.qt, h * HD:(h + 1) * HD]
                    oh, ch = o[:, h * HD:(h + 1) * HD], coef[:, h:h + 1]
                    if which == 0:
                        m = K.dve(V.tensor_scalar, y, oh, ch, None, ALU.mult, after=[done])
                    else:
                        m = K.dve(V.scalar_tensor_tensor, y, oh, ch, y, ALU.mult, ALU.add,
                                  after=[done])
                if which == 2:
                    z = self.gate[:, 3, u.qt * BR:(u.qt + 1) * BR]
                    K.dve(V.tensor_tensor, z, acc[:, u.qt, :], z, ALU.mult)
                return m
            return end

        cmp_l = self.pair_logits(q, kct, [ready, m1, m2, mv])
        slc_l = self.pair_logits(q, ks, [ready])
        win_l = self.pair_logits(q, kw, [ready])
        units = []
        for t in range(QT):
            units.append(Unit(N_CMP, cmp_l(t), self.c.cmp_add[:, t * N_CMP:(t + 1) * N_CMP],
                              self.c.cmp_keep[:, t * N_CMP:(t + 1) * N_CMP],
                              lambda h, b: vc[:, :], finish(0), t))
            units.append(Unit((t + 1) * P, slc_l(t), self.causal(t), None,
                              lambda h, b: v[:, b, 0:HD], finish(1), t))
            units.append(Unit((t + 1) * P, win_l(t), self.causal(t), None,
                              lambda h, b: v[:, b, HD:2 * HD], finish(2), t))
        softmax_attention(K, units, self.scratch)

    def memory(self, l, a):
        K = self.K
        D = a.sub
        nt = N_MEM // P
        q, k, v = self.padded_queries(a), D("k", [P, 2, N_MEM]), D("v", [P, nt, BR])
        mem = D("mem_t", [P, KT, N_MEM])
        K.act.eng.dma_start(mem[:, :, :], self.dram_mem).then_inc(self.mem_sem, 16)
        loaded = (self.mem_sem, 16 * (l + 1))
        marks = []
        for j in range(2):
            i, done = self.features(COL["mem_q"][j * P:(j + 1) * P], (l,), after=a.after)
            marks.append(self.plain(i, done, self.pair_of(q, j)))
        K.dve.wait(loaded)
        K.act.wait(loaded)
        n = K.rms_features(mem, KT, 0, N_MEM, lambda kk: self.small.mem_norm[l][kk], mem, self.sq8,
                           D_MODEL)
        for j in range(2):
            i, done = self.features(np.arange(j * P, (j + 1) * P), (l,), x=mem, name="w_mem_kv",
                                    spans=((0, N_MEM),), after=n)
            m = K.copy(k[:, j, :], K.bank(i)[:, 0:N_MEM], after=[done])
            K.release(i, 1, m)
            marks.append(m)
        marks.append(self.values(BR + np.arange(BR), (l,), v[:, :, :].rearrange("p t c -> p (t c)"),
                                 ntile=nt, x=mem, name="w_mem_kv"))
        logits = self.pair_logits(q, k, marks)
        units = [Unit(N_MEM, logits(t), self.c.causal[:, 0:N_MEM], None,
                      lambda h, b: v[:, b, h * HD:(h + 1) * HD], self.finish_plain(4), t)
                 for t in range(QT)]
        softmax_attention(K, units, self.scratch)

    def merge_later(self, l, b, first):
        K, V, S = self.K, self.K.nc.vector, self.K.nc.scalar

        def gate(d, got):
            i, done = self.features(COL["merge"][b * D_MODEL + d * P:b * D_MODEL + (d + 1) * P], (l,))
            s = self.sig.take()
            g = K.act(S.activation, s.t[:, :], K.bank(i), ACT.Tanh, scale=0.5, after=[done] + s.free)
            K.release(i, 1, g)
            got.extend([s, g])

        def product(d, got):
            s, g = got
            y = self.gate[:, b, :].rearrange("p (j n) -> p j n", j=2)
            i, done = self.features(np.arange(d * P, (d + 1) * P), (l, b), x=y, name="w_branch", k=2,
                                    after=[self.turned_at[b]])
            dst = self.merged[:, d, :] if first else s.t[:, :]
            m = K.dve(V.scalar_tensor_tensor, dst, s.t[:, :], 1.0, K.bank(i), ALU.add, ALU.mult,
                      after=[done, g])
            K.release(i, 1, m)
            if not first:
                m = K.dve(V.tensor_tensor, self.merged[:, d, :], self.merged[:, d, :], s.t[:, :],
                          ALU.add)
            s.free = [m]
            self.merged_ready = m

        for d in range(KT):
            got = []
            K.later.append(lambda d=d, got=got: gate(d, got))
            K.later.append(lambda d=d, got=got: product(d, got))

    def merge_out(self, l, st):
        K, V = self.K, self.K.nc.vector
        merged = Split(K.sb("merged_high", [P, KT, SEQ], st, F32R), K.sb("merged_low", [P, KT, SEQ], st, F32R))
        marks = [K.split(merged[:, k, :], self.merged[:, k, :], after=[self.merged_ready])
                 for k in range(KT)]
        K.dve.wait((self.back_sem, 16 * (l + 1)))
        for d in range(KT):
            i, done = self.features(np.arange(d * P, (d + 1) * P), (l,), x=merged, name="w_out",
                                    each=marks)
            r = K.dve(V.scalar_tensor_tensor, self.x[:, d, :], K.bank(i), 0.25, self.x[:, d, :],
                      ALU.mult, ALU.add, after=[done])
            K.release(i, 1, r)
        return r

    def tables(self, st):
        K, V, S = self.K, self.K.nc.vector, self.K.nc.scalar
        pos_i = K.sb("pos_i", [P, SEQ], st, I32)
        pos, ang, turn, red = (K.sb(n, [P, SEQ], st) for n in ("pos", "angle", "turns", "reduced"))
        K.sp.eng.dma_start(pos_i[:, :], self.dram_pos.partition_broadcast(P)).then_inc(self.pos_sem, 16)
        K.dve(V.tensor_copy, pos[:, :], pos_i[:, :], after=[(self.pos_sem, 16), self.consts_loaded])
        two_pi = 2.0 * np.pi
        c1 = 6.28125
        c2 = float(np.float32(np.round((two_pi - c1) * 2.0 ** 20) / 2.0 ** 20))
        c3 = float(np.float32(two_pi - c1 - c2))
        magic = 1.5 * 2.0 ** 23
        for (cos, sin), inv, sign in ((self.rope64, self.c.inv64, self.c.sign64),
                                      (self.rope32, self.c.inv32, self.c.sign32)):
            K.dve(V.tensor_scalar, ang[:, :], pos[:, :], inv, None, ALU.mult,
                  after=[K.act.last()])
            K.dve(V.tensor_scalar, turn[:, :], ang[:, :], float(1.0 / two_pi), magic, ALU.mult, ALU.add)
            K.dve(V.tensor_scalar, turn[:, :], turn[:, :], magic, None, ALU.subtract)
            for part, src in ((c1, ang), (c2, red), (c3, red)):
                K.dve(V.scalar_tensor_tensor, red[:, :], turn[:, :], -part, src[:, :], ALU.mult, ALU.add)
            pi = float(np.nextafter(np.float32(np.pi), np.float32(0)))
            m = K.dve(V.tensor_scalar, red[:, :], red[:, :], pi, -pi, ALU.min, ALU.max)
            m = K.act(S.activation, sin[:, :], red[:, :], ACT.Sin, after=[m])
            K.dve(V.tensor_scalar, sin[:, :], sin[:, :], sign, None, ALU.mult, after=[m])
            K.dve(V.scalar_tensor_tensor, red[:, :], red[:, :], -1.0, red[:, :], ALU.mult, ALU.min)
            m = K.dve(V.tensor_scalar, red[:, :], red[:, :], float(np.pi / 2), None, ALU.add)
            m = K.act(S.activation, cos[:, :], red[:, :], ACT.Sin, after=[m])
        K.dve.wait(m)

    def run(self):
        K, nc = self.K, self.K.nc
        V = nc.vector
        outer = ExitStack()
        cos64, sin64, cos32, sin32 = (K.sb(n, [P, SEQ], outer) for n in ("cos64", "sin64", "cos32", "sin32"))
        self.rope64, self.rope32 = (cos64[:, :], sin64[:, :]), (cos32[:, :], sin32[:, :])
        st = ExitStack()
        self.tables(st)
        K.barrier()
        st.close()
        for l in range(DEPTH):
            with ExitStack() as st:
                self.h = Split(K.sb("h_high", [P, KT, SEQ], st, F32R), K.sb("h_low", [P, KT, SEQ], st, F32R))
                self.gate = K.sb("gate", [P, N_BRANCH, QT * BR], st)
                self.idx_w = K.sb("idx_w", [P, QT, IDX_HEADS], st)
                self.mix = K.sb("mix", [P, QT, 3 * HEADS], st)
                self.merged = K.sb("merged", [P, KT, SEQ], st)
                self.sig = Ring([Buf(K.sb(f"sig{i}", [P, SEQ], st)) for i in range(2)])
                self.turned_at = {}
                self.modulation.queue(l)
                with ExitStack() as s2:
                    self.sq8 = K.sb("squares", [P, KT, SEQ], s2)
                    self.h_ready = K.rms_features(self.x, KT, 0, SEQ, lambda k: self.small.norm_g[l][k],
                                                  self.h, self.sq8, D_MODEL, rounded=self.sig)
                    if l:
                        K.act.wait(self.x_ready)
                        K.act.eng.dma_start(self.dram_x_kept, self.x[:, :, :]).then_inc(self.kept_sem, 16)
                    self.gates(l)
                    K.barrier(pe=False)
                    if l:
                        for line in (K.dve, K.act):
                            line.wait((self.kept_sem, 16))
                with ExitStack() as s2:
                    self.top8 = K.sb("top8", [P, 8], s2)
                    self.scratch = Scratch(K, s2, self.x)
                    arenas = [Arena(K, s2, "even", 30 * 1024), Arena(K, s2, "odd", 33 * 1024)]
                    K.area = [0, 6, 0]
                    for n, (b, branch) in enumerate(((2, self.sb_attention), (0, self.dsa), (1, self.fox), (3, self.nsa))):
                        a = arenas[n % 2]
                        a.open()
                        branch(l, a)
                        self.turned_at[b] = self.turn_branch(b)
                        self.merge_later(l, b, n == 0)
                        a.close()
                    K.barrier()
                with ExitStack() as s2:
                    self.sq8 = K.sb("squares", [P, KT, N_MEM], s2)
                    self.scratch = Scratch(K, s2, self.x)
                    a = Arena(K, s2, "mem", 24 * 1024)
                    a.after = list(K.fence)
                    a.open()
                    self.memory(l, a)
                    self.turned_at[4] = self.turn_branch(4)
                    self.merge_later(l, 4, False)
                    K.act.wait(self.turned_at[4])
                    K.act.eng.dma_start(self.x[:, :, :], self.dram_x_kept if l else self.dram_x).then_inc(
                        self.back_sem, 16)
                    K.fill(len(K.later))
                    K.area = [0, 8, 0]
                    self.x_ready = self.merge_out(l, s2)
                    K.barrier()
        with ExitStack() as st:
            sq = K.sb("squares", [P, KT, SEQ], st)
            K.rms_features(self.x, KT, 0, SEQ, lambda k: self.small.final_norm[k], self.x, sq, D_MODEL)
            K.barrier()
        outer.close()


class Scratch:

    def __init__(self, K, st, x, keys=SEQ, turned=4):
        self.probs = Ring([Buf(x[:, HEADS * i:HEADS * (i + 1), :]) for i in range(2)])
        self.turned = Ring([Buf(K.sb(f"turned{i}", [P, keys], st)) for i in range(turned)])
        self.cols = Ring([Buf(K.sb(f"softmax_cols{i}", [P, 16], st)) for i in range(3)])


class Arena:

    def __init__(self, K, st, name, size):
        self.K, self.t, self.size = K, K.sb("arena_" + name, [P, size // 4], st), size // 4
        self.after = []

    def open(self):
        self.at = 0
        for line in (self.K.dve, self.K.act, self.K.pool, self.K.pe):
            line.wait(*self.after)

    def sub(self, name, shape):
        n = int(np.prod(shape[1:]))
        if not self.at + n <= self.size:
            raise ValueError(name)
        t = self.t[0:shape[0], self.at:self.at + n]
        self.at += n
        if len(shape) == 3:
            return t.rearrange("p (a b) -> p a b", a=shape[1])
        return t

    def close(self):
        self.after = self.K.all_marks()


AB_COL, _o = {}, 0
for _name, _n in (("a", CONV_DIM), ("g", CONV_DIM), ("q", HEADS * ML_QK), ("k", HEADS * ML_QK),
                  ("v", HEADS * ML_V), ("o", HEADS * ML_V), ("gates", 4 * HEADS)):
    AB_COL[_name] = np.arange(_o, _o + _n)
    _o += _n
TT = TOK // P
CT = CTX // P
PAD = (CONV_WIDTH - 1) // 2
FT = FFN // P
BOTH = ((0, CTX), (CTX, TOK))
LATENT = ((CTX, TOK),)


class Modulation:

    def __init__(self, K, common, at):
        self.K = K
        self.silu_c = K.sb("silu_c", [P, KT, 2])
        self.c = [common[:, at[n]:at[n] + KT] for n in ("c", "c_ctx")]
        self.bias = [common[:, at["ada_b", l]:at["ada_b", l] + 6 * KT] for l in range(DEPTH)]
        self.mods = [K.sb(f"mods{l}", [P, 6 * KT, 2]) for l in range(DEPTH)]
        self.rows = Ring([Buf(K.sb("ada_row", [2, BANK]))])
        self.mods_ready = [None] * DEPTH

    def start(self):
        for side, c in enumerate(self.c):
            self.ready = self.K.act(self.K.nc.scalar.activation, self.silu_c[:, :, side], c, ACT.Silu)

    def queue(self, l):
        K, V, S, T = self.K, self.K.nc.vector, self.K.nc.scalar, self.K.nc.tensor
        half, per = SLOT // BANK, BANK // P

        def products(c, got):
            i = K.next_banks()
            for part in range(KT // half):
                w, ch = K.stream.piece("ada_w_2", (l,), rows_of(half, part * half * P),
                                       np.arange(c * BANK, (c + 1) * BANK))
                for k in range(half):
                    kk = part * half + k
                    done = K.mm(K.bank(i)[0:2, :], self.silu_c[:, kk, :], w[:, k, :], kk == 0,
                                kk == KT - 1, mark=(k == half - 1), after=[self.ready])
                K.stream.used(ch, done)
            row = self.rows.take()
            m = K.act(S.copy, row.t[:, :], K.bank(i)[0:2, :], after=[done] + row.free)
            K.release(i, 1, m)
            got.extend([row, m])

        def columns(c, got):
            row, copied = got
            i = K.next_banks()
            for j in range(per):
                done = K.pe(T.transpose, K.bank(i)[:, 2 * j:2 * j + 2], row.t[0:2, j * P:(j + 1) * P],
                            K.ident[0:2, 0:2], after=[copied], mark=True)
            row.free = [done]
            b = self.bias[l][:, c * per:(c + 1) * per]
            bias = bass.AP(tensor=b.tensor, offset=b.offset, ap=[[b.ap[0][0], P], [1, per], [0, 2]])
            out = self.mods[l][:, c * per:(c + 1) * per, :]
            one = 1.0 if c * per // KT in (1, 4) else 0.0
            m = K.dve(V.scalar_tensor_tensor, out,
                      K.bank(i)[:, 0:2 * per].rearrange("p (j s) -> p j s", s=2), one, bias, ALU.add,
                      ALU.add, after=[done])
            K.release(i, 1, m)
            self.mods_ready[l] = m

        before = None
        for c in range(6 * KT // per):
            got = []

            def step(c=c, got=got, before=before):
                if before:
                    columns(*before)
                products(c, got)
            K.later.append(step)
            before = (c, got)
        K.later.append(lambda: columns(*before))


class SecondBlock:

    def __init__(self, K, consts, small):
        self.K, self.c, self.small = K, consts, small

    def wide(self, w, chunk, x, spans, m=P, after=None, keep=None, k0=0, k1=None, last=True):
        K = self.K
        nk = w.shape[1]
        i = K.next_banks(2) if keep is None else keep
        for lo, hi in spans:
            for k in range(nk):
                first, end = k == 0 and k0 == 0, k == nk - 1 and last
                done = K.mm(K.bank(i, 2)[0:m, BANK - CTX + lo:BANK - CTX + hi], w[:, k, :],
                            x[:, k0 + k, lo:hi], first, end, mark=(k == nk - 1),
                            after=[after[lo][k]] if after else ())
        K.stream.used(chunk, done)
        return i, done

    def pair(self, i, lo=0, hi=TOK, m=P):
        return self.K.bank(i, 2)[0:m, BANK - CTX + lo:BANK - CTX + hi]

    def mod(self, l, which, k, side):
        return self.mods[l][:, which * KT + k, side:side + 1]

    def modulate(self, l, shift, scale, h, sq, with_ctx=True, latent_first=False):
        K = self.K
        sides = ([(1, self.xc, 0, CTX, sq[1])] if with_ctx else []) + [(0, self.x, CTX, SEQ, sq[0])]
        if latent_first:
            sides.reverse()
        norms = []
        for side, x, at, n, s in sides:
            norms.append(Norm(K, x, KT, 0, n, lambda k, side=side: self.mod(l, scale, k, side),
                              h[:, :, at:at + n], s, D_MODEL, rounded=self.rounded,
                              shift=lambda k, side=side: self.mod(l, shift, k, side)))
        for n in norms:
            n.squares([self.mods_ready[l]])
        K.fill()
        for n in norms:
            n.sums()
        K.fill()
        for step in (Norm.logarithms, Norm.exponentials, Norm.newton):
            for n in norms:
                step(n)
        return {side[2]: n.apply() for side, n in zip(sides, norms)}

    def residual(self, i, done, l, which, d, with_ctx=True):
        K, V = self.K, self.K.nc.vector
        m = K.dve(V.scalar_tensor_tensor, self.x[:, d, :], self.pair(i, CTX, TOK),
                  self.mod(l, which, d, 0), self.x[:, d, :], ALU.mult, ALU.add, after=[done])
        if with_ctx:
            m = K.dve(V.scalar_tensor_tensor, self.xc[:, d, :], self.pair(i, 0, CTX),
                      self.mod(l, which, d, 1), self.xc[:, d, :], ALU.mult, ALU.add)
        K.release(i, 2, m)
        return m

    def conformer(self, l, st):
        K, V, S, T = self.K, self.K.nc.vector, self.K.nc.scalar, self.K.nc.tensor
        y = K.sb("mixed_features", [P, 2 * HEADS, TOK], st)
        q, k = K.sb("ml_q", [P, HEADS, TOK], st), K.sb("ml_k", [P, 2, TOK], st)
        v = K.sb("ml_v", [P, TT, HEADS, ML_V + 1], st)
        rows_r = K.sb("ml_rows", [64, TOK], st)
        cols = K.sb("ml_cols", [P, TT, P], st)
        with ExitStack() as s1:
            h = Split(K.sb("h2_high", [P, KT, TOK], s1, F32R),
                      K.sb("h2_low", [P, KT, TOK], s1, F32R))
            with ExitStack() as s2:
                sq = K.sb("squares2", [P, KT, SEQ], s2), K.sb("squares_ctx", [P, KT, CTX], s2)
                self.rounded = Ring([Buf(K.sb(f"rounded{i}", [P, SEQ], s2)) for i in range(2)])
                ready = self.modulate(l, 0, 1, h, sq)
                K.barrier(pe=False)
            lat0 = 3 * PAD + CTX
            up = K.sb("padded", [P, 4, CTX + SEQ + 4 * PAD], s1)
            sig = Ring([Buf(K.sb(f"sig2{i}", [P, TOK], s1)) for i in range(2)])
            pre, tmp = K.sb("gate_pre", [P, TOK], s1), K.sb("gate_tmp", [P, TOK], s1)
            stack = K.sb("gate_stack", [P, TOK], s1)
            b, cmx = K.sb("gate_sum", [64, TOK], s1), K.sb("gate_max", [64, TOK], s1)
            one = K.sb("one_row", [64, TOK], s1)
            m3 = K.pool(K.nc.gpsimd.memset, q[:, :, :], 0.0)
            mz = K.pool(K.nc.gpsimd.memset, up[:, :, :], 0.0)
            m1 = K.pool(K.nc.gpsimd.memset, v[:, :, :, ML_V:ML_V + 1], 1.0)
            m2 = K.pool(K.nc.gpsimd.memset, one[:, :], 1.0)
            K.area = [0, 6, 0]

            def projected(name, c):
                w, ch = K.stream.piece("ab_w_in_2", (0,), rows_of(KT),
                                       AB_COL[name][c * P:(c + 1) * P], split=True)
                taps(2)
                return self.wide(w, ch, h, BOTH, after=ready)

            def gated(c):
                i, done = projected("g", c)
                s = sig.take()
                g = K.act(S.activation, s.t[:, :], self.pair(i), ACT.Sigmoid, after=[done] + s.free)
                K.release(i, 2, g)
                i, done = projected("a", c)
                K.dve(V.tensor_tensor, up[:, c, PAD:PAD + CTX], self.pair(i, 0, CTX), s.t[:, 0:CTX],
                      ALU.mult, after=[done, g, mz])
                m = K.dve(V.tensor_tensor, up[:, c, lat0:lat0 + SEQ], self.pair(i, CTX, TOK),
                          s.t[:, CTX:TOK], ALU.mult)
                K.release(i, 2, m)
                s.free = [m]

            tap_steps = []

            def convolve(c):
                cw = self.small.conv_w[c]

                def step(j0, j1):
                    if j0 == 0:
                        K.dve.wait(*K.banks[6].free, *K.banks[7].free)
                    for j in range(j0, j1):
                        for lo, n, at in ((0, CTX, 0), (CTX, SEQ, lat0 - PAD)):
                            acc = self.pair(6, lo, lo + n)
                            if j == 0:
                                K.dve(V.tensor_scalar, acc, up[:, c, at:at + n], cw[:, 0:1],
                                      self.small.conv_b[c], ALU.mult, ALU.add)
                            else:
                                K.dve(V.scalar_tensor_tensor, acc, up[:, c, at + j:at + j + n],
                                      cw[:, j:j + 1], acc, ALU.mult, ALU.add)

                for j in range(0, CONV_WIDTH, 4):
                    tap_steps.append(lambda j=j: step(j, min(j + 4, CONV_WIDTH)))

            def taps(n):
                for _ in range(min(n, len(tap_steps))):
                    tap_steps.pop(0)()

            def convolved(c):
                taps(len(tap_steps))
                m = K.act(S.copy, y[:, c, :], self.pair(6), after=[K.dve.last()])
                K.release(6, 2, m)

            def queries(j):
                i, done = projected("q", j)
                for g in range(2):
                    half = slice(ML_QK * g, ML_QK * (g + 1))
                    m = K.act(S.copy, q[half, 2 * j + g, :], self.pair(i)[half, :], after=[done, m3])
                K.release(i, 2, m)

            def keys(j):
                i, done = projected("k", j)
                m = K.act(S.activation, k[:, j, :], self.pair(i), ACT.Copy, scale=ML_QK ** -0.5,
                          after=[done])
                K.release(i, 2, m)

            def out_gates(c):
                i, done = projected("o", c)
                m = K.act(S.activation, y[:, 4 + c, :], self.pair(i), ACT.Sigmoid, after=[done])
                K.release(i, 2, m)

            g4 = AB_COL["gates"].reshape(4, HEADS)[[0, 2, 1, 3]]
            w, ch = K.stream.piece("ab_w_in_2", (0,), rows_of(KT), np.tile(g4, (1, 32 // HEADS)).ravel(),
                                   split=True)
            i, done = self.wide(w, ch, h, BOTH, after=ready)
            m = K.dve(V.tensor_scalar, pre[:, :], self.pair(i), self.small.gate_bias, None, ALU.add,
                      after=[done])
            K.release(i, 2, m)
            fg, e = pre[64:128, :], tmp[64:128, :]
            K.dve(V.scalar_tensor_tensor, e, fg, -1.0, fg, ALU.mult, ALU.min)
            K.act(S.activation, e, e, ACT.Exp, after=[K.dve.last()])
            m = K.act(S.activation, e, e, ACT.Ln, bias=1.0)
            lf = tmp[0:64, :]
            K.dve(V.scalar_tensor_tensor, lf, fg, 0.0, e, ALU.min, ALU.subtract, after=[m])

            def scans(out, data, op, init):
                K.dve(V.tensor_tensor_scan, out[0:32, :], one[0:32, :], data[0:32, :], init, ALU.mult,
                      op, after=[m2])
                K.dve(V.tensor_tensor_scan, out[32:64, 0:CTX][:, ::-1], one[32:64, 0:CTX],
                      data[32:64, 0:CTX][:, ::-1], init, ALU.mult, op)
                K.dve(V.tensor_tensor_scan, out[32:64, CTX:TOK][:, ::-1], one[32:64, 0:SEQ],
                      data[32:64, CTX:TOK][:, ::-1], out[32:64, 0:1], ALU.mult, op)

            scans(b, lf, ALU.add, 0.0)
            K.dve(V.tensor_tensor, stack[0:64, :], pre[0:64, :], b[:, :], ALU.subtract)
            scans(cmx, stack, ALU.max, LOWEST)
            K.dve(V.tensor_tensor, cmx[:, :], cmx[:, :], b[:, :], ALU.add)
            K.dve(V.tensor_scalar, cmx[:, :], cmx[:, :], 0.0, None, ALU.max)
            rows_ready = K.dve(V.tensor_tensor, rows_r[:, :], b[:, :], cmx[:, :], ALU.subtract)
            m = K.act(S.activation, stack[64:128, :], cmx[:, :], ACT.Exp, scale=-1.0,
                      after=[rows_ready])
            stack_ready = m
            gated(0)
            for c, (step, j0, j1) in enumerate(((queries, 0, 1), (keys, 0, 1), (out_gates, 0, 1))):
                convolve(c)
                step(j0)
                step(j1)
                gated(c + 1)
                convolved(c)
            i = K.next_banks(2)
            for t in range(TT):
                done = K.pe(T.transpose, K.bank(i, 2)[:, t * P:(t + 1) * P],
                            stack[:, t * P:(t + 1) * P], K.ident, after=[stack_ready], mark=True)
            m = K.act(S.copy, cols[:, :, :].rearrange("p t c -> p (t c)"), K.bank(i, 2)[:, 0:TOK],
                      after=[done])
            K.release(i, 2, m)
            cols_ready = m
            convolve(3)
            half = SLOT // BANK
            for c in range(2):
                first = K.next_banks(3)
                for part in range(KT // half):
                    w, ch = K.stream.piece("ab_w_in_2", (0,), rows_of(half, part * half * P),
                                           AB_COL["v"], split=True)
                    taps(1)
                    for t in range(3):
                        tt = 3 * c + t
                        for kk in range(half):
                            kg = part * half + kk
                            done = K.mm(K.bank(first + t), h[:, kg, tt * P:(tt + 1) * P], w[:, kk, :],
                                        kg == 0, kg == KT - 1, mark=(kk == half - 1))
                        if part == KT // half - 1:
                            m = K.act(S.copy, v[:, tt, :, 0:ML_V],
                                      K.bank(first + t).rearrange("p (h d) -> p h d", h=HEADS),
                                      after=[done])
                            K.release(first + t, 1, m)
                    K.stream.used(ch, done)
            out_gates(2)
            out_gates(3)
            convolved(3)
            K.area = [0, 8, 0]
            K.barrier()
        with ExitStack() as s1:
            self.mlstm(l, s1, y, q, k, v, rows_r, cols, cols_ready, rows_ready)
            K.barrier()
        with ExitStack() as s1:
            ys = Split(K.sb("mixed_high", [P, KT, TOK], s1, F32R), K.sb("mixed_low", [P, KT, TOK], s1, F32R))
            marks = [K.split(ys[:, k, :], y[:, k, :]) for k in range(KT)]
            for d in range(KT):
                w, ch = K.stream.piece("ab_w_out_2", (0,), rows_of(KT), np.arange(d * P, (d + 1) * P),
                                       split=True)
                i, done = self.wide(w, ch, ys, BOTH, after={0: marks, CTX: marks})
                self.residual(i, done, l, 2, d)
            K.barrier()

    def mlstm(self, l, st, y, q, k, v, rows_r, cols, cols_ready, rows_ready):
        K, V, S, T = self.K, self.K.nc.vector, self.K.nc.scalar, self.K.nc.tensor
        n = TT * HEADS
        ss, tmp2, rs = (K.sb(f"ml_small{i}", [P, n], st) for i in range(3))
        sqr = K.sb("ml_squares", [P, ML_V], st)
        hs = K.sb("ml_out", [P, TT, HEADS * ML_V], st)
        weights = Ring([Buf(K.sb(f"ml_weights{i}", [P, TT, TOK], st)) for i in range(3)])
        rowdiag = Ring([Buf(K.sb(f"ml_diag{i}", [P, TT, P], st)) for i in range(2)])
        den = K.sb("ml_den", [P, 16], st)
        todo = [(d, h) for h in range(HEADS) for d in range(2)]

        def seen_by(d, kb):
            if d == 0:
                return [(kb + 1, TT)] if kb + 1 < TT else []
            if kb < CT:
                return ([(0, kb)] if kb else []) + [(CT, TT)]
            return [(CT, kb)] if kb > CT else []

        def rows_of_head(d, h):
            r = 32 * d + h
            one = K.ident[0:64, r:r + 1]
            sel = bass.AP(tensor=one.tensor, offset=one.offset, ap=[[one.ap[0][0], 64], [0, P]])
            i = 0
            K.claim(i, 2)
            for lo, hi in BOTH:
                done = K.mm(self.pair(i, lo, hi), sel, rows_r[0:64, lo:hi], True, True, mark=True,
                            after=[rows_ready])
            rd = rowdiag.take()
            mask = self.c.ml_mask[d]
            mask6 = bass.AP(tensor=mask.tensor, offset=mask.offset,
                            ap=[[mask.ap[0][0], P], [0, TT], [1, P]])
            m = K.dve(V.tensor_tensor, rd.t[:, :, :], self.pair(i).rearrange("p (t c) -> p t c", t=TT),
                      mask6, ALU.add, after=[done] + rd.free)
            return i, rd, m

        def exponentials(d, h):
            i, rd, m = rows_of_head(d, h)
            w = weights.take()
            for kb in range(TT):
                u = cols[:, kb, 32 * d + h:32 * d + h + 1]
                K.act(S.activation, w.t[:, kb, kb * P:(kb + 1) * P], rd.t[:, kb, :], ACT.Exp, bias=u,
                      after=[m, cols_ready] + w.free)
                for a, b in seen_by(d, kb):
                    K.act(S.activation, w.t[:, kb, a * P:b * P], self.pair(i, a * P, b * P), ACT.Exp,
                          bias=u)
            e = K.act.last()
            rd.free = [e]
            K.release(i, 2, e)
            return d, h, w, e

        def scores(d, h, w, e):
            for kb in range(TT):
                s = 2 + 2 * (kb % 2)
                K.claim(s, 2)
                ranges = sorted(seen_by(d, kb) + [(kb, kb + 1)])
                joined = [list(ranges[0])]
                for a, b in ranges[1:]:
                    if a == joined[-1][1]:
                        joined[-1][1] = b
                    else:
                        joined.append([a, b])
                for a, b in joined:
                    for lo, hi in BOTH:
                        x0, x1 = max(a * P, lo), min(b * P, hi)
                        if x0 < x1:
                            done = K.mm(self.pair(s, x0, x1), k[:, h // 2, kb * P:(kb + 1) * P],
                                        q[:, h, x0:x1], True, True, mark=True)
                for a, b in joined:
                    m = K.dve(V.tensor_tensor, w.t[:, kb, a * P:b * P], self.pair(s, a * P, b * P),
                              w.t[:, kb, a * P:b * P], ALU.mult, after=[done, e])
                K.release(s, 2, m)
            return d, h, w, m

        def read(d, h, w, ready):
            n = ML_V + 1
            K.claim(6, 2)
            place = lambda t: 6 * BANK + (t // 3) * BANK + (t % 3) * n
            for t in range(TT):
                kbs = [kb for kb in range(TT) if kb == t or any(a <= t < b for a, b in seen_by(d, kb))]
                for kb in kbs:
                    done = K.mm(K.psum[:, place(t):place(t) + n], w.t[:, kb, t * P:(t + 1) * P],
                                v[:, kb, h, :], kb == kbs[0], kb == kbs[-1], mark=(kb == kbs[-1]),
                                after=[ready])
            w.free = [done]
            o2 = K.bank(6, 2).rearrange("p (b c) -> p b c", b=2)
            dcol = o2[:, :, 0:3 * n].rearrange("p b (t c) -> p b t c", t=3)[:, :, :, ML_V]
            d6 = den[:, 0:TT].rearrange("p (b t) -> p b t", b=2)
            K.dve(V.tensor_scalar, d6, dcol, -1.0, None, ALU.mult, after=[done])
            K.dve(V.tensor_tensor, d6, dcol, d6, ALU.max)
            K.dve(V.tensor_tensor, den[:, 0:TT], den[:, 0:TT], cols[:, :, 64 + 32 * d + h], ALU.max)
            K.dve(V.reciprocal, den[:, 0:TT], den[:, 0:TT])
            for t in range(TT):
                o = hs[:, t, h * ML_V:(h + 1) * ML_V]
                num = K.psum[:, place(t):place(t) + ML_V]
                if d == 0:
                    m = K.dve(V.tensor_scalar, o, num, den[:, t:t + 1], None, ALU.mult)
                else:
                    m = K.dve(V.scalar_tensor_tensor, o, num, den[:, t:t + 1], o, ALU.mult, ALU.add)
            K.release(6, 2, m)
            if d == 1:
                for t in range(TT):
                    K.act(S.activation, sqr[:, :], hs[:, t, h * ML_V:(h + 1) * ML_V], ACT.Square,
                          accum_out=ss[:, t * HEADS + h:t * HEADS + h + 1], after=[m])

        def layer_norm():
            K.area = [2, 6, 0]
            i = K.next_banks(2)
            for lo, hi in BOTH:
                for c in range(4):
                    done = K.mm(self.pair(i, lo, hi), K.ones, y[:, c, lo:hi], c == 0, c == 3,
                                mark=(c == 3))
            for c in range(4):
                m = K.dve(V.scalar_tensor_tensor, y[:, c, :], self.pair(i), -1.0 / CONV_DIM, y[:, c, :],
                          ALU.mult, ALU.add, after=[done])
            K.release(i, 2, m)
            K.rms_features(y[:, 0:4, :], 4, 0, TOK, lambda c: self.small.ln_g[c], y[:, 0:4, :], hs4,
                           CONV_DIM, shift=lambda c: self.small.ln_b[c], after=[m], func=ACT.Silu)
            K.area = [0, 8, 0]

        hs4 = hs[:, :, :].rearrange("p t c -> p (t c)").rearrange("p (c n) -> p c n", c=4)
        made, scored = {}, {}
        for n in range(len(todo) + 2):
            if n < len(todo):
                made[n] = exponentials(*todo[n])
            if n == 0:
                layer_norm()
            if 1 <= n <= len(todo):
                scored[n - 1] = scores(*made[n - 1])
            if n >= 2:
                read(*scored[n - 2])
        n = TT * HEADS
        m = K.dve(V.tensor_scalar, ss[:, :], ss[:, :], 1.0 / ML_V, EPS, ALU.mult, ALU.add,
                  after=[K.act.last()])
        K.rsqrt_small(rs[:, :], ss[:, :], tmp2[:, :], after=[m])
        for h in range(HEADS):
            r = rs[:, h:h + 1]
            rsb = bass.AP(tensor=r.tensor, offset=r.offset, ap=[[n, P], [HEADS, TT], [0, ML_V]])
            hv = hs[:, :, h * ML_V:(h + 1) * ML_V]
            m = K.dve(V.tensor_tensor, hv, hv, rsb, ALU.mult)
            i = 2 * (h % 3)
            K.claim(i, 2)
            for t in range(TT):
                done = K.pe(T.transpose, self.pair(i, t * P, (t + 1) * P),
                            hs[:, t, h * ML_V:(h + 1) * ML_V], K.ident, after=[m], mark=True)
            g = K.dve(V.scalar_tensor_tensor, y[:, HEADS + h, :], self.pair(i), self.small.head_gain[h],
                      y[:, HEADS + h, :], ALU.mult, ALU.mult, after=[done])
            K.release(i, 2, g)

    def latent_attention(self, l, st):
        K, V, S, T = self.K, self.K.nc.vector, self.K.nc.scalar, self.K.nc.tensor
        H = MLA_HEADS
        room = K.sb("mla_latents", [P, QT * H * MLA_V], st)
        cq = room[:, 0:4 * SEQ].rearrange("p (j n) -> p j n", j=4)
        ckv = room[:, 4 * SEQ:4 * SEQ + 2 * TOK].rearrange("p (j n) -> p j n", j=2)
        out = room[:, :].rearrange("p (t c) -> p t c", t=QT)
        kr = K.sb("k_rope", [P, TT, MLA_ROPE], st)
        sk, sq_ = K.sb("sum_k", [P, TT * H], st), K.sb("sum_q", [P, QT * H], st)
        rk, rq = K.sb("rstd_k", [P, TT * H], st), K.sb("rstd_q", [P, QT * H], st)
        small = K.sb("mla_small", [P, TT * H], st)
        with ExitStack() as s2:
            h = Split(K.sb("h2_high", [P, KT, TOK], s2, F32R),
                      K.sb("h2_low", [P, KT, TOK], s2, F32R))
            with ExitStack() as s3:
                sq = K.sb("squares2", [P, KT, SEQ], s3), K.sb("squares_ctx", [P, KT, CTX], s3)
                self.rounded = Ring([Buf(K.sb(f"rounded{i}", [P, SEQ], s3)) for i in range(2)])
                ready = self.modulate(l, 0, 1, h, sq, latent_first=True)
                K.barrier(pe=False)
            for j in range(4):
                w, ch = K.stream.piece("mla_w_in_2", (0,), rows_of(KT), np.arange(j * P, (j + 1) * P),
                                       split=True)
                i, done = self.wide(w, ch, h, LATENT, after=ready)
                m = K.copy(cq[:, j, :], self.pair(i, CTX, TOK), after=[done])
                K.release(i, 2, m)
            mq = [K.act.last(), K.dve.last()]
            for j in range(2):
                w, ch = K.stream.piece("mla_w_in_2", (0,), rows_of(KT),
                                       MLA_Q_LORA + np.arange(j * P, (j + 1) * P), split=True)
                i, done = self.wide(w, ch, h, BOTH, after=ready)
                m = K.copy(ckv[:, j, :], self.pair(i), after=[done])
                K.release(i, 2, m)
            w, ch = K.stream.piece("mla_w_in_2", (0,), rows_of(KT),
                                   MLA_Q_LORA + MLA_KV_LORA + np.arange(MLA_ROPE), split=True)
            i = K.next_banks()
            for t in range(TT):
                for kk in range(KT):
                    done = K.mm(K.bank(i)[:, t * MLA_ROPE:(t + 1) * MLA_ROPE],
                                h[:, kk, t * P:(t + 1) * P], w[:, kk, :], kk == 0, kk == KT - 1,
                                mark=(kk == KT - 1))
            K.stream.used(ch, done)
            m = K.act(S.copy, kr[:, :, :].rearrange("p t c -> p (t c)"),
                      K.bank(i)[:, 0:TT * MLA_ROPE], after=[done])
            K.release(i, 1, m)
            K.barrier()
        kt = K.sb("mla_k", [P, TT, H, MLA_QK], st)
        v = K.sb("mla_v", [P, TT, H, MLA_V], st)
        qt = K.sb("mla_q", [P, QT, H, MLA_QK], st)
        with ExitStack() as s1:
            sq = K.sb("squares4", [P, 4, TOK], s1)
            nq = K.rms_features(cq, 4, 0, SEQ, lambda j: self.small.q_norm[j], cq, sq, MLA_Q_LORA)
            nk = K.rms_features(ckv, 2, 0, TOK, lambda j: self.small.kv_norm2[j], ckv, sq, MLA_KV_LORA,
                                after=nq)
            flat = qt[:, :, :, :].rearrange("p t h d -> p t (h d)")
            squares = Ring([Buf(K.sb(f"mla_sq{i}", [P, BANK], s1)) for i in range(3)])
            sr = K.sb("mla_sr", [P, TT], s1)
            half = MLA_ROPE // 2
            t1 = K.sb("rot1", [P, H, half], s1)
            t2 = K.sb("rot2", [P, H, half], s1)
            per = 4

            def head_sums(x, sums, dim, after):
                s = squares.take()
                sv = s.t[:, 0:per * dim].rearrange("p (h d) -> p h d", h=per)
                q = K.act(S.activation, sv, x, ACT.Square, after=after + s.free)
                m = K.dve(V.tensor_reduce, sums, sv, AX_X, ALU.add, after=[q])
                s.free = [m]
                return q

            def inverse_rms(sums, out, n):
                m = K.dve(V.tensor_scalar, sums, sums, 1.0 / MLA_QK, EPS, ALU.mult, ALU.add)
                return K.rsqrt_small(out, sums, small[:, 0:n], after=[m])

            def rotate(x, heads, cos, sin):
                xp = x.rearrange("p h (i two) -> p h i two", two=2)
                even, odd = xp[:, :, :, 0], xp[:, :, :, 1]
                rep = lambda a: bass.AP(tensor=a.tensor, offset=a.offset,
                                        ap=[[a.ap[0][0], P], [0, heads], [1, half]])
                a, b = t1[:, 0:heads, :], t2[:, 0:heads, :]
                K.dve(V.tensor_tensor, a, even, rep(sin), ALU.mult)
                K.dve(V.tensor_tensor, b, odd, rep(sin), ALU.mult)
                K.dve(V.tensor_tensor, even, even, rep(cos), ALU.mult)
                K.dve(V.tensor_tensor, even, even, b, ALU.subtract)
                K.dve(V.tensor_tensor, odd, odd, rep(cos), ALU.mult)
                K.dve(V.tensor_tensor, odd, odd, a, ALU.add)

            def gain(x, heads, g, after=()):
                gb = bass.AP(tensor=g.tensor, offset=g.offset,
                             ap=[[g.ap[0][0], P], [0, heads], [1, MLA_ROPE]])
                K.dve(V.tensor_tensor, x, x, gb, ALU.mult, after=after)

            def angles(t):
                return (self.c.mla_cos[:, t * half:(t + 1) * half],
                        self.c.mla_sin[:, t * half:(t + 1) * half])

            n = per * MLA_QK
            for c in range(H // per):
                w = Tall(K.stream, "mla_w_uq_2", (0,), 4, np.arange(c * n, (c + 1) * n), False)
                for t in range(QT):
                    i = K.next_banks()
                    for j in range(4):
                        done = K.mm(K.bank(i)[:, 0:n], cq[:, j, t * P:(t + 1) * P], w(j), j == 0,
                                    j == 3, mark=(j == 3), after=nq)
                    m = K.copy(flat[:, t, c * n:(c + 1) * n], K.bank(i)[:, 0:n], after=[done],
                               engine=K.dve)
                    q = head_sums(K.bank(i)[:, 0:n].rearrange("p (h d) -> p h d", h=per),
                                  sq_[:, t * H + c * per:t * H + (c + 1) * per], MLA_QK, [m])
                    K.release(i, 1, q)
                    x = qt[:, t, c * per:(c + 1) * per, MLA_NOPE:]
                    gain(x, per, self.small.q_gain_row, after=[q])
                    rotate(x, per, *angles(t))
                w.used(done)
            kr_marks = []
            for t in range(TT):
                kr_marks.append(K.act(S.activation, small[:, 0:MLA_ROPE], kr[:, t, :], ACT.Square,
                                      accum_out=sr[:, t:t + 1], after=[K.dve.last()]))
            gain(kr[:, 0:CT, :], CT, self.small.k_gain_row, after=kr_marks)
            inverse_rms(sq_[:, :], rq[:, :], QT * H)
            K.dve(V.tensor_scalar, rq[:, :], rq[:, :], MLA_QK ** -0.5, None, ALU.mult)
            n = per * (MLA_NOPE + MLA_V)
            pieces = [K.stream.piece("mla_w_ukv_2", (0,), rows_of(2), np.arange(c * n, (c + 1) * n),
                                     ahead=min(2, NRAW - 1 - c))
                      for c in range(H // per)]

            def finish_keys(t0, t1, last):
                s, r = sk[:, t0 * H:t1 * H], rk[:, t0 * H:t1 * H]
                for t in range(t0, t1):
                    one = sk[:, t * H:(t + 1) * H]
                    K.dve(V.tensor_scalar, one, one, sr[:, t:t + 1], None, ALU.add)
                inverse_rms(s, r, (t1 - t0) * H)
                for t in range(t0, t1):
                    r = rk[:, t * H:(t + 1) * H]
                    rb = lambda n: bass.AP(tensor=r.tensor, offset=r.offset,
                                           ap=[[r.ap[0][0], P], [1, H], [0, n]])
                    K.dve(V.tensor_tensor, kt[:, t, :, 0:MLA_NOPE], kt[:, t, :, 0:MLA_NOPE],
                          rb(MLA_NOPE), ALU.mult, after=[last])
                    kb = kr[:, t, :]
                    kbb = bass.AP(tensor=kb.tensor, offset=kb.offset,
                                  ap=[[kb.ap[0][0], P], [0, H], [1, MLA_ROPE]])
                    K.dve(V.tensor_tensor, kt[:, t, :, MLA_NOPE:], kbb, rb(MLA_ROPE), ALU.mult)

            for t in range(TT):
                for c, (w, ch) in enumerate(pieces):
                    i = K.next_banks()
                    for j in range(2):
                        done = K.mm(K.bank(i), ckv[:, j, t * P:(t + 1) * P], w[:, j, :], j == 0, j == 1,
                                    mark=(j == 1), after=nk)
                    kv = K.bank(i).rearrange("p (h d) -> p h d", h=per)
                    m2 = K.act(S.copy, kt[:, t, per * c:per * (c + 1), 0:MLA_NOPE],
                               kv[:, :, 0:MLA_NOPE], after=[done])
                    q = head_sums(kv[:, :, 0:MLA_NOPE], sk[:, t * H + c * per:t * H + (c + 1) * per],
                              MLA_NOPE, [m2])
                    m1 = K.dve(V.tensor_copy, v[:, t, per * c:per * (c + 1), :], kv[:, :, MLA_NOPE:],
                               after=[q])
                    K.release(i, 1, m1)
                    K.stream.used(ch, done)
                if t < QT:
                    x = kr[:, CT + t:CT + t + 1, :]
                    gain(x, 1, self.small.k_gain_row)
                    rotate(x, 1, *angles(t))
                if t in (TT // 2 - 1, TT - 1):
                    finish_keys(t + 1 - TT // 2, t + 1, m2)
            K.barrier()
        with ExitStack() as s1:
            self.heads_attention(s1, kt, v, qt, rq, out)
            K.barrier()
        with ExitStack() as s1:
            yt = Split(K.sb("mla_out_high", [P, KT, SEQ], s1, F32R), K.sb("mla_out_low", [P, KT, SEQ], s1, F32R))
            marks = []
            for j in range(KT):
                i = K.next_banks()
                for t in range(QT):
                    done = K.pe(T.transpose, K.bank(i)[:, t * P:(t + 1) * P],
                                out[:, t, j * P:(j + 1) * P], K.ident, mark=True)
                m = K.split(yt[:, j, :], K.bank(i), after=[done])
                K.release(i, 1, m)
                marks.append(m)
            for d in range(KT):
                w, ch = K.stream.piece("mla_w_out_2", (0,), rows_of(KT), np.arange(d * P, (d + 1) * P),
                                       split=True)
                i = K.next_banks(2)
                for kk in range(KT):
                    done = K.mm(self.pair(i, CTX, TOK), w[:, kk, :], yt[:, kk, :], kk == 0, kk == KT - 1,
                                mark=(kk == KT - 1), after=[marks[kk]])
                K.stream.used(ch, done)
                self.residual(i, done, l, 2, d, with_ctx=False)
            K.barrier()

    def heads_attention(self, st, kt, v, qt, rq, out):
        K, V, S, T = self.K, self.K.nc.vector, self.K.nc.scalar, self.K.nc.tensor
        H = MLA_HEADS
        kf = Ring([Buf(K.sb(f"k_feat{i}", [P, TOK], st)) for i in range(3)])
        qf = Ring([Buf(K.sb(f"q_feat{i}", [P, SEQ], st)) for i in range(3)])
        for b in kf.bufs + qf.bufs:
            b.free = [K.pool(K.nc.gpsimd.memset, b.t[MLA_QK:P, :], 0.0)]
        zeros = b.free
        probs = Ring([Buf(K.sb(f"mla_probs{i}", [P, TOK], st)) for i in range(3)])
        turned = Ring([Buf(K.sb(f"mla_turned{i}", [P, 3 * P], st)) for i in range(6)])
        colr = Ring([Buf(K.sb(f"mla_cols{i}", [P, 4], st)) for i in range(4)])
        K.area = [4, 3, 0]

        def to_features(src, tiles, dst, gain):
            i = K.next_banks()
            for n, t in enumerate(tiles):
                done = K.pe(T.transpose, K.bank(i)[0:MLA_QK, n * P:(n + 1) * P], src(t),
                            K.ident, mark=True)
            out = dst.t[0:MLA_QK, tiles[0] * P:(tiles[-1] + 1) * P]
            m = K.act(S.activation, out, K.bank(i)[0:MLA_QK, 0:len(tiles) * P], ACT.Copy, scale=gain,
                      after=[done] + dst.free)
            K.release(i, 1, m)
            return m

        def prepare(h):
            hd = Names()
            hd.h, hd.k, hd.q = h, kf.take(), qf.take()
            k_of, q_of = (lambda t: kt[:, t, h, :]), (lambda t: qt[:, t, h, :])

            def step(src, tiles, dst, gain):
                def go():
                    hd.ready = to_features(src, tiles, dst, gain)
                return go
            kg, qg = self.small.k_gain_col, self.small.q_gain_col
            return hd, [step(k_of, [0, 1, 2], hd.k, kg), step(k_of, [3, 4, 5], hd.k, kg),
                        step(q_of, [0, 1, 2, 3], hd.q, qg)]

        def scores(hd, t, n):
            u = Names()
            u.h, u.t, u.p, u.c = hd.h, t, probs.take(), colr.take()
            top, bias, total, u.inv = (u.c.t[:, j:j + 1] for j in range(4))
            i = 2 * (n % 2)
            K.claim(i, 2)
            for lo, hi in ((0, BANK), (BANK, TOK)):
                done = K.mm(K.bank(i, 2)[:, lo:hi], hd.q.t[:, t * P:(t + 1) * P], hd.k.t[:, lo:hi], True,
                            True, mark=True, after=[hd.ready] + zeros)
            hd.k.free, hd.q.free = [done], [done]
            logits = K.bank(i, 2)[:, 0:TOK]
            K.dve(V.tensor_reduce, top, logits, AX_X, ALU.max, after=[done] + u.c.free)
            s = rq[:, t * H + u.h:t * H + u.h + 1]
            m = K.dve(V.scalar_tensor_tensor, bias, top, -1.0, s, ALU.mult, ALU.mult)
            e = K.act(S.activation, u.p.t[:, :], logits, ACT.Exp, bias=bias, scale=s, accum_out=total,
                      after=[m] + u.p.free)
            K.release(i, 2, e)
            u.total, u.ready = total, e
            return u

        def turn(u):
            u.parts = []
            for part in range(2):
                i, pt = K.next_banks(), turned.take()
                for b in range(3):
                    kb = 3 * part + b
                    done = K.pe(T.transpose, K.bank(i)[:, b * P:(b + 1) * P],
                                u.p.t[:, kb * P:(kb + 1) * P], K.ident, after=[u.ready], mark=True)
                m = K.copy(pt.t[:, :], K.bank(i)[:, 0:3 * P], after=[done] + pt.free)
                K.release(i, 1, m)
                u.parts.append((pt, m))
            u.p.free = [done]

        def weigh(u):
            K.claim(7)
            for kb in range(TT):
                pt, m = u.parts[kb // 3]
                done = K.mm(K.bank(7)[:, 0:MLA_V], pt.t[:, (kb % 3) * P:(kb % 3 + 1) * P],
                            v[:, kb, u.h, :], kb == 0, kb == TT - 1, mark=(kb % 3 == 2), after=[m])
                if kb % 3 == 2:
                    pt.free = [done]
            K.dve(V.reciprocal, u.inv, u.total, after=[u.ready])
            m = K.dve(V.tensor_scalar, out[:, u.t, u.h * MLA_V:(u.h + 1) * MLA_V],
                      K.bank(7)[:, 0:MLA_V], u.inv, None, ALU.mult, after=[done])
            u.c.free = [m]
            K.release(7, 1, m)

        units = []
        hd, steps = prepare(0)
        for go in steps:
            go()
        for n in range(QT * H + 2):
            h, t = n // QT, n % QT
            if n < QT * H:
                if t == 0:
                    now = hd
                    if h + 1 < H:
                        hd, steps = prepare(h + 1)
                units.append(scores(now, t, n))
                if t < len(steps) and h + 1 < H:
                    steps[t]()
            if n >= 2:
                weigh(units[n - 2])
            if n and n - 1 < QT * H:
                turn(units[n - 1])
        K.area = [0, 8, 0]

    def feed_forward(self, l, with_ctx):
        K, V, S = self.K, self.K.nc.vector, self.K.nc.scalar
        spans = BOTH if with_ctx else LATENT
        lo0 = 0 if with_ctx else CTX
        with ExitStack() as st:
            act = K.sb("ffn_act", [P, FT, TOK if with_ctx else SEQ], st)
            with ExitStack() as s1:
                h = Split(K.sb("h2_high", [P, KT, TOK], s1, F32R),
                          K.sb("h2_low", [P, KT, TOK], s1, F32R))
                with ExitStack() as s2:
                    sq = K.sb("squares2", [P, KT, SEQ], s2), K.sb("squares_ctx", [P, KT, CTX], s2)
                    self.rounded = Ring([Buf(K.sb(f"rounded{i}", [P, SEQ], s2)) for i in range(2)])
                    ready = self.modulate(l, 3, 4, h, sq, with_ctx)
                    K.barrier(pe=False)
                gap = 2
                row = [Buf(K.sb(f"ffn_row{i}", [P, TOK + 2 * gap], s1)) for i in range(2)]
                for r in row:
                    mz = K.pool(K.nc.gpsimd.memset, r.t[:, :], 0.0)
                rows = Ring(row)
                n = TOK + gap - lo0 if with_ctx else SEQ
                base = 0 if with_ctx else CTX + gap
                for f in range(FT):
                    cw = self.small.ffn_w[l][f]
                    w, ch = K.stream.piece("ffn_w_in_2", (l,), rows_of(KT), np.arange(f * P, (f + 1) * P),
                                           split=True)
                    i, done = self.wide(w, ch, h, spans, after=ready)
                    r = rows.take()
                    if with_ctx:
                        K.act(S.copy, r.t[:, 1:1 + CTX], self.pair(i, 0, CTX), after=[done, mz] + r.free)
                    m = K.act(S.copy, r.t[:, 1 + CTX + gap:1 + TOK + gap], self.pair(i, CTX, TOK),
                              after=[done, mz] + r.free)
                    t = K.bank(i, 2)[:, 0:n]
                    K.dve(V.tensor_scalar, t, r.t[:, base:base + n], cw[:, 0:1], self.small.ffn_b[l][f],
                          ALU.mult, ALU.add, after=[m])
                    for j in (1, 2):
                        m = K.dve(V.scalar_tensor_tensor, t, r.t[:, base + j:base + j + n],
                                  cw[:, j:j + 1], t, ALU.mult, ALU.add)
                    r.free = [m]
                    a = act[:, f, :]
                    if with_ctx:
                        K.act(S.activation, a[:, 0:CTX], t[:, 0:CTX], ACT.Gelu_apprx_tanh, after=[m])
                        g = K.act(S.activation, a[:, CTX:TOK], t[:, CTX + gap:TOK + gap],
                                  ACT.Gelu_apprx_tanh)
                    else:
                        g = K.act(S.activation, a, t, ACT.Gelu_apprx_tanh, after=[m])
                    K.release(i, 2, g)
                    w, ch = K.stream.piece("ffn_w_in_2", (l,), rows_of(KT),
                                           FFN + np.arange(f * P, (f + 1) * P), split=True)
                    i, done = self.wide(w, ch, h, spans, after=ready)
                    m = K.dve(V.tensor_tensor, a, self.pair(i, lo0, TOK), a, ALU.mult, after=[done, g])
                    K.release(i, 2, m)
                K.barrier()
            parts = Ring([Buf(Split(K.sb(f"act_high{i}", [P, SEQ], st, F32R),
                                    K.sb(f"act_low{i}", [P, SEQ], st, F32R))) for i in range(3)])
            for side, (lo, hi) in ((1, (0, CTX)), (0, (CTX, TOK)))[0 if with_ctx else 1:]:
                n = hi - lo
                K.claim(0, KT)

                def split_tile(f):
                    s = parts.take()
                    return s, K.split(s.t[:, 0:n], act[:, f, lo - lo0:hi - lo0], after=s.free)

                ahead = [split_tile(0), split_tile(1)]
                for f in range(FT):
                    w, ch = K.stream.piece("ffn_w_out_2", (l,), rows_of(1, f * P), np.arange(D_MODEL),
                                           split=True)
                    s, m = ahead.pop(0)
                    for d in range(KT):
                        done = K.mm(K.bank(d)[:, 0:n], w[:, 0, d * P:(d + 1) * P], s.t[:, 0:n], f == 0,
                                    f == FT - 1, mark=(d == KT - 1 or f == FT - 1), after=[m])
                    K.stream.used(ch, done)
                    s.free = [done]
                    if f + 2 < FT:
                        ahead.append(split_tile(f + 2))
                x = self.xc if side else self.x
                for d in range(KT):
                    m = K.dve(V.scalar_tensor_tensor, x[:, d, :], K.bank(d)[:, 0:n],
                              self.mod(l, 5, d, side), x[:, d, :], ALU.mult, ALU.add, after=[done])
                    K.release(d, 1, m)
            K.barrier()

    def run(self):
        K, S = self.K, self.K.nc.scalar
        st = ExitStack()
        self.xc = K.sb("context", [P, KT, CTX], st)
        K.act.eng.dma_start(self.xc[:, :, :], self.dram_ctx).then_inc(self.ctx_sem, 16)
        for line in (K.pe, K.dve, K.act):
            line.wait((self.ctx_sem, 32))
        for l in range(DEPTH):
            with ExitStack() as s1:
                if l == 0:
                    self.conformer(l, s1)
                else:
                    self.latent_attention(l, s1)
                K.barrier()
            self.feed_forward(l, l < DEPTH - 1)
        st.close()


class Names:
    pass


def pack_constants():
    common, first = Pack("common"), Pack("first")
    at = {}
    i, j = np.arange(P)[:, None], np.arange(P)[None, :]
    at["ident"] = common.const(np.eye(P))
    at["ones"] = common.const(np.ones((P, P)))
    causal = np.zeros((P, SEQ))
    causal[:, SEQ - P:] = np.where(j <= i, 0.0, NEG)
    at["causal"] = first.const(causal)
    at["before01"] = first.const((i < j) * 1.0)
    at["before_add"] = first.const(np.where(i < j, 0.0, NEG))
    at["from_here"] = first.const((i >= j) * 1.0)

    def partner(dim):
        half = dim // 2
        f = np.arange(P) % dim
        return np.arange(P) + np.where(f < half, half, -half)

    for dim in (64, 32):
        half = dim // 2
        perm = np.zeros((P, P))
        perm[partner(dim), np.arange(P)] = 1.0
        at[f"perm{dim}"] = first.const(perm)
        f = np.arange(P) % dim
        inv = (10000.0 ** (-2.0 * (f % half) / dim)).astype(np.float32)
        at[f"inv{dim}"] = first.const(inv[:, None])
        at[f"sign{dim}"] = first.const(np.where(f < half, -1.0, 1.0)[:, None])
    n = np.arange(N_CMP)[None, None, :]
    t = np.arange(QT)[None, :, None] * P + np.arange(P)[:, None, None]
    seen = n * CMP_STRIDE + CMP_LEN - 1 <= t
    at["cmp_add"] = first.const(np.where(seen, 0.0, NEG).reshape(P, -1))
    at["cmp_keep"] = first.const((seen * 1.0).reshape(P, -1))
    r = np.arange(P) % 32
    mine = lambda h: np.arange(P) // 32 == h
    rows = [c for h in range(HEADS) for c in (mine(h) * (r == 0) / SCALE, mine(h) * (r == 1) * 1.0)]
    at["fox"] = first.const(np.stack(rows + [(r == 1) / -SCALE, (r == 0) * 1.0], 1))
    p = np.arange(P)[:, None]
    feature = np.arange(KT)[None, :] * P + p
    at["c"], at["c_ctx"] = (common.param(n, feature, None) for n in ("c_2", "c_ctx_2"))
    for l in range(DEPTH):
        at["ada_b", l] = common.param("ada_b_2", np.arange(6 * KT)[None, :] * P + p, l)
        at["norm_g", l] = first.param("norm_g", feature, l)
        at["mem_norm", l] = first.param("mem_norm", feature, l)
        at["kv_norm", l] = first.param("kv_norm", p, l)
        at["fox_bias", l] = first.param("fox_bias", p // 32, l)
        pe = (2 * np.arange(CMP_LEN // 2)[None, :] + p // HD) * HD + p % HD
        at["pe_k", l] = first.param("nsa_pe_k", pe, l)
        at["pe_v", l] = first.param("nsa_pe_v", pe, l)
    at["final_norm"] = first.param("final_norm", np.arange(KT)[None, :] * P + p, None)
    second = Pack("second")
    at["le"] = second.const(np.where(i <= j, 0.0, NEG))
    at["ge"] = second.const(np.where(i >= j, 0.0, NEG))
    tok = np.arange(SEQ)
    half = MLA_ROPE // 2
    inv = (10000.0 ** (-np.arange(0, half, 2) / half)).astype(np.float32)
    ang = np.concatenate([(tok // GRID_W).astype(np.float32)[:, None] * inv,
                          (tok % GRID_W).astype(np.float32)[:, None] * inv], 1)
    by_tile = lambda a: a.reshape(QT, P, half).transpose(1, 0, 2).reshape(P, -1)
    at["mla_cos"] = second.const(by_tile(np.cos(ang)))
    at["mla_sin"] = second.const(by_tile(np.sin(ang)))
    at["gate_bias"] = second.param("ab_gate_bias_2",
                                   HEADS * np.array([0, 2, 1, 3])[p // 32] + p % HEADS, 0)
    for c in range(4):
        at["conv_w", c] = second.param("ab_conv_w_2",
                                       np.arange(CONV_WIDTH)[None, :] * CONV_DIM + c * P + p, 0)
    four = np.arange(4)[None, :] * P + p
    for n in ("ab_conv_b_2", "ab_ln_g_2", "ab_ln_b_2", "ab_head_gain_2", "mla_q_norm_2"):
        at[n] = second.param(n, four, 0)
    at["mla_kv_norm_2"] = second.param("mla_kv_norm_2", four[:, 0:2], 0)
    for n in ("mla_q_gain_2", "mla_k_gain_2"):
        at[n] = second.param(n, np.where(p < MLA_NOPE, p, -1), 0)
        at[n, "row"] = second.param(n, MLA_NOPE + np.arange(MLA_ROPE)[None, :] + 0 * p, 0)
    for l in range(DEPTH):
        taps = (np.arange(FT)[None, :, None] * P + p[:, :, None]
                + np.arange(3)[None, None, :] * FFN).reshape(P, -1)
        at["ffn_w", l] = second.param("ffn_conv_w_2", taps, l)
        at["ffn_b", l] = second.param("ffn_conv_b_2", np.arange(FT)[None, :] * P + p, l)
    return common, first, second, at


def name_second(at, second):
    c, s = Names(), Names()
    col = lambda n, w=1, lo=0: second[:, at[n] + lo:at[n] + lo + w]
    c.ml_mask = [col("le", P), col("ge", P)]
    half = MLA_ROPE // 2
    c.mla_cos, c.mla_sin = col("mla_cos", QT * half), col("mla_sin", QT * half)
    s.gate_bias = col("gate_bias")
    s.conv_w = [col(("conv_w", k), CONV_WIDTH) for k in range(4)]
    s.conv_b, s.ln_g, s.ln_b, s.head_gain, s.q_norm = (
        [col(n, 1, k) for k in range(4)]
        for n in ("ab_conv_b_2", "ab_ln_g_2", "ab_ln_b_2", "ab_head_gain_2", "mla_q_norm_2"))
    s.kv_norm2 = [col("mla_kv_norm_2", 1, k) for k in range(2)]
    s.q_gain_col, s.k_gain_col = (col(n)[0:MLA_QK, :] for n in ("mla_q_gain_2", "mla_k_gain_2"))
    s.q_gain_row, s.k_gain_row = (col((n, "row"), MLA_ROPE) for n in ("mla_q_gain_2", "mla_k_gain_2"))
    s.ffn_w = [[col(("ffn_w", l), 3, 3 * f) for f in range(FT)] for l in range(DEPTH)]
    s.ffn_b = [[col(("ffn_b", l), 1, f) for f in range(FT)] for l in range(DEPTH)]
    return c, s


def name_constants(at, common, first):
    c, s = Names(), Names()
    c.causal = first[:, at["causal"]:at["causal"] + SEQ]
    sq = lambda t, n: t[:, at[n]:at[n] + P]
    c.before01, c.before_add, c.from_here = (sq(first, n) for n in ("before01", "before_add", "from_here"))
    c.perm64, c.perm32 = sq(first, "perm64"), sq(first, "perm32")
    col = lambda t, n, w=1: t[:, at[n]:at[n] + w]
    c.inv64, c.inv32, c.sign64, c.sign32 = (col(first, n) for n in ("inv64", "inv32", "sign64", "sign32"))
    c.cmp_add, c.cmp_keep = (col(first, n, QT * N_CMP) for n in ("cmp_add", "cmp_keep"))
    c.fox = col(first, "fox", 2 * HEADS + 2)
    tiles = lambda n: [first[:, at[n] + k:at[n] + k + 1] for k in range(KT)]
    s.norm_g = [tiles(("norm_g", l)) for l in range(DEPTH)]
    s.mem_norm = [tiles(("mem_norm", l)) for l in range(DEPTH)]
    s.kv_norm = [col(first, ("kv_norm", l)) for l in range(DEPTH)]
    s.fox_bias = [col(first, ("fox_bias", l)) for l in range(DEPTH)]
    s.pe = {w: [col(first, ("pe_" + w, l), CMP_LEN // 2) for l in range(DEPTH)] for w in "kv"}
    s.final_norm = tiles("final_norm")
    return c, s


def build(nc, plan=None):
    common, first, second, at = pack_constants()
    dram = lambda name, shape, dt=F32, kind="ExternalInput": nc.dram_tensor(name, shape, dt, kind=kind).ap()
    with ExitStack() as ctx:
        K = Core(nc, ctx)
        d_common, d_first = dram("common_dram", (P, common.n)), dram("first_dram", (P, first.n))
        d_x, d_mem = dram("x_dram", (P, KT, SEQ)), dram("mem_dram", (P, KT, N_MEM))
        d_kept = nc.dram_tensor("x_kept_dram", (P, KT, SEQ), F32, kind="Internal").ap()
        d_pos = dram("positions_dram", (SEQ,), I32)
        d_out = dram("out_dram", (P, KT, SEQ), kind="ExternalOutput")
        K.stream = Stream(K, [K.sem(f"weights_in_slot{i}") for i in range(NRAW)], plan)
        t_common = K.sb("common", [P, common.n])
        K.ident, K.ones = t_common[:, 0:P], t_common[:, P:2 * P]
        K.t_turn = 0
        d_second, d_ctx = dram("second_dram", (P, second.n)), dram("context_dram", (P, KT, CTX))
        x = K.sb("x", [P, KT, SEQ])
        loaded, stored = K.sem("constants_in"), K.sem("output_stored")
        M = Modulation(K, t_common, at)
        with ExitStack() as st:
            t_first = K.sb("first", [P, first.n], st)
            c, small = name_constants(at, t_common, t_first)
            for t, d in ((t_common, d_common), (t_first, d_first), (x, d_x)):
                nc.sync.dma_start(t[:], d).then_inc(loaded, 16)
            for line in (K.pe, K.dve, K.act):
                line.wait((loaded, 48))
            M.start()
            B = FirstBlock(K, c, small)
            B.modulation = M
            B.x, B.dram_mem, B.dram_pos = x, d_mem, d_pos
            B.dram_x, B.dram_x_kept = d_x, d_kept
            B.kept_sem, B.back_sem = K.sem("x_kept"), K.sem("x_back")
            B.mem_sem, B.pos_sem, B.consts_loaded = K.sem("mem_in"), K.sem("positions_in"), (loaded, 48)
            B.run()
        with ExitStack() as st:
            t_second = K.sb("second", [P, second.n], st)
            ctx_sem = K.sem("context_in")
            nc.scalar.dma_start(t_second[:], d_second).then_inc(ctx_sem, 16)
            c, small = name_second(at, t_second)
            B = SecondBlock(K, c, small)
            B.mods, B.mods_ready = M.mods, M.mods_ready
            B.x, B.dram_ctx, B.ctx_sem = x, d_ctx, ctx_sem
            B.run()
        d_stream = dram("stream_dram", (len(K.stream.chunks), P, SLOT))
        K.stream.issue(K.sp, d_stream)
        K.sp.wait(*K.all_marks())
        nc.sync.dma_start(d_out, x[:, :, :]).then_inc(stored, 16)
        nc.sync.wait_ge(stored, 16)
    return K.stream, [common, first, second]


def feature_major(a):
    return np.ascontiguousarray(a.reshape(a.shape[0], -1, P).transpose(2, 1, 0))


def kernel(**inputs):
    import concourse.bacc as bacc
    from concourse.bass_utils import run_bass_kernel_spmd

    inputs = {k: np.asarray(v) for k, v in inputs.items()}
    new = lambda: bacc.Bacc("TRN2", target_bir_lowering=False, num_devices=1,
                            dynamic_dma_scratch_size=1024)
    stream, _ = build(new())
    nc = new()
    stream, packs = build(nc, stream.chunks)
    arrays = {"common_dram": packs[0].fill(inputs), "first_dram": packs[1].fill(inputs),
              "second_dram": packs[2].fill(inputs), "context_dram": feature_major(inputs["ctx_2"][0]),
              "x_dram": feature_major(inputs["x"][0]), "mem_dram": feature_major(inputs["mem"][0]),
              "positions_dram": inputs["positions"][0], "stream_dram": stream.fill(inputs)}
    got = run_bass_kernel_spmd(nc, [arrays], core_ids=[0]).results[0]["out_dram"]
    return np.ascontiguousarray(got.transpose(2, 1, 0)).reshape(1, SEQ, D_MODEL)
```
